# Optimizing a Trainium2 kernel written in Bass

```python
import math
import jax, jax.numpy as jnp
from jax import lax
import numpy as np

D_MODEL = 1024
BATCH = 1
SEQ = 512
DEPTH = 2

CHUNK = 64
N_A_LAYERS = DEPTH // 2
N_B_LAYERS = DEPTH - N_A_LAYERS

SSM_EXPAND = 2
SSM_D_INNER = SSM_EXPAND * D_MODEL
SSM_HEAD_DIM = 64
SSM_HEADS = SSM_D_INNER // SSM_HEAD_DIM
SSM_GROUPS = 4
SSM_STATE = 128
SSM_CONV = 4
SSM_GN = SSM_GROUPS * SSM_STATE
SSM_CONV_DIM = SSM_D_INNER + 2 * SSM_GN
SSM_IN_DIM = SSM_D_INNER + SSM_CONV_DIM + SSM_HEADS

ATTN_HEAD_DIM = 64
ATTN_HEADS = D_MODEL // ATTN_HEAD_DIM
Q_BLOCK = 128

N_EXPERTS = 64
TOP_K = 8
N_EXPERT_GROUPS = 8
TOPK_GROUPS = 4
EXPERT_DIM = D_MODEL // 8
SHARED_DIM = EXPERT_DIM
ROUTED_SCALE = 2.5
EXPERT_BLOCK = 8

DN_ALPHA = (2.0 * DEPTH) ** 0.25
DN_BETA = (8.0 * DEPTH) ** -0.25
LN_EPS = 1e-5
RMS_EPS = 1e-5

kernel_name = "yoco_mamba2_fox_moe_deepnorm_adaln"

F32 = jnp.float32

def layer_norm(x, g, b):
    xf = x.astype(F32)
    mu = jnp.mean(xf, axis=-1, keepdims=True)
    var = jnp.mean(jnp.square(xf - mu), axis=-1, keepdims=True)
    return ((xf - mu) * lax.rsqrt(var + LN_EPS)).astype(x.dtype) * g + b

def rms_norm(x, w):
    xf = x.astype(F32)
    return (xf * lax.rsqrt(jnp.mean(xf * xf, axis=-1, keepdims=True) + RMS_EPS)).astype(x.dtype) * w

def modulate(x, shift, scale):
    return x * (1 + scale[:, None, :]) + shift[:, None, :]

def causal_depthwise_conv(u, w, b):
    ch = u.shape[-1]
    y = lax.conv_general_dilated(
        u, w[:, None, :].astype(u.dtype), window_strides=(1,),
        padding=[(SSM_CONV - 1, 0)], dimension_numbers=('NWC', 'WIO', 'NWC'),
        feature_group_count=ch)
    return y + b

def ssd_chunked_scan(xs, dt, A, Bm, Cm):
    bsz, L, H, P = xs.shape
    G, N = SSM_GROUPS, SSM_STATE
    R = H // G
    nc = L // CHUNK
    xdt = (xs.astype(F32) * dt[..., None]).reshape(bsz, nc, CHUNK, G, R, P)
    dA = (dt * A).reshape(bsz, nc, CHUNK, G, R)
    Bc = Bm.astype(F32).reshape(bsz, nc, CHUNK, G, N)
    Cc = Cm.astype(F32).reshape(bsz, nc, CHUNK, G, N)
    causal = jnp.tril(jnp.ones((CHUNK, CHUNK), dtype=bool))

    def step(state, inp):
        xdt_c, dA_c, B_c, C_c = inp
        acum = jnp.cumsum(dA_c, axis=1)
        seg = acum[:, :, None] - acum[:, None, :]
        decay = jnp.exp(jnp.where(causal[None, :, :, None, None], seg, -jnp.inf))
        cb = jnp.einsum('blgn,bsgn->blsg', C_c, B_c)
        y_diag = jnp.einsum('blsg,blsgr,bsgrp->blgrp', cb, decay, xdt_c)
        y_off = jnp.einsum('blgn,bgrpn,blgr->blgrp', C_c, state, jnp.exp(acum))
        to_end = jnp.exp(acum[:, -1:] - acum)
        new_state = (state * jnp.exp(acum[:, -1])[..., None, None]
                     + jnp.einsum('bsgn,bsgr,bsgrp->bgrpn', B_c, to_end, xdt_c))
        return new_state, y_diag + y_off

    init = jnp.zeros((bsz, G, R, P, N), F32)
    seq_first = lambda a: jnp.moveaxis(a, 1, 0)
    _, ys = lax.scan(step, init, (seq_first(xdt), seq_first(dA), seq_first(Bc), seq_first(Cc)))
    return jnp.moveaxis(ys, 0, 1).reshape(bsz, L, H, P).astype(xs.dtype)

def mamba2_mixer(h, w_in, conv_w, conv_b, dt_bias, a_log, d_skip, norm_w, w_out):
    bsz, L, _ = h.shape
    proj = h @ w_in
    z = proj[..., :SSM_D_INNER]
    xbc = proj[..., SSM_D_INNER:SSM_D_INNER + SSM_CONV_DIM]
    dt_raw = proj[..., SSM_D_INNER + SSM_CONV_DIM:]
    xbc = jax.nn.silu(causal_depthwise_conv(xbc, conv_w, conv_b))
    xs = xbc[..., :SSM_D_INNER].reshape(bsz, L, SSM_HEADS, SSM_HEAD_DIM)
    Bm = xbc[..., SSM_D_INNER:SSM_D_INNER + SSM_GN].reshape(bsz, L, SSM_GROUPS, SSM_STATE)
    Cm = xbc[..., SSM_D_INNER + SSM_GN:].reshape(bsz, L, SSM_GROUPS, SSM_STATE)
    dt = jax.nn.softplus((dt_raw + dt_bias).astype(F32))
    A = -jnp.exp(a_log.astype(F32))
    y = ssd_chunked_scan(xs, dt, A, Bm, Cm)
    y = y + d_skip[:, None] * xs
    y = y.reshape(bsz, L, SSM_D_INNER) * jax.nn.silu(z)
    y = rms_norm(y, norm_w)
    return y @ w_out

def shared_kv(x_a, cond, kv_ada_w, kv_ada_b, kv_w, kv_fb):
    bsz, L, _ = x_a.shape
    shift, scale = jnp.split(cond @ kv_ada_w + kv_ada_b, 2, axis=-1)
    u = modulate(x_a, shift, scale)
    proj = u @ kv_w
    k = proj[..., :D_MODEL].reshape(bsz, L, ATTN_HEADS, ATTN_HEAD_DIM)
    v = proj[..., D_MODEL:2 * D_MODEL].reshape(bsz, L, ATTN_HEADS, ATTN_HEAD_DIM)
    log_f = jax.nn.log_sigmoid((proj[..., 2 * D_MODEL:] + kv_fb).astype(F32))
    cum_f = jnp.cumsum(log_f, axis=1)
    return k, v, jnp.moveaxis(cum_f, 2, 1)

def forgetting_attention(h, w_q, w_o, k, v, cum_f):
    bsz, L, _ = h.shape
    q = (h @ w_q).reshape(bsz, L, ATTN_HEADS, ATTN_HEAD_DIM)
    scale = ATTN_HEAD_DIM ** -0.5
    outs = []
    for i in range(L // Q_BLOCK):
        q0, q1 = i * Q_BLOCK, (i + 1) * Q_BLOCK
        logits = jnp.einsum('bqhd,bkhd->bhqk', q[:, q0:q1], k[:, :q1]).astype(F32) * scale
        logits = logits + cum_f[:, :, q0:q1, None] - cum_f[:, :, None, :q1]
        mask = (q0 + jnp.arange(Q_BLOCK))[:, None] >= jnp.arange(q1)[None, :]
        logits = jnp.where(mask, logits, -jnp.inf)
        p = jax.nn.softmax(logits, axis=-1).astype(v.dtype)
        outs.append(jnp.einsum('bhqk,bkhd->bqhd', p, v[:, :q1]))
    o = jnp.concatenate(outs, axis=1).reshape(bsz, L, D_MODEL)
    return o @ w_o

def moe_ffn(h, w_router, router_bias, w1, w3, w2, ws1, ws3, ws2):
    bsz, L, dm = h.shape
    t = h.reshape(-1, dm)
    T = t.shape[0]
    scores = jax.nn.sigmoid((t @ w_router).astype(F32))
    sel = scores + router_bias.astype(F32)
    grp = sel.reshape(T, N_EXPERT_GROUPS, N_EXPERTS // N_EXPERT_GROUPS)
    grp_score = jnp.sum(lax.top_k(grp, 2)[0], axis=-1)
    _, gidx = lax.top_k(grp_score, TOPK_GROUPS)
    gmask = jnp.sum(jax.nn.one_hot(gidx, N_EXPERT_GROUPS, dtype=F32), axis=1)
    emask = jnp.repeat(gmask, N_EXPERTS // N_EXPERT_GROUPS, axis=1) > 0
    _, eidx = lax.top_k(jnp.where(emask, sel, -jnp.inf), TOP_K)
    wsel = jnp.take_along_axis(scores, eidx, axis=1)
    wsel = wsel / jnp.sum(wsel, axis=-1, keepdims=True) * ROUTED_SCALE
    gate = jnp.einsum('tk,tke->te', wsel, jax.nn.one_hot(eidx, N_EXPERTS, dtype=F32)).astype(h.dtype)
    out = (jax.nn.silu(t @ ws1) * (t @ ws3)) @ ws2
    for e0 in range(0, N_EXPERTS, EXPERT_BLOCK):
        sl = slice(e0, e0 + EXPERT_BLOCK)
        a = jax.nn.silu(jnp.einsum('td,edf->tef', t, w1[sl])) * jnp.einsum('td,edf->tef', t, w3[sl])
        out = out + jnp.einsum('tef,efd->td', a * gate[:, sl, None], w2[sl])
    return out.reshape(bsz, L, dm)

def setup_inputs(seed: int = 0) -> dict:
    key = jax.random.key(seed)
    ks = iter(jax.random.split(key, 48))
    D = D_MODEL
    fan = D ** -0.5

    def nrm(shape, scale):
        return jax.random.normal(next(ks), shape, F32) * scale

    x = nrm((BATCH, SEQ, D), 1.0)
    c = nrm((BATCH, D), 1.0)
    ada_w = nrm((DEPTH, D, 6 * D), 0.2 * fan)
    ada_b = nrm((DEPTH, 6 * D), 0.02)
    ln1_g = 1.0 + nrm((DEPTH, D), 0.05)
    ln1_b = nrm((DEPTH, D), 0.02)
    ln2_g = 1.0 + nrm((DEPTH, D), 0.05)
    ln2_b = nrm((DEPTH, D), 0.02)
    ssm_w_in = nrm((N_A_LAYERS, D, SSM_IN_DIM), fan)
    ssm_conv_w = nrm((N_A_LAYERS, SSM_CONV, SSM_CONV_DIM), SSM_CONV ** -0.5)
    ssm_conv_b = nrm((N_A_LAYERS, SSM_CONV_DIM), 0.02)
    dt0 = jnp.exp(jax.random.uniform(next(ks), (N_A_LAYERS, SSM_HEADS), F32,
                                     minval=math.log(1e-3), maxval=math.log(1e-1)))
    ssm_dt_bias = dt0 + jnp.log(-jnp.expm1(-dt0))
    ssm_a_log = jnp.log(jax.random.uniform(next(ks), (N_A_LAYERS, SSM_HEADS), F32, minval=1.0, maxval=16.0))
    ssm_d = 1.0 + nrm((N_A_LAYERS, SSM_HEADS), 0.1)
    ssm_norm_w = 1.0 + nrm((N_A_LAYERS, SSM_D_INNER), 0.05)
    ssm_w_out = nrm((N_A_LAYERS, SSM_D_INNER, D), SSM_D_INNER ** -0.5 * DN_BETA)
    kv_ada_w = nrm((D, 2 * D), 0.2 * fan)
    kv_ada_b = nrm((2 * D,), 0.02)
    kv_w = jnp.concatenate([nrm((D, D), fan), nrm((D, D), fan * DN_BETA),
                            nrm((D, ATTN_HEADS), fan)], axis=-1)
    kv_fb = jax.random.uniform(next(ks), (ATTN_HEADS,), F32, minval=1.0, maxval=5.0)
    attn_w_q = nrm((N_B_LAYERS, D, D), fan)
    attn_w_o = nrm((N_B_LAYERS, D, D), fan * DN_BETA)
    moe_w_router = nrm((DEPTH, D, N_EXPERTS), fan)
    moe_bias = nrm((DEPTH, N_EXPERTS), 0.01)
    moe_w1 = nrm((DEPTH, N_EXPERTS, D, EXPERT_DIM), fan)
    moe_w3 = nrm((DEPTH, N_EXPERTS, D, EXPERT_DIM), fan)
    moe_w2 = nrm((DEPTH, N_EXPERTS, EXPERT_DIM, D), EXPERT_DIM ** -0.5 * DN_BETA)
    moe_ws1 = nrm((DEPTH, D, SHARED_DIM), fan)
    moe_ws3 = nrm((DEPTH, D, SHARED_DIM), fan)
    moe_ws2 = nrm((DEPTH, SHARED_DIM, D), SHARED_DIM ** -0.5 * DN_BETA)
    return {"x": x, "c": c, "ada_w": ada_w, "ada_b": ada_b,
            "ln1_g": ln1_g, "ln1_b": ln1_b, "ln2_g": ln2_g, "ln2_b": ln2_b,
            "ssm_w_in": ssm_w_in, "ssm_conv_w": ssm_conv_w, "ssm_conv_b": ssm_conv_b,
            "ssm_dt_bias": ssm_dt_bias, "ssm_a_log": ssm_a_log, "ssm_d": ssm_d,
            "ssm_norm_w": ssm_norm_w, "ssm_w_out": ssm_w_out,
            "kv_ada_w": kv_ada_w, "kv_ada_b": kv_ada_b, "kv_w": kv_w, "kv_fb": kv_fb,
            "attn_w_q": attn_w_q, "attn_w_o": attn_w_o,
            "moe_w_router": moe_w_router, "moe_bias": moe_bias,
            "moe_w1": moe_w1, "moe_w3": moe_w3, "moe_w2": moe_w2,
            "moe_ws1": moe_ws1, "moe_ws3": moe_ws3, "moe_ws2": moe_ws2}

def reference(x, c, ada_w, ada_b, ln1_g, ln1_b, ln2_g, ln2_b,
              ssm_w_in, ssm_conv_w, ssm_conv_b, ssm_dt_bias, ssm_a_log, ssm_d,
              ssm_norm_w, ssm_w_out, kv_ada_w, kv_ada_b, kv_w, kv_fb,
              attn_w_q, attn_w_o, moe_w_router, moe_bias,
              moe_w1, moe_w3, moe_w2, moe_ws1, moe_ws3, moe_ws2):
    cond = jax.nn.silu(c)
    k_sh = v_sh = cf_sh = None
    for layer in range(DEPTH):
        mod = cond @ ada_w[layer] + ada_b[layer]
        shift1, scale1, gate1, shift2, scale2, gate2 = jnp.split(mod, 6, axis=-1)
        h = modulate(x, shift1, scale1)
        if layer < N_A_LAYERS:
            a = layer
            y = mamba2_mixer(h, ssm_w_in[a], ssm_conv_w[a], ssm_conv_b[a], ssm_dt_bias[a],
                             ssm_a_log[a], ssm_d[a], ssm_norm_w[a], ssm_w_out[a])
        else:
            b = layer - N_A_LAYERS
            y = forgetting_attention(h, attn_w_q[b], attn_w_o[b], k_sh, v_sh, cf_sh)
        x = layer_norm(DN_ALPHA * x + (1 + gate1[:, None, :]) * y, ln1_g[layer], ln1_b[layer])
        h = modulate(x, shift2, scale2)
        y = moe_ffn(h, moe_w_router[layer], moe_bias[layer], moe_w1[layer], moe_w3[layer],
                    moe_w2[layer], moe_ws1[layer], moe_ws3[layer], moe_ws2[layer])
        x = layer_norm(DN_ALPHA * x + (1 + gate2[:, None, :]) * y, ln2_g[layer], ln2_b[layer])
        if layer == N_A_LAYERS - 1:
            k_sh, v_sh, cf_sh = shared_kv(x, cond, kv_ada_w, kv_ada_b, kv_w, kv_fb)
    return x


_drawn_inputs = setup_inputs


def setup_inputs(seed=0):
    import zlib

    import numpy as np

    out = dict(_drawn_inputs(seed))
    spreads = {}
    factors = {'kv_ada_b': 4.597}
    for name, (base, spread) in spreads.items():
        noise = np.random.default_rng([zlib.crc32(name.encode()), seed]).standard_normal(out[name].shape)
        drawn = base * np.exp(spread * noise) if base else spread * noise
        out[name] = __import__('jax').numpy.asarray(drawn.astype(out[name].dtype))
    for name, factor in factors.items():
        out[name] = (out[name] * factor).astype(out[name].dtype)
    return out
```

```python
from contextlib import ExitStack

import concourse.bass as bass
from concourse import mybir

F32 = mybir.dt.float32
BF16 = mybir.dt.bfloat16
I32 = mybir.dt.int32
ALU = mybir.AluOpType
ACT = mybir.ActivationFunctionType
AX = mybir.AxisListType.X

P = 128
D = 1024
S = 512
T = S // P
KC = D // P
DI = 2048
HEADS = 32
HD = 64
GROUPS = 4
NST = 128
GH = HEADS // GROUPS
GW = GH * HD
GN = GROUPS * NST
CONV = 4
XBC = DI + 2 * GN
XT = DI // P
CT = XBC // P
AH = 16
E = 64
EG = 8
EPG = E // EG
TOPG = 4
TOPK = 8
F = D // 8
ROUTED_SCALE = 2.5
ALPHA = 4.0 ** 0.25
EPS = 1e-5
ASCALE = HD ** -0.5
BIG = 1.0e30
RING = 3
SLOTS = 8
NOWHERE = 2 * S * TOPK


def trunk(nc, x, c, ada_w, ada_b, ln1_g, ln1_b, ln2_g, ln2_b, ssm_w_in, ssm_conv_w, ssm_conv_b,
          ssm_dt_bias, ssm_a_log, ssm_d, ssm_norm_w, ssm_w_out, kv_ada_w, kv_ada_b, kv_w, kv_fb,
          attn_w_q, attn_w_o, moe_w_router, moe_bias, moe_w1, moe_w3, moe_w2, moe_ws1, moe_ws3,
          moe_ws2, out, phases=4, cap=P):
    ctx = ExitStack()
    with ctx:
        def sb(name, shape, dt=F32):
            return ctx.enter_context(nc.sbuf_tensor(name, shape, dt))

        def sem(name):
            return ctx.enter_context(nc.semaphore(name))

        KB = 256
        arena = sb("arena", [P, 191 * KB])

        def view(kb, *dims):
            n = 1
            for d in dims:
                n *= d
            v = arena[:, int(kb * KB):int(kb * KB) + n]
            names = "abcd"[:len(dims)]
            if len(dims) == 1:
                return v
            return v.rearrange(f"p ({' '.join(names)}) -> p {' '.join(names)}",
                               **dict(zip(names[1:], dims[1:])))

        X = view(0, T, D)
        HT = view(16, KC, S)
        ring = [view(143 + 16 * r, KC, 512) for r in range(RING)]
        exp_w = [view(95 + 12 * r, 3, 1024) for r in range(SLOTS)]
        xbcT = view(32, CT, S)
        zs = view(80, T, DI)
        conv_acc = [view(112 + 2 * i, S) for i in range(2)]
        xdt = [view(112 + 2 * i, GW) for i in range(2)]
        xsD = [view(116 + 2 * i, GW) for i in range(2)]
        xdte = [view(120 + 2 * i, GW) for i in range(2)]
        decay = [view(124 + 2 * i, 4 * P) for i in range(2)]
        mixm = [view(128 + 2 * i, 4 * P) for i in range(2)]
        stepm = [view(132 + 0.5 * i, P) for i in range(8)]
        Btok = [view(136 + 0.5 * i, P) for i in range(2)]
        CBm = [view(137 + 0.5 * i, P) for i in range(2)]
        state = view(16, GROUPS, GW)
        yg = [view(24 + 2 * i, GW) for i in range(2)]
        yoff = [view(28 + 2 * i, GW) for i in range(2)]
        sq_out = zs
        kT = view(32, KC, S)
        vtok = view(48, T, D)
        qT = view(64, KC, S)
        otok = view(80, T, D)
        logit = [view(96 + 2 * i, S) for i in range(3)]
        shifted = [view(102 + 2 * i, S) for i in range(3)]
        prob = [view(108 + 2 * i, S) for i in range(3)]
        probT = [view(114 + 2 * i, T, P) for i in range(2)]
        g1bc = view(139, D)
        Rmix = [view(16, T, D), view(32, T, D)]
        lnrow_mix = [view(112, D), view(116, D)]
        diag_mix = view(120, KC, P)
        H2 = view(32, T, D)
        SH = view(48, T, D)
        diag_moe = view(64, KC, P)
        s2bc = view(68, D)
        sh2bc = view(72, D)
        g2bc = view(76, D)
        shw = view(80, 3, 1024)
        aS = [view(92, S), SH[:, T - 1, 512:1024]]
        xg = [view(32 + 4 * i, D) for i in range(4)]
        xeT = [view(80 + 4 * i, KC, P) for i in range(2)]
        s1 = [view(88 + 0.5 * i, P) for i in range(2)]
        aT = [view(89 + 0.5 * i, P) for i in range(2)]
        yrow = [view(64 + 4 * i, D) for i in range(2)]
        part = [view(32 + 8 * i, TOPK, 256) for i in range(2)]
        lnrow_moe = [view(80, D), view(84, D)]
        scores, sel, mask, gate, krank = (view(64 + i, T, E) for i in range(5))
        top8 = view(70, T * EG, 8)
        gcmp = [view(71 + i, T, EG, EG) for i in range(2)]
        pos = view(72, T, E)

        def view_b(kb, *dims):
            v = view(kb, dims[0] * dims[1] // 2).bitcast(BF16)
            return v.rearrange("p (a b) -> p a b", b=dims[1])
        mask_b = view_b(73, T, E)
        onehot = [view_b(73.5 + i, T, P) for i in range(2)]

        ident = sb("ident", [P, P])
        upper = sb("upper", [P, P])
        after = sb("after", [P, P])
        ones = sb("ones", [P, P])
        before_b = sb("before_b", [P, P], BF16)
        ones_b = sb("ones_b", [P, P], BF16)
        slot_no = sb("slot_no", [P, P], BF16)
        low8 = sb("low8", [P, EG, EG])
        cols = sb("cols", [P, 3, P])
        bcs = sb("bcs", [P, 240])
        condT = sb("condT", [P, KC])
        mod = sb("mod", [P, 112])
        wdt = view(139, KC, HEADS)
        wf = sb("wf", [P, KC, AH])
        wr = sb("wr", [P, KC, E])
        dtx = sb("dtx", [P, T, HEADS])
        dts = sb("dts", [P, T, HEADS])
        dA = sb("dA", [P, T, HEADS])
        negA = sb("negA", [P, HEADS])
        sp_all = sb("sp", [P, 4, P])
        sp = [sp_all[:, i, :] for i in range(4)]
        rows = sp_all[:, 0:3, :]
        logf = sb("logf", [P, T, AH])
        ssum = sb("ssum", [P, T])
        exps = [sb(f"exps{i}", [P, 96]) for i in range(2)]
        ssq = sb("ssq", [P, T, GROUPS])
        rsy = sb("rsy", [P, T])
        cumf = sb("cumf", [P, T, AH])
        cumfT = sb("cumfT", [T * AH, P])
        mx = sb("mx", [P, 8])
        rsum = sb("rsum", [P, 2, T])
        rinv = sb("rinv", [P, 2, T])
        bn = sb("bn", [P, T, 2, 6])
        mv = sb("mv", [P, T, 2])
        sd = sb("sd", [P, T])
        rstd = sb("rstd", [P, T])
        gsc = sb("gsc", [P, T, EG])
        grank = sb("grank", [P, T, EG])
        gk = sb("gk", [P, T, TOPK])
        gsum = sb("gsum", [P, T])
        V = sb("V", [P, T, E, 3], BF16)
        destf = sb("destf", [P, E])
        table = view(90, E, 2).bitcast(I32)
        pos1 = view(74.75, T)
        V1 = view_b(74.5, T, 4)
        idx = [sb(f"idx{i}", [P, 2], I32) for i in range(8)]
        passed = sb("passed", [P, SLOTS + 3])
        most = sb("most", [P, 1])
        mosti = sb("mosti", [P, 1], I32)
        psum = ctx.enter_context(nc.psum_tensor("psum", [P, 8, 512], F32))

        rows_dram = nc.dram_tensor("h2_rows", [S, D], F32, kind="Internal").ap()
        part_dram = nc.dram_tensor("expert_rows", [S * TOPK, D], F32, kind="Internal").ap()

        c_col = cols[:, 0, 0:8]
        modb = cols[:, 0, 8:120]
        convw = cols[:, 1, 0:CONV * CT].rearrange("p (k j) -> p k j", k=CONV)
        convb = cols[:, 1, CONV * CT:CONV * CT + CT]
        normw = cols[:, 2, 0:XT]
        dtb_bc, alog_bc, dsk_bc, fb_bc = bcs[:, 0:32], bcs[:, 32:64], bcs[:, 64:96], bcs[:, 96:112]
        rb_bc = [bcs[:, 112:176], bcs[:, 176:240]]
        MODC = {(l, v): 48 * l + 8 * v for l in range(2) for v in range(6)}
        MODC[("kv", 0)], MODC[("kv", 1)] = 96, 104
        SHIFT1, SCALE1, GATE1, SHIFT2, SCALE2, GATE2 = range(6)

        filled = [sem(f"filled{b}") for b in range(8)]
        drained = [sem(f"drained{b}") for b in range(8)]
        ring_in = [sem(f"ring_in{r}") for r in range(RING)]
        exp_in = [sem(f"exp_in{r}") for r in range(SLOTS)]
        small_in = sem("small_in")
        x_in = sem("x_in")
        consts = sem("consts")
        act_step = sem("act_step")
        dve_step = sem("dve_step")
        pool_step = sem("pool_step")
        vec_cols = sem("vec_cols")
        cond_ready = sem("cond_ready")
        acc_ready = sem("acc_ready")
        conv_done = sem("conv_done")
        soft_act = sem("soft_act")
        soft_dve = sem("soft_dve")
        dA_ready = sem("dA_ready")
        exps_ready = sem("exps_ready")
        stepm_ready = sem("stepm_ready")
        xdt_ready = sem("xdt_ready")
        xdte_ready = sem("xdte_ready")
        decay_ready = sem("decay_ready")
        mixm_ready = sem("mixm_ready")
        state_scaled = sem("state_scaled")
        yz_ready = sem("yz_ready")
        squared = sem("squared")
        diag_ready = sem("diag_ready")
        bc_ready = sem("bc_ready")
        res_ready = sem("res_ready")
        sd_ready = sem("sd_ready")
        var_ready = sem("var_ready")
        lnrow_in = sem("lnrow_in")
        ln_scaled = sem("ln_scaled")
        x_ready = sem("x_ready")
        h2_scaled = sem("h2_scaled")
        h2_ready = sem("h2_ready")
        h2_out = sem("h2_out")
        shw_in = sem("shw_in")
        wr_in = sem("wr_in")
        scores_ready = sem("scores_ready")
        mask_ready = sem("mask_ready")
        onehot_ready = sem("onehot_ready")
        onehot_used = sem("onehot_used")
        table_ready = sem("table_ready")
        sh_gated = sem("sh_gated")
        most_ready = sem("most_ready")
        more = [{name: sem(f"more_{name}{l}") for name in (
            "onehot", "dest", "idx", "rows", "turned", "moved", "weights", "up", "silu", "gated", "down", "yrow",
            "sent", "step", "carried")} for l in range(2)]
        idx_ready = [sem(f"idx_ready{i}") for i in range(1)]
        xg_in = [sem(f"xg_in{i}") for i in range(4)]
        y_out = [sem(f"y_out{i}") for i in range(2)]
        s1_ready = sem("s1_ready")
        part_in = [sem(f"part_in{i}") for i in range(2)]
        part_used = sem("part_used")
        logit_ready = sem("logit_ready")
        masked = sem("masked")
        max_ready = sem("max_ready")
        prob_ready = sem("prob_ready")
        logf_ready = sem("logf_ready")
        out_done = sem("out_done")

        MARK = {}
        PART = ([], [])

        def until_filled(eng, key):
            b, n = MARK[key]
            eng.wait_ge(filled[b], n)
            return psum[:, b, :]

        def until_drained(eng, key):
            b, n = MARK[key]
            eng.wait_ge(drained[b], n)

        MORE = S // P - 1

        def when_more(eng, l, blocks):
            eng.wait_ge(most_ready, l + 1)
            m = eng.value_load(mosti[0:1, 0:1])
            with eng.If(m > P):
                blocks()
            with eng.Else():
                eng.nop()

        items = []

        def cols_of(w, n0, n=512):
            return w.rearrange("(k p) n -> p k n", p=P)[:, :, n0:n0 + n]

        def ada_item(l, blk):
            items.append((("ada", l, blk), cols_of(ada_w[l], 512 * blk)))

        def kva_item(blk):
            items.append((("ada", "kv", blk), cols_of(kv_ada_w, 512 * blk)))

        for blk in range(4):
            ada_item(0, blk)
        later = [(0, b) for b in range(4, 12)] + [("kv", b) for b in range(4)] + [(1, b) for b in range(12)]
        w_in = ssm_w_in[0]
        for n, blk in enumerate([4, 5, 0, 1, 2, 3, "z0", "z1", "z2", "z3"]):
            if isinstance(blk, int):
                items.append((("xbc", blk), cols_of(w_in, DI + 512 * blk)))
            else:
                items.append((("z", int(blk[1])), cols_of(w_in, 512 * int(blk[1]))))
            for l, b in later[len(later) * n // 10:len(later) * (n + 1) // 10]:
                (kva_item(b) if l == "kv" else ada_item(l, b))
        for n in range(2):
            for kh in range(2):
                items.append((("w_out", n, kh), cols_of(ssm_w_out[0][D * kh:D * (kh + 1), :], 512 * n)))
        n_items0 = len(items)
        for n in range(4):
            items.append((("kvw", n), cols_of(kv_w, 512 * n)))
        for n in range(2):
            items.append((("wq", n), cols_of(attn_w_q[0], 512 * n)))
        for n in range(2):
            items.append((("wo", n), cols_of(attn_w_o[0], 512 * n)))
        n_items1 = len(items)

        CONSTS = 10
        SMALL = 16 * 16
        TILES = [slice(P * t, P * t + P) for t in range(T)]
        NQ = T * GROUPS
        NG = E // SLOTS

        def stream_order():
            for key, _ in items[4:]:
                if key[0] == "w_out":
                    return
                yield key

        block = ctx.enter_context(nc.Block())

        @block.tensor
        def _(pe):
            uses = [0] * 8
            taken = [0]

            def claim(b):
                if uses[b]:
                    pe.wait_ge(drained[b], uses[b])
                uses[b] += 1
                return psum[:, b, :]

            def fill(ins, b, key):
                ins.then_inc(filled[b], 1)
                MARK[key] = (b, uses[b])

            def take(key):
                i = taken[0]
                assert items[i][0] == key, (items[i][0], key)
                taken[0] += 1
                pe.wait_ge(ring_in[i % RING], 16 * (i // RING + 1))
                return ring[i % RING], ("item", i)

            def done_item(tag, key):
                MARK[tag] = MARK[key]

            def ada(l, blk):
                w, tag = take(("ada", l, blk))
                b = 4 + blk % 2
                ps = claim(b)
                for j in range(4):
                    for k in range(KC):
                        mm = pe.matmul(ps[:, j:j + 1], w[:, k, P * j:P * j + P], condT[:, k:k + 1],
                                       start=(k == 0), stop=(k == KC - 1))
                fill(mm, b, ("mod", l, blk))
                done_item(tag, ("mod", l, blk))

            def turn(name, src, ready):
                for t in range(T):
                    ready(t)
                    for half in range(2):
                        b = 4 * half + t % 2
                        ps = claim(b)
                        for j in range(4):
                            k = 4 * half + j
                            mm = pe.transpose(ps[:, P * j:P * j + P], src[:, t, P * k:P * k + P], ident[:, :])
                        fill(mm, b, (name, t, half))

            def turned(name, t):
                for half in range(2):
                    until_drained(pe, (name, t, half))

            def spread(name, need, banks=(1, 2)):
                pe.wait_ge(diag_ready, need)
                src = diag_mix if name[0] == "g1" else diag_moe
                for half in range(2):
                    b = banks[half]
                    ps = claim(b)
                    mm = pe.matmul(ps[:, :], ones[:, :], src[:, 4 * half:4 * half + 4, :].rearrange("p a b -> p (a b)"),
                                   start=True, stop=True)
                    fill(mm, b, (name, half))

            pe.wait_ge(consts, CONSTS)
            pe.wait_ge(small_in, SMALL)
            ps = claim(4)
            for r, n in enumerate((120, 120, XT)):
                mm = pe.transpose(ps[:, P * r:P * r + n], rows[0:n, r, :], ident[0:n, 0:n])
            fill(mm, 4, "vecs")
            pe.wait_ge(cond_ready, 1)
            for blk in range(4):
                ada(0, blk)

            def x_loaded(t):
                if t == 0:
                    pe.wait_ge(x_in, 16 * T)
            turn("hT0", X, x_loaded)
            for t in range(T):
                turned("hT0", t)
            ps = claim(6)
            for t in range(T):
                for k in range(KC):
                    mm = pe.matmul(ps[:, HEADS * t:HEADS * (t + 1)], HT[:, k, P * t:P * t + P], wdt[:, k, :],
                                   start=(k == 0), stop=(k == KC - 1))
            fill(mm, 6, "dt")
            at = 4
            nb = 0
            while items[at][0][0] != "w_out":
                kind = items[at][0]
                if kind[0] == "ada":
                    ada(kind[1], kind[2])
                elif kind[0] == "xbc":
                    w, tag = take(kind)
                    for j in range(4):
                        b = (0, 1, 2, 3)[nb % 4]
                        nb += 1
                        ps = claim(b)
                        for k in range(KC):
                            mm = pe.matmul(ps[:, :], w[:, k, P * j:P * j + P], HT[:, k, :],
                                           start=(k == 0), stop=(k == KC - 1))
                        fill(mm, b, ("xbc", 4 * kind[1] + j))
                    done_item(tag, ("xbc", 4 * kind[1] + 3))
                else:
                    w, tag = take(kind)
                    for t in range(T):
                        b = (0, 1, 2, 3)[nb % 4]
                        nb += 1
                        ps = claim(b)
                        for k in range(KC):
                            mm = pe.matmul(ps[:, :], HT[:, k, P * t:P * t + P], w[:, k, :],
                                           start=(k == 0), stop=(k == KC - 1))
                        fill(mm, b, ("z", kind[1], t))
                    done_item(tag, ("z", kind[1], T - 1))
                at += 1

            pe.wait_ge(dA_ready, 1)
            pe.wait_ge(conv_done, CT)

            def tok(t):
                return slice(P * t, P * t + P)

            def scan_a(q):
                ch, g = divmod(q, GROUPS)
                if g == 0:
                    ps = claim(0)
                    for n, m in enumerate((upper, after, ones)):
                        mm = pe.matmul(ps[:, HEADS * n:HEADS * (n + 1)], m[:, :], dA[:, ch, :], start=True, stop=True)
                    fill(mm, 0, ("sums", ch))
                ps = claim(4)
                for j in range(4):
                    mm = pe.transpose(ps[:, P * j:P * j + P], xbcT[:, 4 * g + j, tok(ch)], ident[:, :])
                fill(mm, 4, ("xs", q))
                ps = claim(5)
                pe.transpose(ps[:, 0:P], xbcT[:, XT + g, tok(ch)], ident[:, :])
                mm = pe.matmul(ps[:, P:2 * P], xbcT[:, XT + g, tok(ch)], xbcT[:, XT + GROUPS + g, tok(ch)],
                               start=True, stop=True)
                fill(mm, 5, ("bc", q))
                for half in range(2):
                    pe.wait_ge(stepm_ready, 2 * q + half + 1)
                    ps = claim(1 + half)
                    for j in range(4):
                        mm = pe.matmul(ps[:, P * j:P * j + P], stepm[4 * half + j], upper[:, :], start=True, stop=True)
                    fill(mm, 1 + half, ("seg", q, half))

            def scan_b(q):
                ch, g = divmod(q, GROUPS)
                if ch:
                    until_drained(pe, ("st", q - GROUPS))
                    ps = claim(6)
                    mm = pe.matmul(ps[:, :], xbcT[:, XT + GROUPS + g, tok(ch)], state[:, g, :], start=True, stop=True)
                    fill(mm, 6, ("yoff", q))
                if ch < T - 1:
                    pe.wait_ge(xdte_ready, q + 1)
                    until_drained(pe, ("bc", q))
                    ps = claim(3)
                    mm = pe.matmul(ps[:, :], Btok[q % 2], xdte[q % 2], start=True, stop=True)
                    fill(mm, 3, ("st", q))
                pe.wait_ge(xdt_ready, q + 1)
                ps = claim(7)
                for h in range(GH):
                    if h % 4 == 0:
                        pe.wait_ge(mixm_ready, 2 * q + h // 4 + 1)
                    mm = pe.matmul(ps[:, HD * h:HD * h + HD], mixm[h // 4][:, P * (h % 4):P * (h % 4) + P],
                                   xdt[q % 2][:, HD * h:HD * h + HD], start=True, stop=True)
                fill(mm, 7, ("yd", q))

            def turn_y(ch):
                for g in range(GROUPS):
                    b = (0, 3, 4, 5)[g]
                    pe.wait_ge(yz_ready, GROUPS * ch + g + 1)
                    ps = claim(b)
                    for j in range(4):
                        k = 4 * g + j
                        mm = pe.transpose(ps[:, P * j:P * j + P], zs[:, ch, P * k:P * k + P], ident[:, :])
                    fill(mm, b, ("yT", ch, g))

            NQ = T * GROUPS
            scan_a(0)
            for q in range(NQ):
                if q + 1 < NQ:
                    scan_a(q + 1)
                scan_b(q)
                if q % GROUPS == 0 and q:
                    turn_y(q // GROUPS - 1)
            turn_y(T - 1)

            spread(("g1", 0), 1)
            for n in range(2):
                w0, tag0 = take(("w_out", n, 0))
                w1, tag1 = take(("w_out", n, 1))
                for t in range(T):
                    if n == 0:
                        for g in range(GROUPS):
                            until_drained(pe, ("yT", t, g))
                    b = 4 + t
                    ps = claim(b)
                    for k in range(XT):
                        w = (w0, w1)[k // KC]
                        mm = pe.matmul(ps[:, :], xbcT[:, k, tok(t)], w[:, k % KC, :],
                                       start=(k == 0), stop=(k == XT - 1))
                    fill(mm, b, ("mix", 0, n, t))
                done_item(tag0, ("mix", 0, n, T - 1))
                done_item(tag1, ("mix", 0, n, T - 1))

            def experts(l):
                nd = 1 + 4 * l
                spread(("s2", l), nd + 1)
                spread(("sh2", l), nd + 2)
                spread(("g2", l), nd + 3)

                def ready(t):
                    pe.wait_ge(h2_ready, T * l + t + 1)
                turn(("h2T", l), H2, ready)
                for t in range(T):
                    turned(("h2T", l), t)
                pe.wait_ge(wr_in, 16 * l) if l else None
                ps = claim(6)
                for t in range(T):
                    for k in range(KC):
                        mm = pe.matmul(ps[:, E * t:E * t + E], HT[:, k, tok(t)], wr[:, k, :],
                                       start=(k == 0), stop=(k == KC - 1))
                fill(mm, 6, ("router", l))
                if l == 0:
                    done_item("wr0", ("router", 0))
                pe.wait_ge(shw_in, 48 * (l + 1))
                for n in range(2):
                    b = 1 + n
                    ps = claim(b)
                    w = shw[:, n, :].rearrange("p (k f) -> p k f", k=KC)
                    for k in range(KC):
                        mm = pe.matmul(ps[:, :], w[:, k, :], HT[:, k, :], start=(k == 0), stop=(k == KC - 1))
                    fill(mm, b, ("shared_in", l, n))
                pe.wait_ge(sh_gated, l + 1)
                for t in range(T):
                    for n in range(2):
                        b = (0, 3)[n]
                        ps = claim(b)
                        mm = pe.matmul(ps[:, :], aS[0][:, tok(t)], shw[:, 2, 512 * n:512 * n + 512], start=True, stop=True)
                        fill(mm, b, ("shared", l, t, n))
                pe.wait_ge(mask_ready, l + 1)
                ps = claim(7)
                for t in range(T):
                    for u in range(t + 1):
                        mm = pe.matmul(ps[:, E * t:E * t + E], (before_b if u == t else ones_b)[:, :], mask_b[:, u, :],
                                       start=(u == 0), stop=(u == t))
                for u in range(T):
                    mm = pe.matmul(ps[:, E * T:E * T + E], ones_b[:, :], mask_b[:, u, :], start=(u == 0), stop=(u == T - 1))
                fill(mm, 7, ("places", l))

                def build_table(n0):
                    ps = claim(4)
                    for e in range(E):
                        pe.wait_ge(onehot_ready, n0 + e + 1)
                        for t in range(T):
                            mm = pe.matmul(ps[:, 3 * e:3 * e + 3], onehot[e % 2][:, t, :], V[:, t, e, :],
                                           start=(t == 0), stop=(t == T - 1))
                        if e < E - 1:
                            mm.then_inc(onehot_used, 1)
                    fill(mm, 4, ("table", l))
                build_table(E * l)

                base = list(uses)
                ebase = E * l

                def rows_in(g, u):
                    i = SLOTS * g + u
                    pe.wait_ge(xg_in[u % 4], 16 * (2 * g + u // 4 + 1 + ebase // 4))
                    for half in range(2):
                        b = 4 * half
                        first = base[b] if (isinstance(i, int) and i == 0) else None
                        pe.wait_ge(drained[b], base[b] + i)
                        for j in range(4):
                            k = 4 * half + j
                            mm = pe.transpose(psum[:, b, P * j:P * j + P], xg[u % 4][:, P * k:P * k + P], ident[:, :])
                        mm.then_inc(filled[b], 1)

                def up(g, u):
                    i = SLOTS * g + u
                    pe.wait_ge(exp_in[u], 48 * (g + 1 + l * (E // SLOTS)))
                    pe.wait_ge(drained[0], base[0] + i + 1)
                    pe.wait_ge(drained[4], base[4] + i + 1)
                    for n in range(2):
                        b = 1 + 4 * n + u % 2
                        pe.wait_ge(drained[b], base[b] + 4 * g + u // 2)
                        w = exp_w[u][:, n, :].rearrange("p (k f) -> p k f", k=KC)
                        for k in range(KC):
                            mm = pe.matmul(psum[:, b, 0:P], w[:, k, :], xeT[u % 2][:, k, :],
                                           start=(k == 0), stop=(k == KC - 1))
                        mm.then_inc(filled[b], 1)

                def down(g, u):
                    i = SLOTS * g + u
                    pe.wait_ge(drained[5 + u % 2], base[5 + u % 2] + 4 * g + u // 2 + 1)
                    for n in range(2):
                        b = 3 + 4 * n
                        pe.wait_ge(drained[b], base[b] + i)
                        mm = pe.matmul(psum[:, b, :], aT[u % 2], exp_w[u][:, 2, 512 * n:512 * n + 512],
                                       start=True, stop=True)
                        mm.then_inc(filled[b], 1)

                def group(g, first=False, last=False):
                    for u in range(SLOTS):
                        if not (last and u == SLOTS - 1):
                            rows_in(*((g, u + 1) if u + 1 < SLOTS else (g + 1, 0)))
                        up(g, u)
                        if u:
                            down(g, u - 1)
                        elif not first:
                            down(g - 1, SLOTS - 1)
                NG = E // SLOTS
                rows_in(0, 0)
                group(0, first=True)
                with pe.Fori(1, NG - 1) as g:
                    group(g)
                group(NG - 1, last=True)
                down(NG - 1, SLOTS - 1)

                def more_blocks():
                    done = more[l]
                    for b in range(8):
                        n = E if b in (0, 4, 3, 7) else E // 2
                        pe.wait_ge(drained[b], base[b] + n)

                    def unit(i):
                        pe.wait_ge(done["onehot"], i + 1)
                        for t in range(T):
                            mm = pe.matmul(psum[:, 6, 0:3], onehot[0][:, t, :], V1[:, t, 0:3], start=(t == 0), stop=(t == T - 1))
                        mm.then_inc(done["dest"], 1)
                        pe.wait_ge(done["rows"], 16 * i + 16)
                        for k in range(KC):
                            mm = pe.transpose(psum[:, k // 4, P * (k % 4):P * (k % 4) + P], xg[0][:, P * k:P * k + P], ident[:, :])
                        mm.then_inc(done["turned"], 1)
                        pe.wait_ge(done["moved"], 2 * i + 2)
                        pe.wait_ge(done["weights"], 48 * i + 48)
                        for n in range(2):
                            w = exp_w[0][:, n, :].rearrange("p (k f) -> p k f", k=KC)
                            for k in range(KC):
                                mm = pe.matmul(psum[:, 2 + n, 0:P], w[:, k, :], xeT[0][:, k, :],
                                               start=(k == 0), stop=(k == KC - 1))
                        mm.then_inc(done["up"], 1)
                        pe.wait_ge(done["gated"], i + 1)
                        for n in range(2):
                            mm = pe.matmul(psum[:, 4 + n, :], aT[0], exp_w[0][:, 2, 512 * n:512 * n + 512], start=True, stop=True)
                        mm.then_inc(done["down"], 1)
                    for b in range(MORE):
                        with pe.Fori(0, E) as e:
                            unit(E * b + e)
                    pe.wait_ge(done["yrow"], 2 * MORE * E)
                when_more(pe, l, more_blocks)
                MARK[("loop", l)] = list(base)
                for b in (0, 4, 3, 7):
                    uses[b] += E
                for b in (1, 2, 5, 6):
                    uses[b] += E // 2

            if phases >= 2:
                experts(0)

            def attention():
                spread(("g1", 1), 5)

                def ready(t):
                    pe.wait_ge(x_ready, T + t + 1)
                turn("uT", X, ready)
                for t in range(T):
                    turned("uT", t)
                ps = claim(6)
                for t in range(T):
                    for k in range(KC):
                        mm = pe.matmul(ps[:, AH * t:AH * (t + 1)], HT[:, k, tok(t)], wf[:, k, :],
                                       start=(k == 0), stop=(k == KC - 1))
                fill(mm, 6, "forget")
                nb = 0
                for n in range(2):
                    w, tag = take(("kvw", n))
                    for j in range(4):
                        b = (0, 1, 2, 3)[nb % 4]
                        nb += 1
                        ps = claim(b)
                        for k in range(KC):
                            mm = pe.matmul(ps[:, :], w[:, k, P * j:P * j + P], HT[:, k, :],
                                           start=(k == 0), stop=(k == KC - 1))
                        fill(mm, b, ("kT", 4 * n + j))
                    done_item(tag, ("kT", 4 * n + 3))
                pe.wait_ge(logf_ready, 1)
                ps = claim(7)
                lf = logf
                for t in range(T):
                    for u in range(t + 1):
                        mm = pe.matmul(ps[:, AH * t:AH * (t + 1)], (upper if u == t else ones)[:, :], lf[:, u, :],
                                       start=(u == 0), stop=(u == t))
                fill(mm, 7, "cumf")
                for n in range(2):
                    w, tag = take(("kvw", 2 + n))
                    for t in range(T):
                        b = (0, 1, 2, 3)[nb % 4]
                        nb += 1
                        ps = claim(b)
                        for k in range(KC):
                            mm = pe.matmul(ps[:, :], HT[:, k, tok(t)], w[:, k, :], start=(k == 0), stop=(k == KC - 1))
                        fill(mm, b, ("v", n, t))
                    done_item(tag, ("v", n, T - 1))
                until_drained(pe, "cumf")
                ps = claim(7)
                mm = pe.transpose(ps[0:T * AH, 0:P], cumf[:, :, :].rearrange("p a b -> p (a b)"), ident[:, :])
                fill(mm, 7, "cumfT")
                turn("qhT", X, lambda t: None)
                for t in range(T):
                    turned("qhT", t)
                for n in range(2):
                    w, tag = take(("wq", n))
                    for j in range(4):
                        b = (0, 1, 2, 3)[nb % 4]
                        nb += 1
                        ps = claim(b)
                        for k in range(KC):
                            mm = pe.matmul(ps[:, :], w[:, k, P * j:P * j + P], HT[:, k, :],
                                           start=(k == 0), stop=(k == KC - 1))
                        fill(mm, b, ("qT", 4 * n + j))
                    done_item(tag, ("qT", 4 * n + 3))
                until_drained(pe, "cumfT")
                for j in range(KC):
                    until_drained(pe, ("qT", j))
                    until_drained(pe, ("kT", j))
                for n in range(2):
                    for t in range(T):
                        until_drained(pe, ("v", n, t))

                def scores_of(n):
                    h, i = divmod(n, T)
                    if i == 0:
                        ps = claim(h % 2)
                        for t in range(T):
                            r = AH * t + h
                            mm = pe.matmul(ps[:, tok(t)], ident[0:T * AH, r:r + 1].to_broadcast([T * AH, P]),
                                           cumfT[:, :], start=True, stop=True)
                        fill(mm, h % 2, ("ncf", h))
                    ps = claim(2 + n % 2)
                    lo = HD * (h % 2)
                    nk = P * (i + 1)
                    mm = pe.matmul(ps[:, 0:nk], qT[lo:lo + HD, h // 2, tok(i)], kT[lo:lo + HD, h // 2, 0:nk],
                                   start=True, stop=True)
                    fill(mm, 2 + n % 2, ("qk", n))

                def turn_probs(n):
                    h, i = divmod(n, T)
                    pe.wait_ge(prob_ready, n + 1)
                    ps = claim(4 + n % 2)
                    for j in range(i + 1):
                        mm = pe.transpose(ps[:, tok(j)], prob[n % 3][:, tok(j)], ident[:, :])
                    fill(mm, 4 + n % 2, ("pT", n))

                def weigh(n):
                    h, i = divmod(n, T)
                    until_drained(pe, ("pT", n))
                    b = 6 + h % 2
                    if i == 0:
                        claim(b)
                    ps = psum[:, b, :]
                    for j in range(i + 1):
                        mm = pe.matmul(ps[:, HD * i:HD * i + HD], probT[n % 2][:, j, :], vtok[:, j, HD * h:HD * h + HD],
                                       start=(j == 0), stop=(j == i))
                    if i == T - 1:
                        fill(mm, b, ("o", h))

                NU = AH * T
                scores_of(0)
                scores_of(1)
                for n in range(NU):
                    if n + 2 < NU:
                        scores_of(n + 2)
                    turn_probs(n)
                    if n:
                        weigh(n - 1)
                weigh(NU - 1)

                def o_ready(t):
                    if t == 0:
                        until_drained(pe, ("o", AH - 1))
                        until_drained(pe, ("o", AH - 2))
                turn("oT", otok, o_ready)
                for n in range(2):
                    w, tag = take(("wo", n))
                    for t in range(T):
                        turned("oT", t)
                        b = 4 + t
                        ps = claim(b)
                        for k in range(KC):
                            mm = pe.matmul(ps[:, :], HT[:, k, tok(t)], w[:, k, :], start=(k == 0), stop=(k == KC - 1))
                        fill(mm, b, ("mix", 1, n, t))
                    done_item(tag, ("mix", 1, n, T - 1))

            if phases >= 3:
                attention()
            if phases >= 4:
                experts(1)


        @block.scalar
        def _(act):
            def move(key, dst, func=ACT.Copy, **kw):
                ps = until_filled(act, key)
                act.activation(dst, ps, func, **kw).then_inc(drained[MARK[key][0]], 1)

            def move_turned(name, half, dst):
                for t in range(T):
                    ps = until_filled(act, (name, t, half))
                    act.activation(dst[:, 4 * half:4 * half + 4, TILES[t]], ps.rearrange("p (a b) -> p a b", a=4),
                                   ACT.Copy).then_inc(drained[MARK[(name, t, half)][0]], 1)

            def move_modulated(name, half, dst, scale, shift):
                for t in range(T):
                    ps = until_filled(act, (name, t, half))
                    for j in range(4):
                        k = 4 * half + j
                        ins = act.activation(dst[:, k, TILES[t]], ps[:, P * j:P * j + P], ACT.Identity,
                                             scale=mod[:, scale + k:scale + k + 1], bias=mod[:, shift + k:shift + k + 1])
                    ins.then_inc(drained[MARK[(name, t, half)][0]], 1)

            def until_mod(l, v):
                until_drained(act, ("mod", l, (8 * v) // 4))
                until_drained(act, ("mod", l, (8 * v) // 4 + 1))

            def move_spread(name, dst):
                for half in range(2):
                    move((name, half), dst[:, 512 * half:512 * half + 512])

            soft = [0]

            def softplus_act(x, n, x_done):
                x_done()
                act.activation(sp[0][:, 0:n], x, ACT.Abs).then_inc(soft_act, 1)
                soft[0] += 1
                act.wait_ge(soft_act, soft[0])
                act.activation(sp[0][:, 0:n], sp[0][:, 0:n], ACT.Exp, scale=-1.0).then_inc(soft_act, 1)
                soft[0] += 1

            def softplus_ln(n, m):
                act.wait_ge(soft_dve, m)
                act.activation(sp[2][:, 0:n], sp[1][:, 0:n], ACT.Ln).then_inc(soft_act, 1)
                soft[0] += 1

            until_drained(act, "vecs")
            act.activation(condT[:, :], c_col, ACT.Silu).then_inc(cond_ready, 1)
            for v in (SHIFT1, SCALE1):
                until_mod(0, v)
            move_modulated("hT0", 0, HT, MODC[(0, SCALE1)], MODC[(0, SHIFT1)])
            act.activation(negA[:, :], alog_bc, ACT.Exp).then_inc(soft_act, 1)
            soft[0] += 1
            softplus_act(dtx[:, :, :].rearrange("p a b -> p (a b)"), P, lambda: until_drained(act, "dt"))
            softplus_ln(P, 1)
            waiting = []

            def finish_conv():
                if waiting:
                    j, n = waiting.pop()
                    until_drained(act, ("xbc", j))
                    act.activation(xbcT[:, j, :], conv_acc[n % 2], ACT.Silu).then_inc(conv_done, 1)
            n = 0
            for key in stream_order():
                if key[0] == "xbc":
                    for j in range(4 * key[1], 4 * key[1] + 4):
                        ps = until_filled(act, ("xbc", j))
                        if n >= 2:
                            act.wait_ge(conv_done, n - 1)
                        act.activation(conv_acc[n % 2], ps, ACT.Identity, scale=convw[:, CONV - 1, j:j + 1],
                                       bias=convb[:, j:j + 1]).then_inc(acc_ready, 1)
                        finish_conv()
                        waiting.append((j, n))
                        n += 1
                elif key[0] == "z":
                    finish_conv()
                    for t in range(T):
                        move(("z", key[1], t), zs[:, t, 512 * key[1]:512 * key[1] + 512], ACT.Silu)

            def scan_exps(q):
                ch, g = divmod(q, GROUPS)
                if g == 0:
                    if ch >= 2:
                        act.wait_ge(yz_ready, GROUPS * (ch - 1))
                    ps = until_filled(act, ("sums", ch))
                    act.activation(exps[ch % 2][:, :], ps[:, 0:96], ACT.Exp).then_inc(drained[0], 1)
                for half in range(2):
                    if q:
                        act.wait_ge(mixm_ready, 2 * (q - 1) + half + 1)
                    ps = until_filled(act, ("seg", q, half))
                    act.activation(decay[half], ps, ACT.Exp).then_inc(drained[1 + half], 1)

            def square(q):
                ch, g = divmod(q, GROUPS)
                act.wait_ge(yz_ready, q + 1)
                if q:
                    act.wait_ge(squared, q)
                act.activation(view(139, GW), zs[:, ch, GW * g:GW * g + GW], ACT.Square,
                               accum_out=ssq[:, ch, g:g + 1]).then_inc(squared, 1)

            def move_y(ch):
                for g in range(2):
                    ps = until_filled(act, ("yT", ch, g))
                    for j in range(4):
                        k = 4 * g + j
                        ins = act.activation(xbcT[:, k, TILES[ch]], ps[:, P * j:P * j + P], ACT.Copy,
                                             scale=normw[:, k:k + 1])
                    ins.then_inc(drained[MARK[("yT", ch, g)][0]], 1)
            scan_exps(0)
            for q in range(NQ):
                if q + 1 < NQ:
                    scan_exps(q + 1)
                if q:
                    square(q - 1)
                if q % GROUPS == 0 and q:
                    move_y(q // GROUPS - 1)
            square(NQ - 1)
            move_y(T - 1)

            def root(n):
                act.wait_ge(var_ready, n)
                act.activation(sd[:, :], sd[:, :], ACT.Sqrt).then_inc(sd_ready, 1)
            root(1)
            act.wait_ge(squared, NQ)
            move_spread(("g1", 0), g1bc)
            root(2)

            def experts(l):
                move_spread(("s2", l), s2bc)
                move_spread(("sh2", l), sh2bc)
                move_spread(("g2", l), g2bc)
                move_turned(("h2T", l), 0, HT)
                ps = until_filled(act, ("router", l))
                act.activation(scores[:, :, :].rearrange("p a b -> p (a b)"), ps[:, 0:T * E], ACT.Sigmoid).then_inc(drained[6], 1)
                move(("shared_in", l, 0), aS[0], ACT.Silu)
                move(("shared_in", l, 1), aS[1])
                for t in range(T):
                    for n in range(2):
                        move(("shared", l, t, n), SH[:, t, 512 * n:512 * n + 512])
                base = MARK[("loop", l)]

                def rows_in(g, u):
                    act.wait_ge(filled[0], base[0] + SLOTS * g + u + 1)
                    act.activation(xeT[u % 2][:, 0:4, :], psum[:, 0, :].rearrange("p (a b) -> p a b", a=4),
                                   ACT.Copy).then_inc(drained[0], 1)

                def gelu(g, u):
                    b = 1 + u % 2
                    act.wait_ge(filled[b], base[b] + 4 * g + u // 2 + 1)
                    act.activation(s1[u % 2], psum[:, b, 0:P], ACT.Silu).then_inc(drained[b], 1)

                def rows_out(g, u, first=False):
                    act.wait_ge(filled[3], base[3] + SLOTS * g + u + 1)
                    if not (first and u < 2 and l == 0):
                        act.wait_ge(y_out[u % 2], 16 * (4 * g + u // 2) + 16 * (E // 2) * l)
                    act.activation(yrow[u % 2][:, 0:512], psum[:, 3, :], ACT.Copy).then_inc(drained[3], 1)

                def group(g, first=False, last=False):
                    for u in range(SLOTS):
                        if not (last and u == SLOTS - 1):
                            rows_in(*((g, u + 1) if u + 1 < SLOTS else (g + 1, 0)))
                        gelu(g, u)
                        if u:
                            rows_out(g, u - 1, first)
                        elif not first:
                            rows_out(g - 1, SLOTS - 1)
                rows_in(0, 0)
                group(0, first=True)
                with act.Fori(1, NG - 1) as g:
                    group(g)
                group(NG - 1, last=True)
                rows_out(NG - 1, SLOTS - 1)

                def more_blocks():
                    done = more[l]

                    def unit(i):
                        act.wait_ge(done["turned"], i + 1)
                        act.activation(xeT[0][:, 0:4, :], psum[:, 0, :].rearrange("p (a b) -> p a b", a=4),
                                       ACT.Copy).then_inc(done["moved"], 1)
                        act.wait_ge(done["up"], i + 1)
                        act.activation(s1[0], psum[:, 2, 0:P], ACT.Silu).then_inc(done["silu"], 1)
                        act.wait_ge(done["down"], i + 1)
                        act.activation(yrow[0][:, 0:512], psum[:, 4, :], ACT.Copy).then_inc(done["yrow"], 1)
                    for b in range(MORE):
                        with act.Fori(0, E) as e:
                            unit(E * b + e)
                when_more(act, l, more_blocks)
                root(3 + 2 * l)

            def attention():
                move_spread(("g1", 1), g1bc)
                for v in (0, 1):
                    until_mod("kv", v)
                move_modulated("uT", 0, HT, MODC[("kv", 1)], MODC[("kv", 0)])
                softplus_act(dts[:, 0:2, :].rearrange("p a b -> p (a b)"), T * AH, lambda: act.wait_ge(soft_dve, 9))
                for j in range(0, KC, 2):
                    move(("kT", j), kT[:, j, :])
                    if j == 0:
                        softplus_ln(T * AH, 10)
                for n in range(2):
                    for t in range(0, T, 2):
                        move(("v", n, t), vtok[:, t, 512 * n:512 * n + 512])
                for v in (SHIFT1, SCALE1):
                    until_mod(1, v)
                move_modulated("qhT", 0, HT, MODC[(1, SCALE1)], MODC[(1, SHIFT1)])
                for j in range(0, KC, 2):
                    move(("qT", j), qT[:, j, :])
                until_drained(act, "cumf")

                def scaled(n):
                    h, i = divmod(n, T)
                    if n >= 3:
                        act.wait_ge(max_ready, n - 2)
                    ps = until_filled(act, ("qk", n))
                    act.activation(logit[n % 3][:, 0:P * (i + 1)], ps[:, 0:P * (i + 1)], ACT.Identity, scale=ASCALE,
                                   bias=cumf[:, i, h:h + 1]).then_inc(drained[MARK[("qk", n)][0]], 1)

                def soften(n):
                    h, i = divmod(n, T)
                    act.wait_ge(max_ready, n + 1)
                    if n >= 3:
                        until_filled(act, ("pT", n - 3))
                    if i == 0 and h >= 2:
                        until_drained(act, ("o", h - 2))
                    nk = P * (i + 1)
                    act.activation(prob[n % 3][:, 0:nk], shifted[n % 3][:, 0:nk], ACT.Exp, bias=mx[:, 4 + n % 4:5 + n % 4],
                                   accum_out=rsum[:, h % 2, i:i + 1]).then_inc(prob_ready, 1)
                NU = AH * T
                scaled(0)
                scaled(1)
                for n in range(NU):
                    if n + 2 < NU:
                        scaled(n + 2)
                    soften(n)
                move_turned("oT", 0, HT)
                root(4)

            if phases >= 2:
                experts(0)
            if phases >= 3:
                attention()
            if phases >= 4:
                experts(1)

        @block.vector
        def _(dve):
            steps = [0]

            def step(ins):
                ins.then_inc(dve_step, 1)
                steps[0] += 1

            def settle():
                dve.wait_ge(dve_step, steps[0])

            def move(key, dst):
                ps = until_filled(dve, key)
                dve.tensor_copy(dst, ps).then_inc(drained[MARK[key][0]], 1)

            def move_turned(name, half, dst):
                for t in range(T):
                    ps = until_filled(dve, (name, t, half))
                    dve.tensor_copy(dst[:, 4 * half:4 * half + 4, TILES[t]],
                                    ps.rearrange("p (a b) -> p a b", a=4)).then_inc(drained[MARK[(name, t, half)][0]], 1)

            def move_modulated(name, half, dst, scale, shift):
                for t in range(T):
                    ps = until_filled(dve, (name, t, half))
                    for j in range(4):
                        k = 4 * half + j
                        ins = dve.tensor_scalar(dst[:, k, TILES[t]], ps[:, P * j:P * j + P],
                                                mod[:, scale + k:scale + k + 1], mod[:, shift + k:shift + k + 1],
                                                ALU.mult, ALU.add)
                    ins.then_inc(drained[MARK[(name, t, half)][0]], 1)

            def ada(l, blk):
                ps = until_filled(dve, ("mod", l, blk))
                at = {0: 0, 1: 48, "kv": 96}[l] + 4 * blk
                add1 = 1.0 if (blk // 2 in (1, 2, 4, 5)) else 0.0
                dve.scalar_tensor_tensor(mod[:, at:at + 4], ps[:, 0:4], add1, modb[:, at:at + 4], ALU.add,
                                         ALU.add).then_inc(drained[MARK[("mod", l, blk)][0]], 1)

            def until_mod(l, v):
                until_drained(dve, ("mod", l, 2 * v))
                until_drained(dve, ("mod", l, 2 * v + 1))

            def diagonals(l, v, dst):
                until_mod(l, v)
                for k in range(KC):
                    col = MODC[(l, v)] + k
                    ins = dve.tensor_scalar(dst[:, k, :], ident[:, :], mod[:, col:col + 1], None, ALU.mult)
                ins.then_inc(diag_ready, 1)

            def soft(ins):
                ins.then_inc(soft_dve, 1)
                softs[0] += 1

            softs = [0]

            def softplus(x, out, n, act0):
                t_, u_, l_, m_ = (sp[i][:, 0:n] for i in range(4))
                dve.wait_ge(soft_act, act0 + 2)
                soft(dve.tensor_scalar(u_, t_, 1.0, None, ALU.add))
                dve.wait_ge(soft_act, act0 + 3)

                def then(ins):
                    soft(ins)
                    dve.wait_ge(soft_dve, softs[0])
                then(dve.tensor_scalar(u_, u_, -1.0, None, ALU.add))
                then(dve.tensor_scalar(m_, u_, 0.0, None, ALU.is_equal))
                then(dve.tensor_tensor(u_, u_, m_, ALU.add))
                then(dve.tensor_tensor(l_, l_, m_, ALU.add))
                then(dve.reciprocal(u_, u_))
                then(dve.tensor_tensor(l_, l_, u_, ALU.mult))
                then(dve.tensor_tensor(l_, l_, t_, ALU.mult))
                step(dve.scalar_tensor_tensor(out, x, 0.0, l_, ALU.max, ALU.add))
                settle()

            ps = until_filled(dve, "vecs")
            for r, n in enumerate((120, 120, XT)):
                ins = dve.tensor_copy(cols[:, r, 0:n], ps[:, P * r:P * r + n])
            ins.then_inc(drained[4], 1)
            until_drained(dve, "vecs")
            for blk in range(4):
                ada(0, blk)
            until_mod(0, SHIFT1)
            until_mod(0, SCALE1)
            move_modulated("hT0", 1, HT, MODC[(0, SCALE1)], MODC[(0, SHIFT1)])
            dve.wait_ge(small_in, SMALL)
            ps = until_filled(dve, "dt")
            dve.tensor_tensor(dtx[:, :, :], ps[:, 0:P].rearrange("p (a b) -> p a b", a=T),
                              dtb_bc.unsqueeze(1).to_broadcast([P, T, HEADS]), ALU.add).then_inc(drained[6], 1)
            until_drained(dve, "dt")
            softplus(dtx[:, :, :].rearrange("p a b -> p (a b)"), dts[:, :, :].rearrange("p a b -> p (a b)"), P, 1)
            step(dve.tensor_scalar(negA[:, :], negA[:, :], -1.0, None, ALU.mult))
            settle()
            dve.tensor_tensor(dA[:, :, :], dts[:, :, :], negA[:, :].unsqueeze(1).to_broadcast([P, T, HEADS]),
                              ALU.mult).then_inc(dA_ready, 1)

            n = 0
            for key in stream_order():
                if key[0] == "ada":
                    ada(key[1], key[2])
                elif key[0] == "xbc":
                    for j in range(4 * key[1], 4 * key[1] + 4):
                        ps = until_filled(dve, ("xbc", j))
                        dve.wait_ge(acc_ready, n + 1)
                        for s in range(1, CONV):
                            ins = dve.scalar_tensor_tensor(conv_acc[n % 2][:, s:S], ps[:, 0:S - s],
                                                           convw[:, CONV - 1 - s, j:j + 1], conv_acc[n % 2][:, s:S],
                                                           ALU.mult, ALU.add)
                            if s < CONV - 1:
                                step(ins)
                                settle()
                        ins.then_inc(drained[MARK[("xbc", j)][0]], 1)
                        n += 1

            dve.wait_ge(conv_done, CT)

            def heads(v):
                return v.rearrange("p (h d) -> p h d", h=GH)

            def bch(v):
                return v.unsqueeze(2).to_broadcast([P, GH, HD])

            def scan_a(q):
                ch, g = divmod(q, GROUPS)
                hs = slice(GH * g, GH * g + GH)
                ps = until_filled(dve, ("xs", q))
                if q >= 2:
                    dve.wait_ge(xdte_ready, min(q - 1, NQ - GROUPS))
                    until_drained(dve, ("yd", q - 2))
                dve.tensor_tensor(heads(xdt[q % 2]), heads(ps), bch(dts[:, ch, hs]), ALU.mult).then_inc(xdt_ready, 1)
                dve.tensor_tensor(heads(xsD[q % 2]), heads(ps), bch(dsk_bc[:, hs]), ALU.mult).then_inc(drained[4], 1)
                ps = until_filled(dve, ("bc", q))
                dve.tensor_copy(Btok[q % 2], ps[:, 0:P])
                dve.tensor_tensor(CBm[q % 2], ps[:, P:2 * P], upper[:, :], ALU.mult).then_inc(drained[5], 1)

            def scan_g(q):
                until_drained(dve, ("bc", q))
                for half in range(2):
                    until_drained(dve, ("seg", q, half))
                    if q:
                        until_filled(dve, ("yd", q - 1))
                    dve.tensor_tensor(mixm[half].rearrange("p (h l) -> p h l", h=4),
                                      decay[half].rearrange("p (h l) -> p h l", h=4),
                                      CBm[q % 2].unsqueeze(1).to_broadcast([P, 4, P]), ALU.mult).then_inc(mixm_ready, 1)

            def scan_b(q):
                ch, g = divmod(q, GROUPS)
                hs = slice(GH * g, GH * g + GH)
                if q >= 2:
                    dve.wait_ge(yz_ready, q - 1)
                if ch:
                    ps = until_filled(dve, ("yoff", q))
                    until_drained(dve, ("sums", ch))
                    dve.tensor_tensor(heads(yoff[q % 2]), heads(ps), bch(exps[ch % 2][:, hs]), ALU.mult).then_inc(drained[6], 1)
                if ch < T - 1:
                    ps = until_filled(dve, ("st", q))
                    if ch:
                        dve.wait_ge(state_scaled, q - GROUPS + 1)
                        dve.tensor_tensor(state[:, g, :], state[:, g, :], ps, ALU.add).then_inc(drained[3], 1)
                    else:
                        dve.tensor_copy(state[:, g, :], ps).then_inc(drained[3], 1)
                ps = until_filled(dve, ("yd", q))
                until_drained(dve, ("xs", q))
                dve.tensor_tensor(yg[q % 2], ps, xsD[q % 2], ALU.add).then_inc(drained[7], 1)

            def move_y(ch):
                for g in range(2, 4):
                    ps = until_filled(dve, ("yT", ch, g))
                    for j in range(4):
                        k = 4 * g + j
                        ins = dve.tensor_scalar(xbcT[:, k, TILES[ch]], ps[:, P * j:P * j + P], normw[:, k:k + 1], None,
                                                ALU.mult)
                    ins.then_inc(drained[MARK[("yT", ch, g)][0]], 1)
            scan_a(0)
            for q in range(NQ):
                scan_g(q)
                if q + 1 < NQ:
                    scan_a(q + 1)
                scan_b(q)
                if q % GROUPS == 0 and q:
                    move_y(q // GROUPS - 1)
            dve.wait_ge(squared, NQ)
            step(dve.tensor_reduce(ssum[:, :], ssq[:, :, :], AX, ALU.add))
            settle()
            dve.tensor_scalar(sd[:, :], ssum[:, :], 1.0 / DI, EPS, ALU.mult, ALU.add).then_inc(var_ready, 1)
            diagonals(0, GATE1, diag_mix)
            move_y(T - 1)
            dve.wait_ge(sd_ready, 1)
            step(dve.reciprocal(rsy[:, :], sd[:, :]))
            settle()

            def mixed(l, R):
                for half in range(2):
                    until_drained(dve, ((("g1", l), half)))
                for n in range(2):
                    for t in range(T):
                        r = R[:, t, 512 * n:512 * n + 512]
                        ps = until_filled(dve, ("mix", l, n, t))
                        gb = g1bc[:, 512 * n:512 * n + 512]
                        if l == 0:
                            ins = dve.scalar_tensor_tensor(r, ps, rsy[:, t:t + 1], gb, ALU.mult, ALU.mult)
                        else:
                            ins = dve.tensor_tensor(r, ps, gb, ALU.mult)
                        ins.then_inc(drained[MARK[("mix", l, n, t)][0]], 1)
                        until_drained(dve, ("mix", l, n, t))
                        step(dve.scalar_tensor_tensor(r, X[:, t, 512 * n:512 * n + 512], ALPHA, r, ALU.mult, ALU.add))

            def layer_norm(k, R, lnrow):
                settle()
                for t in range(T):
                    for n in range(2):
                        ins = dve.bn_stats(bn[:, t, n, :], R[:, t, 512 * n:512 * n + 512])
                step(ins)
                settle()
                for t in range(T):
                    ins = dve.bn_aggr(mv[:, t, :], bn[:, t, :, :])
                step(ins)
                settle()
                dve.tensor_scalar(sd[:, :], mv[:, :, 1], EPS, None, ALU.add).then_inc(var_ready, 1)
                dve.wait_ge(sd_ready, k + 2)
                step(dve.reciprocal(rstd[:, :], sd[:, :]))
                settle()
                dve.wait_ge(lnrow_in, 32 * (k + 1))
                for t in range(T):
                    step(dve.tensor_scalar(X[:, t, :], R[:, t, :], mv[:, t, 0:1], rstd[:, t:t + 1], ALU.subtract, ALU.mult))
                    settle()
                    dve.tensor_tensor(X[:, t, :], X[:, t, :], lnrow[0], ALU.mult).then_inc(ln_scaled, 1)
            mixed(0, Rmix[0])
            layer_norm(0, Rmix[0], lnrow_mix)

            def experts(l):
                dve.wait_ge(x_ready, T * (2 * l + 1))
                diagonals(l, SCALE2, diag_moe)
                until_filled(dve, (("s2", l), 1))
                diagonals(l, SHIFT2, diag_moe)
                until_filled(dve, (("sh2", l), 1))
                diagonals(l, GATE2, diag_moe)
                for half in range(2):
                    until_drained(dve, (("s2", l), half))
                for t in range(T):
                    dve.tensor_tensor(H2[:, t, :], X[:, t, :], s2bc, ALU.mult).then_inc(h2_scaled, 1)
                move_turned(("h2T", l), 1, HT)

                until_drained(dve, ("router", l))
                step(dve.tensor_tensor(sel[:, :, :], scores[:, :, :], rb_bc[l].unsqueeze(1).to_broadcast([P, T, E]), ALU.add))
                settle()
                for t in range(T):
                    for g in range(EG):
                        ins = dve.max(top8[:, EG * t + g, :], sel[:, t, EPG * g:EPG * g + EPG])
                step(ins)
                settle()
                step(dve.tensor_tensor(gsc[:, :, :].rearrange("p a b -> p (a b)"), top8[:, :, 0], top8[:, :, 1], ALU.add))
                settle()
                for t in range(T):
                    other = gsc[:, t, :].unsqueeze(1).to_broadcast([P, EG, EG])
                    own = gsc[:, t, :].unsqueeze(2).to_broadcast([P, EG, EG])
                    dve.tensor_tensor(gcmp[0][:, t, :, :], other, own, ALU.is_gt)
                    step(dve.tensor_tensor(gcmp[1][:, t, :, :], other, own, ALU.is_equal))
                    settle()
                    step(dve.tensor_tensor(gcmp[1][:, t, :, :], gcmp[1][:, t, :, :], low8[:, :, :], ALU.mult))
                    settle()
                    step(dve.tensor_tensor(gcmp[0][:, t, :, :], gcmp[0][:, t, :, :], gcmp[1][:, t, :, :], ALU.add))
                settle()
                step(dve.tensor_reduce(grank[:, :, :].rearrange("p a b -> p (a b)"),
                                       gcmp[0][:, :, :, :].rearrange("p a b c -> p (a b) c"), AX, ALU.add))
                settle()
                step(dve.tensor_scalar(grank[:, :, :], grank[:, :, :], float(TOPG), -BIG, ALU.is_ge, ALU.mult))
                settle()
                step(dve.tensor_tensor(sel[:, :, :].rearrange("p t (g e) -> p (t g) e", g=EG),
                                       sel[:, :, :].rearrange("p t (g e) -> p (t g) e", g=EG),
                                       grank[:, :, :].rearrange("p a b -> p (a b)").unsqueeze(2).to_broadcast([P, T * EG, EPG]),
                                       ALU.add))
                settle()
                for t in range(T):
                    ins = dve.max(top8[:, t, :], sel[:, t, :])
                step(ins)
                settle()
                for t in range(T):
                    ins = dve.match_replace(pos[:, t, :], top8[:, t, :], sel[:, t, :], -3.0e38)
                step(ins)
                settle()
                step(dve.tensor_tensor(mask[:, :, :], pos[:, :, :], sel[:, :, :], ALU.not_equal))
                settle()
                for t in range(T):
                    ins = dve.tensor_tensor_scan(krank[:, t, :], mask[:, t, :], mask[:, t, :], 0.0, ALU.add, ALU.bypass)
                step(dve.tensor_copy(mask_b[:, :, :], mask[:, :, :]))
                settle()
                step(dve.tensor_tensor(krank[:, :, :], krank[:, :, :], mask[:, :, :], ALU.subtract))
                settle()
                dve.tensor_copy(V[:, :, :, 2], krank[:, :, :]).then_inc(mask_ready, 1)
                ps = until_filled(dve, ("places", l))
                step(dve.scalar_tensor_tensor(pos[:, :, :].rearrange("p a b -> p (a b)"),
                                              mask[:, :, :].rearrange("p a b -> p (a b)"), -4096.0, ps[:, 0:T * E],
                                              ALU.mult, ALU.add))
                dve.tensor_reduce(most[:, 0:1], ps[:, E * T:E * T + E], AX, ALU.max).then_inc(drained[7], 1)
                until_drained(dve, ("places", l))
                dve.tensor_copy(mosti[:, :], most[:, :]).then_inc(most_ready, 1)
                settle()
                step(dve.tensor_scalar(pos[:, :, :], pos[:, :, :], 4096.0, None, ALU.add))
                settle()

                def build_table(n0):
                    for e in range(E):
                        if e >= 2:
                            dve.wait_ge(onehot_used, (E - 1) * (n0 // E) + e - 1)
                        for t in range(T):
                            ins = dve.tensor_scalar(onehot[e % 2][:, t, :], slot_no[:, :], pos[:, t, e:e + 1], None,
                                                    ALU.is_equal)
                        ins.then_inc(onehot_ready, 1)
                    ps = until_filled(dve, ("table", l))
                    dve.tensor_reduce(destf[:, :], ps[:, 0:3 * E].rearrange("p (e c) -> p e c", c=3), AX,
                                      ALU.add).then_inc(drained[4], 1)
                    until_drained(dve, ("table", l))
                    step(dve.tensor_scalar(table[:, :, 0], destf[:, :], float(NOWHERE), None, ALU.add))
                    settle()
                    dve.tensor_scalar(table[:, :, 1], table[:, :, 0], 3, None,
                                      ALU.logical_shift_right).then_inc(table_ready, 1)
                build_table(E * l)

                step(dve.tensor_tensor(gate[:, :, :], mask[:, :, :], scores[:, :, :], ALU.mult))
                settle()
                step(dve.tensor_reduce(gsum[:, :], gate[:, :, :], AX, ALU.add))
                settle()
                step(dve.reciprocal(gsum[:, :], gsum[:, :]))
                settle()
                for t in range(T):
                    ins = dve.tensor_scalar(gate[:, t, :], gate[:, t, :], gsum[:, t:t + 1], ROUTED_SCALE, ALU.mult, ALU.mult)
                step(ins)
                settle()
                for k in range(TOPK):
                    step(dve.scalar_tensor_tensor(sel[:, :, :].rearrange("p a b -> p (a b)"),
                                                  krank[:, :, :].rearrange("p a b -> p (a b)"), float(k),
                                                  gate[:, :, :].rearrange("p a b -> p (a b)"), ALU.is_equal, ALU.mult))
                    settle()
                    step(dve.tensor_reduce(gk[:, :, k], sel[:, :, :], AX, ALU.add))
                    settle()

                base = MARK[("loop", l)]

                def rows_in(g, u):
                    dve.wait_ge(filled[4], base[4] + SLOTS * g + u + 1)
                    dve.tensor_copy(xeT[u % 2][:, 4:8, :], psum[:, 4, :].rearrange("p (a b) -> p a b", a=4)).then_inc(drained[4], 1)

                def glu(g, u):
                    b = 5 + u % 2
                    dve.wait_ge(filled[b], base[b] + 4 * g + u // 2 + 1)
                    dve.wait_ge(drained[1 + u % 2], base[1 + u % 2] + 4 * g + u // 2 + 1)
                    dve.tensor_tensor(aT[u % 2], s1[u % 2], psum[:, b, 0:P], ALU.mult).then_inc(drained[b], 1)

                def rows_out(g, u, first=False):
                    dve.wait_ge(filled[7], base[7] + SLOTS * g + u + 1)
                    if not (first and u < 2 and l == 0):
                        dve.wait_ge(y_out[u % 2], 16 * (4 * g + u // 2) + 16 * (E // 2) * l)
                    dve.tensor_copy(yrow[u % 2][:, 512:1024], psum[:, 7, :]).then_inc(drained[7], 1)

                def group(g, first=False, last=False):
                    for u in range(SLOTS):
                        if not (last and u == SLOTS - 1):
                            rows_in(*((g, u + 1) if u + 1 < SLOTS else (g + 1, 0)))
                        glu(g, u)
                        if u:
                            rows_out(g, u - 1, first)
                        elif not first:
                            rows_out(g - 1, SLOTS - 1)
                rows_in(0, 0)
                group(0, first=True)
                with dve.Fori(1, NG - 1) as g:
                    group(g)
                group(NG - 1, last=True)
                rows_out(NG - 1, SLOTS - 1)

                def more_blocks():
                    done = more[l]
                    own = [0]

                    def unit(b, e):
                        i = E * b + e
                        OWN = 3

                        def own_step(ins, n):
                            ins.then_inc(done["step"], 1)
                            dve.wait_ge(done["step"], OWN * i + n)
                        dve.tensor_copy(V1[:, :, 0:3], V[:, :, bass.ds(e, 1), :].rearrange("p t o c -> p (t o) c"))
                        own_step(dve.tensor_copy(pos1[:, :], pos[:, :, bass.ds(e, 1)].rearrange("p t o -> p (t o)")), 1)
                        own_step(dve.tensor_scalar(pos1[:, :], pos1[:, :], -float(P * (b + 1)), None, ALU.add), 2)
                        for t in range(T):
                            ins = dve.tensor_scalar(onehot[0][:, t, :], slot_no[:, :], pos1[:, t:t + 1], None, ALU.is_equal)
                        ins.then_inc(done["onehot"], 1)
                        dve.wait_ge(done["dest"], i + 1)
                        own_step(dve.tensor_reduce(destf[:, 0:1], psum[:, 6, 0:3], AX, ALU.add), 3)
                        dve.tensor_scalar(idx[0][:, 0:1], destf[:, 0:1], float(NOWHERE), None, ALU.add).then_inc(done["idx"], 1)
                        dve.wait_ge(done["idx"], 2 * i + 1)
                        dve.tensor_scalar(idx[0][:, 1:2], idx[0][:, 0:1], 3, None, ALU.logical_shift_right).then_inc(done["idx"], 1)
                        dve.wait_ge(done["turned"], i + 1)
                        dve.tensor_copy(xeT[0][:, 4:8, :], psum[:, 1, :].rearrange("p (a b) -> p a b", a=4)
                                        ).then_inc(done["moved"], 1)
                        dve.wait_ge(done["silu"], i + 1)
                        dve.tensor_tensor(aT[0], s1[0], psum[:, 3, 0:P], ALU.mult).then_inc(done["gated"], 1)
                        dve.wait_ge(done["down"], i + 1)
                        dve.tensor_copy(yrow[0][:, 512:1024], psum[:, 5, :]).then_inc(done["yrow"], 1)
                        dve.wait_ge(done["sent"], 16 * i + 16)
                    for b in range(2):
                        dve.wait_ge(y_out[b], 16 * (E // 2) * (l + 1))
                    for b in range(MORE):
                        with dve.Fori(0, E) as e:
                            unit(b, e)
                when_more(dve, l, more_blocks)

                settle()
                for t in range(T):
                    for n in range(2):
                        until_drained(dve, ("shared", l, t, n))
                for j in range(4 * T):
                    t, quarter = divmod(j, 4)
                    dve.wait_ge(part_in[j % 2], 16 * (j // 2 + 1 + 2 * T * l))
                    s = SH[:, t, 256 * quarter:256 * quarter + 256]
                    for k in range(TOPK):
                        ins = dve.scalar_tensor_tensor(s, part[j % 2][:, k, :], gk[:, t, k:k + 1], s, ALU.mult, ALU.add)
                        step(ins)
                        settle()
                    PART[l].append(steps[0])
                for t in range(T):
                    step(dve.tensor_tensor(SH[:, t, :], SH[:, t, :], g2bc, ALU.mult))
                    settle()
                    step(dve.scalar_tensor_tensor(SH[:, t, :], X[:, t, :], ALPHA, SH[:, t, :], ALU.mult, ALU.add))
                layer_norm(2 * l + 1, SH, lnrow_moe)

            def attention():
                dve.wait_ge(x_ready, 2 * T)
                diagonals(1, GATE1, diag_mix)
                for v in (0, 1):
                    until_mod("kv", v)
                move_modulated("uT", 1, HT, MODC[("kv", 1)], MODC[("kv", 0)])
                ps = until_filled(dve, "forget")
                x2 = dts[:, 0:2, :].rearrange("p a b -> p (a b)")
                dve.scalar_tensor_tensor(x2.rearrange("p (a b) -> p a b", a=T), ps[:, 0:T * AH].rearrange("p (a b) -> p a b", a=T),
                                         -1.0, fb_bc.unsqueeze(1).to_broadcast([P, T, AH]), ALU.mult,
                                         ALU.subtract).then_inc(drained[6], 1)
                until_drained(dve, "forget")
                soft(dve.tensor_scalar(x2, x2, 1.0, None, ALU.mult))
                softplus(x2, logf[:, :, :].rearrange("p a b -> p (a b)"), T * AH, 4)
                dve.tensor_scalar(logf[:, :, :], logf[:, :, :], -1.0, None, ALU.mult).then_inc(logf_ready, 1)
                for j in range(1, KC, 2):
                    move(("kT", j), kT[:, j, :])
                ps = until_filled(dve, "cumf")
                dve.tensor_copy(cumf[:, :, :].rearrange("p a b -> p (a b)"), ps[:, 0:T * AH]).then_inc(drained[7], 1)
                for n in range(2):
                    for t in range(1, T, 2):
                        move(("v", n, t), vtok[:, t, 512 * n:512 * n + 512])
                ps = until_filled(dve, "cumfT")
                dve.tensor_copy(cumfT[:, :], ps[0:T * AH, 0:P]).then_inc(drained[7], 1)
                move_modulated("qhT", 1, HT, MODC[(1, SCALE1)], MODC[(1, SHIFT1)])
                for j in range(1, KC, 2):
                    move(("qT", j), qT[:, j, :])

                def maximum(n):
                    h, i = divmod(n, T)
                    nk = P * (i + 1)
                    dve.wait_ge(masked, n + 1)
                    if n >= 3:
                        dve.wait_ge(prob_ready, n - 2)
                    ps = until_filled(dve, ("ncf", h))
                    ins = dve.tensor_tensor_reduce(shifted[n % 3][:, 0:nk], logit[n % 3][:, 0:nk], ps[:, 0:nk], 1.0, -3.0e38,
                                                   ALU.subtract, ALU.max, mx[:, n % 4:n % 4 + 1])
                    if i == T - 1:
                        ins.then_inc(drained[MARK[("ncf", h)][0]], 1)
                        until_drained(dve, ("ncf", h))
                    else:
                        step(ins)
                        settle()
                    dve.tensor_scalar(mx[:, 4 + n % 4:5 + n % 4], mx[:, n % 4:n % 4 + 1], -1.0, None, ALU.mult).then_inc(max_ready, 1)

                def move_probs(n):
                    h, i = divmod(n, T)
                    ps = until_filled(dve, ("pT", n))
                    dve.tensor_copy(probT[n % 2][:, 0:i + 1, :], ps[:, 0:P * (i + 1)].rearrange("p (a b) -> p a b", b=P)
                                    ).then_inc(drained[MARK[("pT", n)][0]], 1)

                def head_out(h):
                    ps = until_filled(dve, ("o", h))
                    dve.wait_ge(prob_ready, T * h + T)
                    step(dve.reciprocal(rinv[:, h % 2, :], rsum[:, h % 2, :]))
                    settle()
                    dve.tensor_tensor(otok[:, :, HD * h:HD * h + HD], ps[:, 0:T * HD].rearrange("p (a b) -> p a b", a=T),
                                      rinv[:, h % 2, :].unsqueeze(2).to_broadcast([P, T, HD]), ALU.mult
                                      ).then_inc(drained[MARK[("o", h)][0]], 1)
                NU = AH * T
                maximum(0)
                for n in range(NU):
                    if n + 1 < NU:
                        maximum(n + 1)
                    move_probs(n)
                    if n % T == 1 and n > T:
                        head_out(n // T - 1)
                head_out(AH - 1)
                move_turned("oT", 1, HT)
                mixed(1, Rmix[1])
                layer_norm(2, Rmix[1], lnrow_mix)

            if phases >= 2:
                experts(0)
            if phases >= 3:
                attention()
            if phases >= 4:
                experts(1)

        @block.gpsimd
        def _(pool):
            steps = [0]

            def step(ins):
                ins.then_inc(pool_step, 1)
                steps[0] += 1

            def settle():
                pool.wait_ge(pool_step, steps[0])

            last_row, last_part = pool.alloc_register("last_row"), pool.alloc_register("last_part")
            pool.reg_mov(last_row, S - 1)
            pool.reg_mov(last_part, S * TOPK - 1)
            step(pool.memset(ident[:, :], 0.0))
            step(pool.memset(upper[:, :], 1.0))
            step(pool.memset(after[:, :], 1.0))
            step(pool.memset(before_b[:, :], 1.0))
            step(pool.memset(low8[:, :, :], 1.0))
            pool.memset(ones[:, :], 1.0).then_inc(consts, 1)
            pool.memset(ones_b[:, :], 1.0).then_inc(consts, 1)
            pool.iota(slot_no[:, :], [[1, P]], base=0, channel_multiplier=0,
                      allow_small_or_imprecise_dtypes=True).then_inc(consts, 1)
            pool.iota(V[:, :, :, 0], [[0, T], [0, E]], base=0, channel_multiplier=TOPK,
                      allow_small_or_imprecise_dtypes=True).then_inc(consts, 1)
            pool.iota(V[:, :, :, 1], [[P * TOPK, T], [0, E]], base=-NOWHERE, channel_multiplier=0,
                      allow_small_or_imprecise_dtypes=True).then_inc(consts, 1)
            settle()
            pool.affine_select(out=ident[:, :], in_=ident[:, :], compare_op=ALU.not_equal, fill=1.0, base=0,
                               pattern=[[-1, P]], channel_multiplier=1).then_inc(consts, 1)
            pool.affine_select(out=upper[:, :], in_=upper[:, :], compare_op=ALU.is_ge, fill=0.0, base=0,
                               pattern=[[1, P]], channel_multiplier=-1).then_inc(consts, 1)
            pool.affine_select(out=after[:, :], in_=after[:, :], compare_op=ALU.is_gt, fill=0.0, base=0,
                               pattern=[[-1, P]], channel_multiplier=1).then_inc(consts, 1)
            pool.affine_select(out=before_b[:, :], in_=before_b[:, :], compare_op=ALU.is_gt, fill=0.0, base=0,
                               pattern=[[1, P]], channel_multiplier=-1).then_inc(consts, 1)
            pool.affine_select(out=low8[:, :, :], in_=low8[:, :, :], compare_op=ALU.is_gt, fill=0.0, base=0,
                               pattern=[[1, EG], [-1, EG]], channel_multiplier=0).then_inc(consts, 1)
            pool.wait_ge(consts, CONSTS)

            pool.wait_ge(dA_ready, 1)

            def segments(q):
                ch, g = divmod(q, GROUPS)
                for half in range(2):
                    if q:
                        until_filled(pool, ("seg", q - 1, half))
                    for j in range(4):
                        h = GH * g + 4 * half + j
                        ins = pool.tensor_scalar(stepm[4 * half + j], after[:, :], dA[:, ch, h:h + 1], 1.0, ALU.mult, ALU.mult)
                    ins.then_inc(stepm_ready, 1)

            def heads(v):
                return v.rearrange("p (h d) -> p h d", h=GH)

            def bch(v):
                return v.unsqueeze(2).to_broadcast([P, GH, HD])

            def scan_pool(q):
                ch, g = divmod(q, GROUPS)
                until_drained(pool, ("sums", ch))
                pool.wait_ge(xdt_ready, q + 1)
                if q >= 2 and ch < T - 1:
                    until_filled(pool, ("st", q - 2))
                if ch < T - 1:
                    pool.tensor_tensor(heads(xdte[q % 2]), heads(xdt[q % 2]),
                                       bch(exps[ch % 2][:, HEADS + GH * g:HEADS + GH * g + GH]), ALU.mult).then_inc(xdte_ready, 1)
                if 0 < ch < T - 1:
                    until_filled(pool, ("yoff", q))
                    pool.tensor_tensor(heads(state[:, g, :]), heads(state[:, g, :]),
                                       bch(exps[ch % 2][:, 2 * HEADS + GH * g:2 * HEADS + GH * g + GH]),
                                       ALU.mult).then_inc(state_scaled, 1)
                until_drained(pool, ("yd", q))
                if ch:
                    until_drained(pool, ("yoff", q))
                    step(pool.tensor_tensor(yg[q % 2], yg[q % 2], yoff[q % 2], ALU.add))
                    settle()
                z = zs[:, ch, GW * g:GW * g + GW]
                pool.tensor_tensor(z, yg[q % 2], z, ALU.mult).then_inc(yz_ready, 1)
            segments(0)
            for q in range(NQ):
                if q + 1 < NQ:
                    segments(q + 1)
                scan_pool(q)

            def layer_norm(k, lnrow):
                for t in range(T):
                    pool.wait_ge(ln_scaled, T * k + t + 1)
                    pool.tensor_tensor(X[:, t, :], X[:, t, :], lnrow[1], ALU.add).then_inc(x_ready, 1)
            layer_norm(0, lnrow_mix)

            def experts(l):
                for half in range(2):
                    until_drained(pool, (("sh2", l), half))
                for t in range(T):
                    pool.wait_ge(h2_scaled, T * l + t + 1)
                    pool.tensor_tensor(H2[:, t, :], H2[:, t, :], sh2bc, ALU.add).then_inc(h2_ready, 1)
                for t in range(T):
                    pool.wait_ge(h2_ready, T * l + t + 1)
                    pool.dma_start(rows_dram[TILES[t], :], H2[:, t, :]).then_inc(h2_out, 16)
                until_drained(pool, (("shared_in", l, 0)))
                until_drained(pool, (("shared_in", l, 1)))
                pool.tensor_tensor(aS[0], aS[0], aS[1], ALU.mult).then_inc(sh_gated, 1)
                pool.wait_ge(table_ready, l + 1)
                pool.wait_ge(h2_out, 16 * T * (l + 1))
                base = MARK[("loop", l)]

                def carrier(n):
                    return pool.tensor_tensor(passed[:, n:n + 1], ones[:, 0:1], ones[:, 1:2], ALU.mult)

                def fetch(g, u, first=False):
                    if not first:
                        pool.wait_ge(y_out[u % 2], 16 * (4 * g + u // 2 - 3) + 16 * (E // 2) * l)
                    if not (first and u < 4):
                        pool.wait_ge(filled[4], base[4] + SLOTS * g + u - 3)
                    pool.tensor_copy(idx[u][:, :], table[:, bass.ds(SLOTS * g + u, 1), :].rearrange("p a b -> p (a b)")
                                     ).then_inc(idx_ready[0], 1)
                    pool.wait_ge(idx_ready[0], E * l + SLOTS * g + u + 1)
                    carrier(SLOTS)
                    pool.indirect_dma_start(out=xg[u % 4], out_offset=None, in_=rows_dram,
                                            in_offset=bass.IndirectOffsetOnAxis(ap=idx[u][:, 1:2], axis=0),
                                            bounds_check=last_row, oob_is_err=False).then_inc(xg_in[u % 4], 16)

                def send(g, u):
                    for b in (3, 7):
                        pool.wait_ge(drained[b], base[b] + SLOTS * g + u + 1)
                    carrier(u)
                    pool.indirect_dma_start(out=part_dram,
                                            out_offset=bass.IndirectOffsetOnAxis(ap=idx[u][:, 0:1], axis=0),
                                            in_=yrow[u % 2], in_offset=None,
                                            bounds_check=last_part, oob_is_err=False).then_inc(y_out[u % 2], 16)

                AHEAD = 3

                def group(g, first=False, last=False):
                    for u in range(SLOTS):
                        v = u + AHEAD
                        if v < SLOTS:
                            fetch(g, v, first)
                        elif not last:
                            fetch(g + 1, v - SLOTS)
                        send(g, u)
                for t in range(T):
                    until_filled(pool, ((("h2T", l)), t, 1))
                for u in range(AHEAD):
                    fetch(0, u, True)
                group(0, first=True)
                with pool.Fori(1, NG - 1) as g:
                    group(g)
                group(NG - 1, last=True)

                def more_blocks():
                    done = more[l]

                    def unit(i):
                        pool.wait_ge(done["idx"], 2 * i + 2)
                        carrier(SLOTS + 1).then_inc(done["carried"], 1)
                        pool.indirect_dma_start(out=xg[0], out_offset=None, in_=rows_dram,
                                                in_offset=bass.IndirectOffsetOnAxis(ap=idx[0][:, 1:2], axis=0),
                                                bounds_check=last_row, oob_is_err=False).then_inc(done["rows"], 16)
                        pool.wait_ge(done["yrow"], 2 * i + 2)
                        pool.wait_ge(done["carried"], i + 1)
                        carrier(SLOTS + 2)
                        pool.indirect_dma_start(out=part_dram,
                                                out_offset=bass.IndirectOffsetOnAxis(ap=idx[0][:, 0:1], axis=0),
                                                in_=yrow[0], in_offset=None,
                                                bounds_check=last_part, oob_is_err=False).then_inc(done["sent"], 16)
                    for b in range(MORE):
                        with pool.Fori(0, E) as e:
                            unit(E * b + e)
                when_more(pool, l, more_blocks)
                layer_norm(2 * l + 1, lnrow_moe)

            def attention():
                NU = AH * T
                for n in range(NU):
                    h, i = divmod(n, T)
                    until_drained(pool, ("qk", n))
                    d = logit[n % 3][:, P * i:P * i + P]
                    pool.affine_select(out=d, in_=d, compare_op=ALU.is_ge, fill=-BIG, base=0, pattern=[[-1, P]],
                                       channel_multiplier=1).then_inc(masked, 1)
                layer_norm(2, lnrow_mix)

            if phases >= 2:
                experts(0)
            if phases >= 3:
                attention()
            if phases >= 4:
                experts(1)

        @block.sync
        def _(sp_):
            small = [0]

            def load(dst, src):
                sp_.dma_start(dst, src).then_inc(small_in, 16)
                small[0] += 16

            def as_rows(v, n):
                return v.rearrange("(n p) -> n p", p=P)

            load(rows[0:8, 0, :], c[0].rearrange("(n p) -> n p", p=P))
            load(rows[8:56, 0, :], as_rows(ada_b[0], 48))
            load(rows[56:104, 0, :], as_rows(ada_b[1], 48))
            load(rows[104:120, 0, :], as_rows(kv_ada_b, 16))
            load(rows[0:CONV * CT, 1, :], ssm_conv_w[0].rearrange("k (n p) -> (k n) p", p=P))
            load(rows[CONV * CT:CONV * CT + CT, 1, :], as_rows(ssm_conv_b[0], CT))
            load(rows[0:XT, 2, :], as_rows(ssm_norm_w[0], XT))
            at = 0
            for v in (ssm_dt_bias[0], ssm_a_log[0], ssm_d[0], kv_fb, moe_bias[0], moe_bias[1]):
                n = v.shape[0]
                load(bcs[:, at:at + n], v.partition_broadcast(P))
                at += n
            load(wdt[:, :, :], ssm_w_in[0].rearrange("(k p) n -> p k n", p=P)[:, :, DI + XBC:DI + XBC + HEADS])
            load(wf[:, :, :], kv_w.rearrange("(k p) n -> p k n", p=P)[:, :, 2 * D:2 * D + AH])
            load(wr[:, :, :], moe_w_router[0].rearrange("(k p) n -> p k n", p=P))
            assert small[0] == SMALL, small[0]
            for t in range(T):
                sp_.dma_start(X[:, t, :], x[0, TILES[t], :]).then_inc(x_in, 16)

            def stream(i):
                if i >= RING:
                    b, n = MARK[("item", i - RING)]
                    sp_.wait_ge(filled[b], n)
                sp_.dma_start(ring[i % RING], items[i][1]).then_inc(ring_in[i % RING], 16)
            for i in range(n_items0):
                stream(i)

            def ln_rows(k, dst, g, b):
                sp_.dma_start(dst[0], g.partition_broadcast(P)).then_inc(lnrow_in, 16)
                sp_.dma_start(dst[1], b.partition_broadcast(P)).then_inc(lnrow_in, 16)

            def experts(l):
                b, n = MARK[("mix", l, 1, T - 1)]
                sp_.wait_ge(filled[b], n)
                sp_.dma_start(shw[:, 0, :].rearrange("p (k f) -> p k f", k=KC),
                              moe_ws1[l].rearrange("(k p) f -> p k f", p=P)).then_inc(shw_in, 16)
                sp_.dma_start(shw[:, 1, :].rearrange("p (k f) -> p k f", k=KC),
                              moe_ws3[l].rearrange("(k p) f -> p k f", p=P)).then_inc(shw_in, 16)
                sp_.dma_start(shw[:, 2, :], moe_ws2[l]).then_inc(shw_in, 16)

                def fetch(i, u):
                    for n, w in enumerate((moe_w1, moe_w3)):
                        src = w[l][bass.ds(i, 1), :, :] if not isinstance(i, int) else w[l][i:i + 1, :, :]
                        sp_.dma_start(exp_w[u][:, n, :].rearrange("p (k f) -> p k f", k=KC),
                                      src.rearrange("o (k p) f -> p (o k) f", p=P)).then_inc(exp_in[u], 16)
                    src = moe_w2[l][bass.ds(i, 1), :, :] if not isinstance(i, int) else moe_w2[l][i:i + 1, :, :]
                    sp_.dma_start(exp_w[u][:, 2, :], src.rearrange("o f d -> f (o d)")).then_inc(exp_in[u], 16)
                base = MARK[("loop", l)]
                for u in range(4, SLOTS):
                    fetch(u, u)
                sp_.wait_ge(x_ready, T * (2 * l + 1))
                for u in range(4):
                    fetch(u, u)
                with sp_.Fori(1, NG) as g:
                    for u in range(SLOTS):
                        sp_.wait_ge(filled[7], base[7] + SLOTS * g + u - SLOTS + 1)
                        fetch(SLOTS * g + u, u)
                for b in range(2):
                    sp_.wait_ge(y_out[b], 16 * (E // 2) * (l + 1))

                def more_blocks():
                    done = more[l]

                    def unit(b, e):
                        sp_.wait_ge(done["onehot"], E * b + e + 1)
                        for n, w in enumerate((moe_w1, moe_w3)):
                            sp_.dma_start(exp_w[0][:, n, :].rearrange("p (k f) -> p k f", k=KC),
                                          w[l][bass.ds(e, 1), :, :].rearrange("o (k p) f -> p (o k) f", p=P)
                                          ).then_inc(done["weights"], 16)
                        sp_.dma_start(exp_w[0][:, 2, :], moe_w2[l][bass.ds(e, 1), :, :].rearrange("o f d -> f (o d)")
                                      ).then_inc(done["weights"], 16)
                    for b in range(MORE):
                        with sp_.Fori(0, E) as e:
                            unit(b, e)
                    sp_.wait_ge(done["sent"], 16 * MORE * E)
                when_more(sp_, l, more_blocks)
                ln_rows(2 * l + 1, lnrow_moe, ln2_g[l], ln2_b[l])
                rows_of = part_dram.rearrange("(t p k) d -> t p k d", p=P, k=TOPK)
                for j in range(4 * T):
                    t, quarter = divmod(j, 4)
                    if j >= 2:
                        sp_.wait_ge(dve_step, PART[l][j - 2])
                    sp_.dma_start(part[j % 2], rows_of[t, :, :, 256 * quarter:256 * quarter + 256]).then_inc(part_in[j % 2], 16)

            sp_.wait_ge(squared, NQ)
            until_filled(sp_, ("mix", 0, 0, 0))
            ln_rows(0, lnrow_mix, ln1_g[0], ln1_b[0])
            if phases >= 2:
                experts(0)
            if phases >= 3:
                until_filled(sp_, "wr0")
                sp_.dma_start(wr[:, :, :], moe_w_router[1].rearrange("(k p) n -> p k n", p=P)).then_inc(wr_in, 16)
                for i in range(n_items0, n_items1):
                    if i < n_items0 + RING:
                        sp_.dma_start(ring[i % RING], items[i][1]).then_inc(ring_in[i % RING], 16)
                    else:
                        stream(i)
                until_filled(sp_, ("mix", 1, 0, 0))
                ln_rows(2, lnrow_mix, ln1_g[1], ln1_b[1])
            if phases >= 4:
                experts(1)
            for t in range(T):
                sp_.wait_ge(x_ready, T * (phases - 1) + t + 1)
                sp_.dma_start(out[0, TILES[t], :], X[:, t, :]).then_inc(out_done, 16)
            sp_.wait_ge(out_done, 16 * T)


_INS = ["x", "c", "ada_w", "ada_b", "ln1_g", "ln1_b", "ln2_g", "ln2_b", "ssm_w_in", "ssm_conv_w", "ssm_conv_b",
        "ssm_dt_bias", "ssm_a_log", "ssm_d", "ssm_norm_w", "ssm_w_out", "kv_ada_w", "kv_ada_b", "kv_w", "kv_fb",
        "attn_w_q", "attn_w_o", "moe_w_router", "moe_bias", "moe_w1", "moe_w3", "moe_w2", "moe_ws1", "moe_ws3",
        "moe_ws2"]
_OUTS = [((1, 512, 1024), "float32")]


def kernel(**inputs):
    import numpy as _np
    import concourse.bacc as _bacc
    from concourse import mybir as _mybir
    from concourse.bass_utils import run_bass_kernel_spmd as _run

    nc = _bacc.Bacc("TRN2", target_bir_lowering=False, num_devices=1)
    arrays, args = {}, []
    for name in _INS:
        a = _np.ascontiguousarray(inputs[name])
        arrays[f"in_{name}_dram"] = a
        args.append(nc.dram_tensor(f"in_{name}_dram", a.shape, _mybir.dt.from_np(a.dtype), kind="ExternalInput").ap())
    for i, (shape, dtype) in enumerate(_OUTS):
        dt = _mybir.dt.from_np(_np.dtype(dtype))
        args.append(nc.dram_tensor(f"out_{i}_dram", shape, dt, kind="ExternalOutput").ap())
    trunk(nc, *args)
    r = _run(nc, [arrays], core_ids=[0])
    got = tuple(r.results[0][f"out_{i}_dram"] for i in range(len(_OUTS)))
    return got[0]
```

```python
from contextlib import ExitStack

import concourse.bass as bass
from concourse import mybir

F32 = mybir.dt.float32
BF16 = mybir.dt.bfloat16
I32 = mybir.dt.int32
ALU = mybir.AluOpType
ACT = mybir.ActivationFunctionType
AX = mybir.AxisListType.X

P = 128
D = 1024
S = 512
T = S // P
KC = D // P
DI = 2048
HEADS = 32
HD = 64
GROUPS = 4
NST = 128
GH = HEADS // GROUPS
GW = GH * HD
GN = GROUPS * NST
CONV = 4
XBC = DI + 2 * GN
XT = DI // P
CT = XBC // P
AH = 16
E = 64
EG = 8
EPG = E // EG
TOPG = 4
TOPK = 8
F = D // 8
ROUTED_SCALE = 2.5
ALPHA = 4.0 ** 0.25
EPS = 1e-5
ASCALE = HD ** -0.5
BIG = 1.0e30
RING = 3
SLOTS = 8
YROWS = 4
NOWHERE = 2 * S * TOPK


def trunk(nc, x, c, ada_w, ada_b, ln1_g, ln1_b, ln2_g, ln2_b, ssm_w_in, ssm_conv_w, ssm_conv_b,
          ssm_dt_bias, ssm_a_log, ssm_d, ssm_norm_w, ssm_w_out, kv_ada_w, kv_ada_b, kv_w, kv_fb,
          attn_w_q, attn_w_o, moe_w_router, moe_bias, moe_w1, moe_w3, moe_w2, moe_ws1, moe_ws3,
          moe_ws2, out, phases=4, cap=P):
    ctx = ExitStack()
    with ctx:
        def sb(name, shape, dt=F32):
            return ctx.enter_context(nc.sbuf_tensor(name, shape, dt))

        def sem(name):
            return ctx.enter_context(nc.semaphore(name))

        KB = 256
        arena = sb("arena", [P, 191 * KB])

        def view(kb, *dims):
            n = 1
            for d in dims:
                n *= d
            v = arena[:, int(kb * KB):int(kb * KB) + n]
            names = "abcd"[:len(dims)]
            if len(dims) == 1:
                return v
            return v.rearrange(f"p ({' '.join(names)}) -> p {' '.join(names)}",
                               **dict(zip(names[1:], dims[1:])))

        X = view(0, T, D)
        HT = view(16, KC, S)
        ring = [view(143 + 16 * r, KC, 512) for r in range(RING)]
        exp_w = [view(95 + 12 * r, 3, 1024) for r in range(SLOTS)]
        xbcT = view(32, CT, S)
        zs = view(80, T, DI)
        ada_dve = view(120, KC, 512)
        ada_pool = [view(80 + 16 * i, KC, 512) for i in range(2)]
        ada_acc = [view(116 + 2 * i, 512) for i in range(2)]
        conv_acc = [view(112 + 2 * i, S) for i in range(2)]
        xdt = [view(112 + 2 * i, GW) for i in range(2)]
        xsD = [view(116 + 2 * i, GW) for i in range(2)]
        xdte = [view(120 + 2 * i, GW) for i in range(2)]
        decay = [view(124 + 2 * i, 4 * P) for i in range(2)]
        mixm = [view(128 + 2 * i, 4 * P) for i in range(2)]
        stepm = [view(132 + 0.5 * i, P) for i in range(8)]
        Btok = [view(136 + 0.5 * i, P) for i in range(2)]
        CBm = [view(137 + 0.5 * i, P) for i in range(2)]
        state = view(16, GROUPS, GW)
        yg = [view(24 + 2 * i, GW) for i in range(2)]
        yoff = [view(28 + 2 * i, GW) for i in range(2)]
        sq_out = zs
        kT = view(32, KC, S)
        vtok = view(48, T, D)
        qT = view(64, KC, S)
        otok = view(80, T, D)
        logit = [view(96 + 2 * i, S) for i in range(3)]
        shifted = [view(102 + 2 * i, S) for i in range(3)]
        prob = [view(108 + 2 * i, S) for i in range(3)]
        probT = [view(114 + 2 * i, T, P) for i in range(2)]
        g1bc = view(139, D)
        Rmix = [view(16, T, D), view(32, T, D)]
        lnrow_mix = [view(112, D), view(116, D)]
        diag = {name: view(120 + 4 * i, KC, P) for i, name in enumerate(("g1", "s2", "sh2", "g2"))}
        H2 = view(32, T, D)
        SH = view(48, T, D)
        s2bc = view(68, D)
        sh2bc = view(72, D)
        g2bc = view(76, D)
        shw = view(80, 3, 1024)
        aS = [view(92, S), SH[:, T - 1, 512:1024]]
        xg = [view(32 + 4 * i, D) for i in range(4)]
        xeT = [view(80 + 4 * i, KC, P) for i in range(2)]
        s1 = [view(88 + 0.5 * i, P) for i in range(2)]
        aT = [view(89 + 0.5 * i, P) for i in range(2)]
        yrow = [view(16 + 4 * i, D) for i in range(YROWS)]
        part = [view(kb, TOPK, 512) for kb in (95, 111, 32)]
        lnrow_moe = [view(80, D), view(84, D)]
        scores, sel, mask, gate, krank = (view(64 + i, T, E) for i in range(5))
        top8 = view(70, T * EG, 8)
        gcmp = [view(71 + i, T, EG, EG) for i in range(2)]
        pos = view(72, T, E)

        def view_b(kb, *dims):
            v = view(kb, dims[0] * dims[1] // 2).bitcast(BF16)
            return v.rearrange("p (a b) -> p a b", b=dims[1])
        mask_b = view_b(73, T, E)
        onehot = [view_b(73.5 + i, T, P) for i in range(2)]

        ident = sb("ident", [P, P])
        upper = sb("upper", [P, P])
        after = sb("after", [P, P])
        ones = sb("ones", [P, P])
        before_b = sb("before_b", [P, P], BF16)
        ones_b = sb("ones_b", [P, P], BF16)
        slot_no = sb("slot_no", [P, P], BF16)
        low8 = sb("low8", [P, EG, EG])
        cols = sb("cols", [P, 3, P])
        bcs = sb("bcs", [P, 240])
        condT = sb("condT", [P, KC])
        mod = sb("mod", [P, 112])
        wdt = view(139, KC, HEADS)
        wf = sb("wf", [P, KC, AH])
        wr = sb("wr", [P, KC, E])
        dtx = sb("dtx", [P, T, HEADS])
        dts = sb("dts", [P, T, HEADS])
        dA = sb("dA", [P, T, HEADS])
        negA = sb("negA", [P, HEADS])
        sp_all = sb("sp", [P, 4, P])
        sp = [sp_all[:, i, :] for i in range(4)]
        rows = sp_all[:, 0:3, :]
        logf = sb("logf", [P, T, AH])
        ssum = sb("ssum", [P, T])
        exps = [sb(f"exps{i}", [P, 96]) for i in range(2)]
        ssq = sb("ssq", [P, T, GROUPS])
        rsy = sb("rsy", [P, T])
        cumf = sb("cumf", [P, T, AH])
        cumfT = sb("cumfT", [T * AH, P])
        mx = sb("mx", [P, 8])
        rsum = sb("rsum", [P, 2, T])
        rinv = sb("rinv", [P, 2, T])
        bn = sb("bn", [P, T, 2, 6])
        mv = sb("mv", [P, T, 2])
        sd = sb("sd", [P, T])
        rstd = sb("rstd", [P, T])
        gsc = sb("gsc", [P, T, EG])
        grank = sb("grank", [P, T, EG])
        gk = sb("gk", [P, T, TOPK])
        gsum = sb("gsum", [P, T])
        V = sb("V", [P, T, E, 3], BF16)
        destf = sb("destf", [P, E])
        table = view(90, E, 2).bitcast(I32)
        pos1 = view(74.75, T)
        V1 = view_b(74.5, T, 4)
        idx = [sb(f"idx{i}", [P, 2], I32) for i in range(8)]
        passed = sb("passed", [P, SLOTS + 3])
        most = sb("most", [P, 1])
        mosti = sb("mosti", [P, 1], I32)
        psum = ctx.enter_context(nc.psum_tensor("psum", [P, 8, 512], F32))

        rows_dram = nc.dram_tensor("h2_rows", [S, D], F32, kind="Internal").ap()
        part_dram = nc.dram_tensor("expert_rows", [S * TOPK, D], F32, kind="Internal").ap()

        c_col = cols[:, 0, 0:8]
        modb = cols[:, 0, 8:120]
        convw = cols[:, 1, 0:CONV * CT].rearrange("p (k j) -> p k j", k=CONV)
        convb = cols[:, 1, CONV * CT:CONV * CT + CT]
        normw = cols[:, 2, 0:XT]
        dtb_bc, alog_bc, dsk_bc, fb_bc = bcs[:, 0:32], bcs[:, 32:64], bcs[:, 64:96], bcs[:, 96:112]
        rb_bc = [bcs[:, 112:176], bcs[:, 176:240]]
        MODC = {(l, v): 48 * l + 8 * v for l in range(2) for v in range(6)}
        MODC[("kv", 0)], MODC[("kv", 1)] = 96, 104
        SHIFT1, SCALE1, GATE1, SHIFT2, SCALE2, GATE2 = range(6)

        filled = [sem(f"filled{b}") for b in range(8)]
        drained = [sem(f"drained{b}") for b in range(8)]
        ring_in = [sem(f"ring_in{r}") for r in range(RING)]
        exp_in = [sem(f"exp_in{r}") for r in range(SLOTS)]
        rows_in_sem = sem("rows_in")
        small_in = sem("small_in")
        ada_dve_in = [sem(f"ada_dve_in{i}") for i in range(2)]
        ada_half = sem("ada_half")
        ada_pool_in = [sem(f"ada_pool_in{i}") for i in range(2)]
        ada_scaled = sem("ada_scaled")
        ada_summed = [sem(f"ada_summed{i}") for i in range(2)]
        x_in = sem("x_in")
        consts = sem("consts")
        act_step = sem("act_step")
        dve_step = sem("dve_step")
        pool_step = sem("pool_step")
        vec_cols = sem("vec_cols")
        cond_ready = sem("cond_ready")
        acc_ready = sem("acc_ready")
        conv_done = sem("conv_done")
        soft_act = sem("soft_act")
        soft_dve = sem("soft_dve")
        dA_ready = sem("dA_ready")
        exps_ready = sem("exps_ready")
        stepm_ready = sem("stepm_ready")
        xdt_ready = sem("xdt_ready")
        xdte_ready = sem("xdte_ready")
        decay_ready = sem("decay_ready")
        mixm_ready = sem("mixm_ready")
        state_scaled = sem("state_scaled")
        yz_ready = sem("yz_ready")
        squared = sem("squared")
        diag_ready = sem("diag_ready")
        bc_ready = sem("bc_ready")
        res_ready = sem("res_ready")
        sd_ready = sem("sd_ready")
        var_ready = sem("var_ready")
        lnrow_in = sem("lnrow_in")
        ln_scaled = sem("ln_scaled")
        x_scaled = sem("x_scaled")
        base_ready = sem("base_ready")
        x_ready = sem("x_ready")
        h2_scaled = sem("h2_scaled")
        h2_ready = sem("h2_ready")
        h2_out = sem("h2_out")
        shw_in = sem("shw_in")
        wr_in = sem("wr_in")
        scores_ready = sem("scores_ready")
        mask_ready = sem("mask_ready")
        onehot_ready = sem("onehot_ready")
        onehot_used = sem("onehot_used")
        table_ready = sem("table_ready")
        sh_gated = sem("sh_gated")
        most_ready = sem("most_ready")
        more = [{name: sem(f"more_{name}{l}") for name in (
            "onehot", "dest", "idx", "rows", "turned", "moved", "weights", "up", "silu", "gated", "down", "yrow",
            "sent", "step", "carried")} for l in range(2)]
        idx_ready = [sem(f"idx_ready{i}") for i in range(1)]
        xg_in = [sem(f"xg_in{i}") for i in range(4)]
        y_out = [sem(f"y_out{i}") for i in range(YROWS)]
        s1_ready = sem("s1_ready")
        part_in = [sem(f"part_in{i}") for i in range(3)]
        part_used = sem("part_used")
        logit_ready = sem("logit_ready")
        masked = sem("masked")
        max_ready = sem("max_ready")
        prob_ready = sem("prob_ready")
        logf_ready = sem("logf_ready")
        out_done = sem("out_done")

        MARK = {}
        PART = ([], [])
        PARTS_OF = [len(range(i, 2 * T, 3)) for i in range(3)]

        def until_filled(eng, key):
            b, n = MARK[key]
            eng.wait_ge(filled[b], n)
            return psum[:, b, :]

        def until_drained(eng, key):
            b, n = MARK[key]
            eng.wait_ge(drained[b], n)

        MORE = S // P - 1

        def when_more(eng, l, blocks):
            eng.wait_ge(most_ready, l + 1)
            m = eng.value_load(mosti[0:1, 0:1])
            with eng.If(m > P):
                blocks()
            with eng.Else():
                eng.nop()

        items = []

        def cols_of(w, n0, n=512):
            return w.rearrange("(k p) n -> p k n", p=P)[:, :, n0:n0 + n]

        w_in = ssm_w_in[0]
        for n, blk in enumerate([4, 5, 0, 1, 2, 3, "z0", "z1", "z2", "z3"]):
            if isinstance(blk, int):
                items.append((("xbc", blk), cols_of(w_in, DI + 512 * blk)))
            else:
                items.append((("z", int(blk[1])), cols_of(w_in, 512 * int(blk[1]))))
        for n in range(2):
            for kh in range(2):
                items.append((("w_out", n, kh), cols_of(ssm_w_out[0][D * kh:D * (kh + 1), :], 512 * n)))
        n_items0 = len(items)
        ada_blocks = [(0, b) for b in range(12)] + [("kv", b) for b in range(4)] + [(1, b) for b in range(12)]
        ADA_FIRST, ADA_BESIDE = 4, 4

        def ada_beside(n, half):
            at = ADA_FIRST + ADA_BESIDE * n + 2 * half
            return range(at, at + 2)
        for n in range(4):
            items.append((("kvw", n), cols_of(kv_w, 512 * n)))
        for n in range(2):
            items.append((("wq", n), cols_of(attn_w_q[0], 512 * n)))
        for n in range(2):
            items.append((("wo", n), cols_of(attn_w_o[0], 512 * n)))
        n_items1 = len(items)

        CONSTS = 10
        ROWS = 7 * 16
        SMALL = 9 * 16
        TILES = [slice(P * t, P * t + P) for t in range(T)]
        NQ = T * GROUPS
        NG = E // SLOTS

        def stream_order():
            for key, _ in items:
                if key[0] == "w_out":
                    return
                yield key

        block = ctx.enter_context(nc.Block())

        @block.tensor
        def _(pe):
            uses = [0] * 8
            taken = [0]

            def claim(b):
                if uses[b]:
                    pe.wait_ge(drained[b], uses[b])
                uses[b] += 1
                return psum[:, b, :]

            def fill(ins, b, key):
                ins.then_inc(filled[b], 1)
                MARK[key] = (b, uses[b])

            def take(key):
                i = taken[0]
                assert items[i][0] == key, (items[i][0], key)
                taken[0] += 1
                pe.wait_ge(ring_in[i % RING], 16 * (i // RING + 1))
                return ring[i % RING], ("item", i)

            def done_item(tag, key):
                MARK[tag] = MARK[key]

            def ada(a):
                l, blk = ada_blocks[a]
                b = 4 + a % 2
                pe.wait_ge(ada_summed[a % 2], a // 2 + 1)
                ps = claim(b)
                for j in range(4):
                    mm = pe.matmul(ps[:, j:j + 1], ada_acc[a % 2][:, P * j:P * j + P], ones[:, 0:1], start=True, stop=True)
                fill(mm, b, ("mod", l, blk))

            def turn(name, src, ready):
                for t in range(T):
                    ready(t)
                    for half in range(2):
                        b = 4 * half + t % 2
                        ps = claim(b)
                        for j in range(4):
                            k = 4 * half + j
                            mm = pe.transpose(ps[:, P * j:P * j + P], src[:, t, P * k:P * k + P], ident[:, :])
                        fill(mm, b, (name, t, half))

            def turned(name, t):
                for half in range(2):
                    until_drained(pe, (name, t, half))

            def spread(name, need, banks=(1, 2)):
                pe.wait_ge(diag_ready, need)
                src = diag[name[0]]
                for half in range(2):
                    b = banks[half]
                    ps = claim(b)
                    mm = pe.matmul(ps[:, :], ones[:, :], src[:, 4 * half:4 * half + 4, :].rearrange("p a b -> p (a b)"),
                                   start=True, stop=True)
                    fill(mm, b, (name, half))

            def moe_spreads(l):
                spread(("s2", l), 4 * l + 2)
                spread(("sh2", l), 4 * l + 3, banks=(0, 3))
                spread(("g2", l), 4 * l + 4)

            pe.wait_ge(consts, CONSTS)
            pe.wait_ge(rows_in_sem, ROWS)
            ps = claim(4)
            for r, n in enumerate((120, 120, XT)):
                mm = pe.transpose(ps[:, P * r:P * r + n], rows[0:n, r, :], ident[0:n, 0:n])
            fill(mm, 4, "vecs")
            for a in range(ADA_FIRST):
                ada(a)

            def x_loaded(t):
                if t == 0:
                    pe.wait_ge(x_in, 16 * T)
            turn("hT0", X, x_loaded)
            for t in range(T):
                turned("hT0", t)
            pe.wait_ge(small_in, SMALL)
            ps = claim(6)
            for t in range(T):
                for k in range(KC):
                    mm = pe.matmul(ps[:, HEADS * t:HEADS * (t + 1)], HT[:, k, P * t:P * t + P], wdt[:, k, :],
                                   start=(k == 0), stop=(k == KC - 1))
            fill(mm, 6, "dt")
            at = 0
            nb = 0
            while items[at][0][0] != "w_out":
                kind = items[at][0]
                if kind[0] == "xbc":
                    w, tag = take(kind)
                    for j in range(4):
                        b = (0, 1, 2, 3)[nb % 4]
                        nb += 1
                        ps = claim(b)
                        for k in range(KC):
                            mm = pe.matmul(ps[:, :], w[:, k, P * j:P * j + P], HT[:, k, :],
                                           start=(k == 0), stop=(k == KC - 1))
                        fill(mm, b, ("xbc", 4 * kind[1] + j))
                        if j % 2:
                            for a in ada_beside(at, j // 2):
                                ada(a)
                    done_item(tag, ("xbc", 4 * kind[1] + 3))
                else:
                    w, tag = take(kind)
                    for t in range(T):
                        b = (0, 1, 2, 3)[nb % 4]
                        nb += 1
                        ps = claim(b)
                        for k in range(KC):
                            mm = pe.matmul(ps[:, :], HT[:, k, P * t:P * t + P], w[:, k, :],
                                           start=(k == 0), stop=(k == KC - 1))
                        fill(mm, b, ("z", kind[1], t))
                    done_item(tag, ("z", kind[1], T - 1))
                at += 1

            pe.wait_ge(dA_ready, 1)
            pe.wait_ge(conv_done, CT)

            def tok(t):
                return slice(P * t, P * t + P)

            def scan_a(q):
                ch, g = divmod(q, GROUPS)
                if g == 0:
                    ps = claim(0)
                    for n, m in enumerate((upper, after, ones)):
                        mm = pe.matmul(ps[:, HEADS * n:HEADS * (n + 1)], m[:, :], dA[:, ch, :], start=True, stop=True)
                    fill(mm, 0, ("sums", ch))
                ps = claim(4)
                for j in range(4):
                    mm = pe.transpose(ps[:, P * j:P * j + P], xbcT[:, 4 * g + j, tok(ch)], ident[:, :])
                fill(mm, 4, ("xs", q))
                ps = claim(5)
                pe.transpose(ps[:, 0:P], xbcT[:, XT + g, tok(ch)], ident[:, :])
                mm = pe.matmul(ps[:, P:2 * P], xbcT[:, XT + g, tok(ch)], xbcT[:, XT + GROUPS + g, tok(ch)],
                               start=True, stop=True)
                fill(mm, 5, ("bc", q))
                for half in range(2):
                    pe.wait_ge(stepm_ready, 2 * q + half + 1)
                    ps = claim(1 + half)
                    for j in range(4):
                        mm = pe.matmul(ps[:, P * j:P * j + P], stepm[4 * half + j], upper[:, :], start=True, stop=True)
                    fill(mm, 1 + half, ("seg", q, half))

            def scan_b(q):
                ch, g = divmod(q, GROUPS)
                if ch:
                    until_drained(pe, ("st", q - GROUPS))
                    ps = claim(6)
                    mm = pe.matmul(ps[:, :], xbcT[:, XT + GROUPS + g, tok(ch)], state[:, g, :], start=True, stop=True)
                    fill(mm, 6, ("yoff", q))
                if ch < T - 1:
                    pe.wait_ge(xdte_ready, q + 1)
                    until_drained(pe, ("bc", q))
                    ps = claim(3)
                    mm = pe.matmul(ps[:, :], Btok[q % 2], xdte[q % 2], start=True, stop=True)
                    fill(mm, 3, ("st", q))
                pe.wait_ge(xdt_ready, q + 1)
                ps = claim(7)
                for h in range(GH):
                    if h % 4 == 0:
                        pe.wait_ge(mixm_ready, 2 * q + h // 4 + 1)
                    mm = pe.matmul(ps[:, HD * h:HD * h + HD], mixm[h // 4][:, P * (h % 4):P * (h % 4) + P],
                                   xdt[q % 2][:, HD * h:HD * h + HD], start=True, stop=True)
                fill(mm, 7, ("yd", q))

            def turn_y(ch):
                for g in range(GROUPS):
                    b = (0, 3, 4, 5)[g]
                    pe.wait_ge(yz_ready, GROUPS * ch + g + 1)
                    ps = claim(b)
                    for j in range(4):
                        k = 4 * g + j
                        mm = pe.transpose(ps[:, P * j:P * j + P], zs[:, ch, P * k:P * k + P], ident[:, :])
                    fill(mm, b, ("yT", ch, g))

            NQ = T * GROUPS
            scan_a(0)
            for q in range(NQ):
                if q + 1 < NQ:
                    scan_a(q + 1)
                scan_b(q)
                if q % GROUPS == 0 and q:
                    turn_y(q // GROUPS - 1)
            turn_y(T - 1)

            spread(("g1", 0), 1)
            for n in range(2):
                if n:
                    moe_spreads(0)
                w0, tag0 = take(("w_out", n, 0))
                w1, tag1 = take(("w_out", n, 1))
                for t in range(T):
                    if n == 0:
                        for g in range(GROUPS):
                            until_drained(pe, ("yT", t, g))
                    b = 4 + t
                    ps = claim(b)
                    for k in range(XT):
                        w = (w0, w1)[k // KC]
                        mm = pe.matmul(ps[:, :], xbcT[:, k, tok(t)], w[:, k % KC, :],
                                       start=(k == 0), stop=(k == XT - 1))
                    fill(mm, b, ("mix", 0, n, t))
                done_item(tag0, ("mix", 0, n, T - 1))
                done_item(tag1, ("mix", 0, n, T - 1))

            def experts(l):
                def ready(t):
                    pe.wait_ge(h2_ready, T * l + t + 1)
                turn(("h2T", l), H2, ready)
                for t in range(T):
                    turned(("h2T", l), t)
                pe.wait_ge(wr_in, 16 * l) if l else None
                ps = claim(6)
                for t in range(T):
                    for k in range(KC):
                        mm = pe.matmul(ps[:, E * t:E * t + E], HT[:, k, tok(t)], wr[:, k, :],
                                       start=(k == 0), stop=(k == KC - 1))
                fill(mm, 6, ("router", l))
                if l == 0:
                    done_item("wr0", ("router", 0))
                pe.wait_ge(shw_in, 48 * (l + 1))
                for n in range(2):
                    b = 1 + n
                    ps = claim(b)
                    w = shw[:, n, :].rearrange("p (k f) -> p k f", k=KC)
                    for k in range(KC):
                        mm = pe.matmul(ps[:, :], w[:, k, :], HT[:, k, :], start=(k == 0), stop=(k == KC - 1))
                    fill(mm, b, ("shared_in", l, n))
                pe.wait_ge(sh_gated, l + 1)
                for t in range(T):
                    for n in range(2):
                        b = (0, 3)[n]
                        ps = claim(b)
                        mm = pe.matmul(ps[:, :], aS[0][:, tok(t)], shw[:, 2, 512 * n:512 * n + 512], start=True, stop=True)
                        fill(mm, b, ("shared", l, t, n))
                pe.wait_ge(mask_ready, l + 1)
                ps = claim(7)
                for t in range(T):
                    for u in range(t + 1):
                        mm = pe.matmul(ps[:, E * t:E * t + E], (before_b if u == t else ones_b)[:, :], mask_b[:, u, :],
                                       start=(u == 0), stop=(u == t))
                for u in range(T):
                    mm = pe.matmul(ps[:, E * T:E * T + E], ones_b[:, :], mask_b[:, u, :], start=(u == 0), stop=(u == T - 1))
                fill(mm, 7, ("places", l))

                def build_table(n0):
                    ps = claim(4)
                    for e in range(E):
                        pe.wait_ge(onehot_ready, n0 + e + 1)
                        for t in range(T):
                            mm = pe.matmul(ps[:, 3 * e:3 * e + 3], onehot[e % 2][:, t, :], V[:, t, e, :],
                                           start=(t == 0), stop=(t == T - 1))
                        if e < E - 1:
                            mm.then_inc(onehot_used, 1)
                    fill(mm, 4, ("table", l))
                build_table(E * l)

                base = list(uses)
                ebase = E * l

                def rows_in(g, u):
                    i = SLOTS * g + u
                    pe.wait_ge(xg_in[u % 4], 16 * (2 * g + u // 4 + 1 + ebase // 4))
                    for half in range(2):
                        b = 4 * half
                        first = base[b] if (isinstance(i, int) and i == 0) else None
                        pe.wait_ge(drained[b], base[b] + i)
                        for j in range(4):
                            k = 4 * half + j
                            mm = pe.transpose(psum[:, b, P * j:P * j + P], xg[u % 4][:, P * k:P * k + P], ident[:, :])
                        mm.then_inc(filled[b], 1)

                def up(g, u):
                    i = SLOTS * g + u
                    pe.wait_ge(exp_in[u], 48 * (g + 1 + l * (E // SLOTS)))
                    pe.wait_ge(drained[0], base[0] + i + 1)
                    pe.wait_ge(drained[4], base[4] + i + 1)
                    for n in range(2):
                        b = 1 + 4 * n + u % 2
                        pe.wait_ge(drained[b], base[b] + 4 * g + u // 2)
                        w = exp_w[u][:, n, :].rearrange("p (k f) -> p k f", k=KC)
                        for k in range(KC):
                            mm = pe.matmul(psum[:, b, 0:P], w[:, k, :], xeT[u % 2][:, k, :],
                                           start=(k == 0), stop=(k == KC - 1))
                        mm.then_inc(filled[b], 1)

                def down(g, u):
                    i = SLOTS * g + u
                    pe.wait_ge(drained[5 + u % 2], base[5 + u % 2] + 4 * g + u // 2 + 1)
                    for n in range(2):
                        b = 3 + 4 * n
                        pe.wait_ge(drained[b], base[b] + i)
                        mm = pe.matmul(psum[:, b, :], aT[u % 2], exp_w[u][:, 2, 512 * n:512 * n + 512],
                                       start=True, stop=True)
                        mm.then_inc(filled[b], 1)

                def group(g, first=False, last=False):
                    for u in range(SLOTS):
                        if not (last and u == SLOTS - 1):
                            rows_in(*((g, u + 1) if u + 1 < SLOTS else (g + 1, 0)))
                        up(g, u)
                        if u:
                            down(g, u - 1)
                        elif not first:
                            down(g - 1, SLOTS - 1)
                NG = E // SLOTS
                rows_in(0, 0)
                group(0, first=True)
                with pe.Fori(1, NG - 1) as g:
                    group(g)
                group(NG - 1, last=True)
                down(NG - 1, SLOTS - 1)

                def more_blocks():
                    done = more[l]
                    for b in range(8):
                        n = E if b in (0, 4, 3, 7) else E // 2
                        pe.wait_ge(drained[b], base[b] + n)

                    def unit(i):
                        pe.wait_ge(done["onehot"], i + 1)
                        for t in range(T):
                            mm = pe.matmul(psum[:, 6, 0:3], onehot[0][:, t, :], V1[:, t, 0:3], start=(t == 0), stop=(t == T - 1))
                        mm.then_inc(done["dest"], 1)
                        pe.wait_ge(done["rows"], 16 * i + 16)
                        for k in range(KC):
                            mm = pe.transpose(psum[:, k // 4, P * (k % 4):P * (k % 4) + P], xg[0][:, P * k:P * k + P], ident[:, :])
                        mm.then_inc(done["turned"], 1)
                        pe.wait_ge(done["moved"], 2 * i + 2)
                        pe.wait_ge(done["weights"], 48 * i + 48)
                        for n in range(2):
                            w = exp_w[0][:, n, :].rearrange("p (k f) -> p k f", k=KC)
                            for k in range(KC):
                                mm = pe.matmul(psum[:, 2 + n, 0:P], w[:, k, :], xeT[0][:, k, :],
                                               start=(k == 0), stop=(k == KC - 1))
                        mm.then_inc(done["up"], 1)
                        pe.wait_ge(done["gated"], i + 1)
                        for n in range(2):
                            mm = pe.matmul(psum[:, 4 + n, :], aT[0], exp_w[0][:, 2, 512 * n:512 * n + 512], start=True, stop=True)
                        mm.then_inc(done["down"], 1)
                    for b in range(MORE):
                        with pe.Fori(0, E) as e:
                            unit(E * b + e)
                    pe.wait_ge(done["yrow"], 2 * MORE * E)
                when_more(pe, l, more_blocks)
                MARK[("loop", l)] = list(base)
                for b in (0, 4, 3, 7):
                    uses[b] += E
                for b in (1, 2, 5, 6):
                    uses[b] += E // 2

            if phases >= 2:
                experts(0)

            def attention():
                def ready(t):
                    pe.wait_ge(x_ready, T + t + 1)
                turn("uT", X, ready)
                for t in range(T):
                    turned("uT", t)
                ps = claim(6)
                for t in range(T):
                    for k in range(KC):
                        mm = pe.matmul(ps[:, AH * t:AH * (t + 1)], HT[:, k, tok(t)], wf[:, k, :],
                                       start=(k == 0), stop=(k == KC - 1))
                fill(mm, 6, "forget")
                nb = 0
                for n in range(2):
                    w, tag = take(("kvw", n))
                    for j in range(4):
                        b = (0, 1, 2, 3)[nb % 4]
                        nb += 1
                        ps = claim(b)
                        for k in range(KC):
                            mm = pe.matmul(ps[:, :], w[:, k, P * j:P * j + P], HT[:, k, :],
                                           start=(k == 0), stop=(k == KC - 1))
                        fill(mm, b, ("kT", 4 * n + j))
                    done_item(tag, ("kT", 4 * n + 3))
                pe.wait_ge(logf_ready, 1)
                ps = claim(7)
                lf = logf
                for t in range(T):
                    for u in range(t + 1):
                        mm = pe.matmul(ps[:, AH * t:AH * (t + 1)], (upper if u == t else ones)[:, :], lf[:, u, :],
                                       start=(u == 0), stop=(u == t))
                fill(mm, 7, "cumf")
                for n in range(2):
                    w, tag = take(("kvw", 2 + n))
                    for t in range(T):
                        b = (0, 1, 2, 3)[nb % 4]
                        nb += 1
                        ps = claim(b)
                        for k in range(KC):
                            mm = pe.matmul(ps[:, :], HT[:, k, tok(t)], w[:, k, :], start=(k == 0), stop=(k == KC - 1))
                        fill(mm, b, ("v", n, t))
                    done_item(tag, ("v", n, T - 1))
                until_drained(pe, "cumf")
                ps = claim(7)
                mm = pe.transpose(ps[0:T * AH, 0:P], cumf[:, :, :].rearrange("p a b -> p (a b)"), ident[:, :])
                fill(mm, 7, "cumfT")
                turn("qhT", X, lambda t: None)
                for t in range(T):
                    turned("qhT", t)
                for n in range(2):
                    w, tag = take(("wq", n))
                    for j in range(4):
                        b = (0, 1, 2, 3)[nb % 4]
                        nb += 1
                        ps = claim(b)
                        for k in range(KC):
                            mm = pe.matmul(ps[:, :], w[:, k, P * j:P * j + P], HT[:, k, :],
                                           start=(k == 0), stop=(k == KC - 1))
                        fill(mm, b, ("qT", 4 * n + j))
                    done_item(tag, ("qT", 4 * n + 3))
                until_drained(pe, "cumfT")
                for j in range(KC):
                    until_drained(pe, ("qT", j))
                    until_drained(pe, ("kT", j))
                for n in range(2):
                    for t in range(T):
                        until_drained(pe, ("v", n, t))

                def scores_of(n):
                    h, i = divmod(n, T)
                    if i == 0:
                        ps = claim(h % 2)
                        for t in range(T):
                            r = AH * t + h
                            mm = pe.matmul(ps[:, tok(t)], ident[0:T * AH, r:r + 1].to_broadcast([T * AH, P]),
                                           cumfT[:, :], start=True, stop=True)
                        fill(mm, h % 2, ("ncf", h))
                    ps = claim(2 + n % 2)
                    lo = HD * (h % 2)
                    nk = P * (i + 1)
                    mm = pe.matmul(ps[:, 0:nk], qT[lo:lo + HD, h // 2, tok(i)], kT[lo:lo + HD, h // 2, 0:nk],
                                   start=True, stop=True)
                    fill(mm, 2 + n % 2, ("qk", n))

                def turn_probs(n):
                    h, i = divmod(n, T)
                    pe.wait_ge(prob_ready, n + 1)
                    ps = claim(4 + n % 2)
                    for j in range(i + 1):
                        mm = pe.transpose(ps[:, tok(j)], prob[n % 3][:, tok(j)], ident[:, :])
                    fill(mm, 4 + n % 2, ("pT", n))

                def weigh(n):
                    h, i = divmod(n, T)
                    until_drained(pe, ("pT", n))
                    b = 6 + h % 2
                    if i == 0:
                        claim(b)
                    ps = psum[:, b, :]
                    for j in range(i + 1):
                        mm = pe.matmul(ps[:, HD * i:HD * i + HD], probT[n % 2][:, j, :], vtok[:, j, HD * h:HD * h + HD],
                                       start=(j == 0), stop=(j == i))
                    if i == T - 1:
                        fill(mm, b, ("o", h))

                NU = AH * T
                scores_of(0)
                scores_of(1)
                for n in range(NU):
                    if n + 2 < NU:
                        scores_of(n + 2)
                    turn_probs(n)
                    if n:
                        weigh(n - 1)
                weigh(NU - 1)

                def o_ready(t):
                    if t == 0:
                        until_drained(pe, ("o", AH - 1))
                        until_drained(pe, ("o", AH - 2))
                spread(("g1", 1), 5)
                turn("oT", otok, o_ready)
                for n in range(2):
                    if n:
                        moe_spreads(1)
                    w, tag = take(("wo", n))
                    for t in range(T):
                        turned("oT", t)
                        b = 4 + t
                        ps = claim(b)
                        for k in range(KC):
                            mm = pe.matmul(ps[:, :], HT[:, k, tok(t)], w[:, k, :], start=(k == 0), stop=(k == KC - 1))
                        fill(mm, b, ("mix", 1, n, t))
                    done_item(tag, ("mix", 1, n, T - 1))

            if phases >= 3:
                attention()
            if phases >= 4:
                experts(1)


        @block.scalar
        def _(act):
            def move(key, dst, func=ACT.Copy, **kw):
                ps = until_filled(act, key)
                act.activation(dst, ps, func, **kw).then_inc(drained[MARK[key][0]], 1)

            def move_turned(name, half, dst):
                for t in range(T):
                    ps = until_filled(act, (name, t, half))
                    act.activation(dst[:, 4 * half:4 * half + 4, TILES[t]], ps.rearrange("p (a b) -> p a b", a=4),
                                   ACT.Copy).then_inc(drained[MARK[(name, t, half)][0]], 1)

            def move_modulated(name, half, dst, scale, shift):
                for t in range(T):
                    ps = until_filled(act, (name, t, half))
                    for j in range(4):
                        k = 4 * half + j
                        ins = act.activation(dst[:, k, TILES[t]], ps[:, P * j:P * j + P], ACT.Identity,
                                             scale=mod[:, scale + k:scale + k + 1], bias=mod[:, shift + k:shift + k + 1])
                    ins.then_inc(drained[MARK[(name, t, half)][0]], 1)

            def until_mod(l, v):
                until_drained(act, ("mod", l, (8 * v) // 4))
                until_drained(act, ("mod", l, (8 * v) // 4 + 1))

            def move_spread(name, dst):
                for half in range(2):
                    move((name, half), dst[:, 512 * half:512 * half + 512])

            soft = [0]

            def softplus_act(x, n, x_done):
                x_done()
                act.activation(sp[0][:, 0:n], x, ACT.Abs).then_inc(soft_act, 1)
                soft[0] += 1
                act.wait_ge(soft_act, soft[0])
                act.activation(sp[0][:, 0:n], sp[0][:, 0:n], ACT.Exp, scale=-1.0).then_inc(soft_act, 1)
                soft[0] += 1

            def softplus_ln(n, m):
                act.wait_ge(soft_dve, m)
                act.activation(sp[2][:, 0:n], sp[1][:, 0:n], ACT.Ln).then_inc(soft_act, 1)
                soft[0] += 1

            def ada_scale(a):
                w = ada_pool[a // 2 % 2]
                act.wait_ge(ada_pool_in[a // 2 % 2], 16 * (a // 4 + 1))
                for k in range(KC):
                    ins = act.activation(w[:, k, :], w[:, k, :], ACT.Copy, scale=condT[:, k:k + 1])
                ins.then_inc(ada_scaled, 1)

            until_drained(act, "vecs")
            act.activation(condT[:, :], c_col, ACT.Silu).then_inc(cond_ready, 1)
            act.wait_ge(cond_ready, 1)
            for a in range(1, ADA_FIRST, 2):
                ada_scale(a)
            for v in (SHIFT1, SCALE1):
                until_mod(0, v)
            move_modulated("hT0", 0, HT, MODC[(0, SCALE1)], MODC[(0, SHIFT1)])
            act.wait_ge(small_in, SMALL)
            act.activation(negA[:, :], alog_bc, ACT.Exp).then_inc(soft_act, 1)
            soft[0] += 1
            softplus_act(dtx[:, :, :].rearrange("p a b -> p (a b)"), P, lambda: until_drained(act, "dt"))
            softplus_ln(P, 1)
            waiting = []

            def finish_conv():
                if waiting:
                    j, n = waiting.pop()
                    until_drained(act, ("xbc", j))
                    act.activation(xbcT[:, j, :], conv_acc[n % 2], ACT.Silu).then_inc(conv_done, 1)
            n = 0
            for key in stream_order():
                if key[0] == "xbc":
                    for j in range(4 * key[1], 4 * key[1] + 4):
                        if n % 2 == 0:
                            ada_scale(ada_beside(n // 4, n % 4 // 2)[1])
                        ps = until_filled(act, ("xbc", j))
                        if n >= 2:
                            act.wait_ge(conv_done, n - 1)
                        act.activation(conv_acc[n % 2], ps, ACT.Identity, scale=convw[:, CONV - 1, j:j + 1],
                                       bias=convb[:, j:j + 1]).then_inc(acc_ready, 1)
                        finish_conv()
                        waiting.append((j, n))
                        n += 1
                elif key[0] == "z":
                    finish_conv()
                    if key[1] == 0:
                        for i in range(2):
                            act.wait_ge(ada_summed[i], len(ada_blocks) // 2)
                    for t in range(T):
                        move(("z", key[1], t), zs[:, t, 512 * key[1]:512 * key[1] + 512], ACT.Silu)

            def scan_exps(q):
                ch, g = divmod(q, GROUPS)
                if g == 0:
                    if ch >= 2:
                        act.wait_ge(yz_ready, GROUPS * (ch - 1))
                    ps = until_filled(act, ("sums", ch))
                    act.activation(exps[ch % 2][:, :], ps[:, 0:96], ACT.Exp).then_inc(drained[0], 1)
                for half in range(2):
                    if q:
                        act.wait_ge(mixm_ready, 2 * (q - 1) + half + 1)
                    ps = until_filled(act, ("seg", q, half))
                    act.activation(decay[half], ps, ACT.Exp).then_inc(drained[1 + half], 1)

            def square(q):
                ch, g = divmod(q, GROUPS)
                act.wait_ge(yz_ready, q + 1)
                if q:
                    act.wait_ge(squared, q)
                act.activation(view(139, GW), zs[:, ch, GW * g:GW * g + GW], ACT.Square,
                               accum_out=ssq[:, ch, g:g + 1]).then_inc(squared, 1)

            def move_y(ch):
                for g in range(2):
                    ps = until_filled(act, ("yT", ch, g))
                    for j in range(4):
                        k = 4 * g + j
                        ins = act.activation(xbcT[:, k, TILES[ch]], ps[:, P * j:P * j + P], ACT.Copy,
                                             scale=normw[:, k:k + 1])
                    ins.then_inc(drained[MARK[("yT", ch, g)][0]], 1)
            scan_exps(0)
            for q in range(NQ):
                if q + 1 < NQ:
                    scan_exps(q + 1)
                if q:
                    square(q - 1)
                if q % GROUPS == 0 and q:
                    move_y(q // GROUPS - 1)
            square(NQ - 1)
            move_y(T - 1)

            act.wait_ge(var_ready, 1)
            act.activation(sd[:, :], sd[:, :], ACT.Sqrt).then_inc(sd_ready, 1)
            act.wait_ge(squared, NQ)
            move_spread(("g1", 0), g1bc)

            def roots(k):
                for t in range(T):
                    act.wait_ge(var_ready, 2 + T * k + t)
                    act.activation(sd[:, t:t + 1], sd[:, t:t + 1], ACT.Sqrt).then_inc(sd_ready, 1)

            def moe_spreads(l):
                move_spread(("s2", l), s2bc)
                move_spread(("sh2", l), sh2bc)
                move_spread(("g2", l), g2bc)
            moe_spreads(0)
            roots(0)

            def experts(l):
                for t in range(T):
                    act.wait_ge(h2_scaled, T * l + t + 1)
                    act.activation(X[:, t, :], X[:, t, :], ACT.Copy, scale=ALPHA).then_inc(x_scaled, 1)
                move_turned(("h2T", l), 0, HT)
                ps = until_filled(act, ("router", l))
                act.activation(scores[:, :, :].rearrange("p a b -> p (a b)"), ps[:, 0:T * E], ACT.Sigmoid).then_inc(drained[6], 1)
                move(("shared_in", l, 0), aS[0], ACT.Silu)
                move(("shared_in", l, 1), aS[1])
                for t in range(T):
                    for n in range(2):
                        move(("shared", l, t, n), SH[:, t, 512 * n:512 * n + 512])
                base = MARK[("loop", l)]

                def rows_in(g, u):
                    for half in range(2):
                        b = 4 * half
                        act.wait_ge(filled[b], base[b] + SLOTS * g + u + 1)
                        act.activation(xeT[u % 2][:, 4 * half:4 * half + 4, :],
                                       psum[:, b, :].rearrange("p (a b) -> p a b", a=4), ACT.Copy).then_inc(drained[b], 1)

                def silu(g, u):
                    b = 1 + u % 2
                    act.wait_ge(filled[b], base[b] + 4 * g + u // 2 + 1)
                    act.activation(s1[u % 2], psum[:, b, 0:P], ACT.Silu).then_inc(drained[b], 1)

                def group(g, last=False):
                    for u in range(SLOTS):
                        if not (last and u == SLOTS - 1):
                            rows_in(*((g, u + 1) if u + 1 < SLOTS else (g + 1, 0)))
                        silu(g, u)
                rows_in(0, 0)
                group(0)
                with act.Fori(1, NG - 1) as g:
                    group(g)
                group(NG - 1, last=True)

                def more_blocks():
                    done = more[l]

                    def unit(i):
                        act.wait_ge(done["turned"], i + 1)
                        for half in range(2):
                            act.activation(xeT[0][:, 4 * half:4 * half + 4, :],
                                           psum[:, half, :].rearrange("p (a b) -> p a b", a=4),
                                           ACT.Copy).then_inc(done["moved"], 1)
                        act.wait_ge(done["up"], i + 1)
                        act.activation(s1[0], psum[:, 2, 0:P], ACT.Silu).then_inc(done["silu"], 1)
                    for b in range(MORE):
                        with act.Fori(0, E) as e:
                            unit(E * b + e)
                when_more(act, l, more_blocks)
                roots(2 * l + 1)

            def attention():
                for v in (0, 1):
                    until_mod("kv", v)
                move_modulated("uT", 0, HT, MODC[("kv", 1)], MODC[("kv", 0)])
                softplus_act(dts[:, 0:2, :].rearrange("p a b -> p (a b)"), T * AH, lambda: act.wait_ge(soft_dve, 9))
                for j in range(0, KC, 2):
                    move(("kT", j), kT[:, j, :])
                    if j == 0:
                        softplus_ln(T * AH, 10)
                for n in range(2):
                    for t in range(0, T, 2):
                        move(("v", n, t), vtok[:, t, 512 * n:512 * n + 512])
                for v in (SHIFT1, SCALE1):
                    until_mod(1, v)
                move_modulated("qhT", 0, HT, MODC[(1, SCALE1)], MODC[(1, SHIFT1)])
                for j in range(0, KC, 2):
                    move(("qT", j), qT[:, j, :])
                until_drained(act, "cumf")

                def scaled(n):
                    h, i = divmod(n, T)
                    if n >= 3:
                        act.wait_ge(max_ready, n - 2)
                    ps = until_filled(act, ("qk", n))
                    act.activation(logit[n % 3][:, 0:P * (i + 1)], ps[:, 0:P * (i + 1)], ACT.Identity, scale=ASCALE,
                                   bias=cumf[:, i, h:h + 1]).then_inc(drained[MARK[("qk", n)][0]], 1)

                def soften(n):
                    h, i = divmod(n, T)
                    act.wait_ge(max_ready, n + 1)
                    if n >= 3:
                        until_filled(act, ("pT", n - 3))
                    if i == 0 and h >= 2:
                        until_drained(act, ("o", h - 2))
                    nk = P * (i + 1)
                    act.activation(prob[n % 3][:, 0:nk], shifted[n % 3][:, 0:nk], ACT.Exp, bias=mx[:, 4 + n % 4:5 + n % 4],
                                   accum_out=rsum[:, h % 2, i:i + 1]).then_inc(prob_ready, 1)
                NU = AH * T
                scaled(0)
                scaled(1)
                for n in range(NU):
                    if n + 2 < NU:
                        scaled(n + 2)
                    soften(n)
                move_spread(("g1", 1), g1bc)
                move_turned("oT", 0, HT)
                moe_spreads(1)
                roots(2)

            if phases >= 2:
                experts(0)
            if phases >= 3:
                attention()
            if phases >= 4:
                experts(1)

        @block.vector
        def _(dve):
            steps = [0]

            def step(ins):
                ins.then_inc(dve_step, 1)
                steps[0] += 1

            def settle():
                dve.wait_ge(dve_step, steps[0])

            def move(key, dst):
                ps = until_filled(dve, key)
                dve.tensor_copy(dst, ps).then_inc(drained[MARK[key][0]], 1)

            def move_turned(name, half, dst):
                for t in range(T):
                    ps = until_filled(dve, (name, t, half))
                    dve.tensor_copy(dst[:, 4 * half:4 * half + 4, TILES[t]],
                                    ps.rearrange("p (a b) -> p a b", a=4)).then_inc(drained[MARK[(name, t, half)][0]], 1)

            def move_modulated(name, half, dst, scale, shift):
                for t in range(T):
                    ps = until_filled(dve, (name, t, half))
                    for j in range(4):
                        k = 4 * half + j
                        ins = dve.tensor_scalar(dst[:, k, TILES[t]], ps[:, P * j:P * j + P],
                                                mod[:, scale + k:scale + k + 1], mod[:, shift + k:shift + k + 1],
                                                ALU.mult, ALU.add)
                    ins.then_inc(drained[MARK[(name, t, half)][0]], 1)

            def ada_sum(a):
                if a >= 2:
                    until_filled(dve, ("mod",) + ada_blocks[a - 2])
                dve.wait_ge(ada_dve_in[0], 16 * (a // 2 + 1))
                step(dve.tensor_scalar(ada_acc[0], ada_dve[:, 0, :], condT[:, 0:1], None, ALU.mult))
                for k in range(1, KC):
                    if k == KC // 2:
                        dve.wait_ge(ada_half, a // 2 + 1)
                        dve.wait_ge(ada_dve_in[1], 16 * (a // 2 + 1))
                    else:
                        settle()
                    ins = dve.scalar_tensor_tensor(ada_acc[0], ada_dve[:, k, :], condT[:, k:k + 1], ada_acc[0],
                                                   ALU.mult, ALU.add)
                    if k == KC // 2 - 1:
                        ins.then_inc(ada_half, 1)
                    elif k < KC - 1:
                        step(ins)
                ins.then_inc(ada_summed[0], 1)

            def ada(l, blk):
                ps = until_filled(dve, ("mod", l, blk))
                at = {0: 0, 1: 48, "kv": 96}[l] + 4 * blk
                add1 = 1.0 if (blk // 2 in (1, 2, 4, 5)) else 0.0
                dve.scalar_tensor_tensor(mod[:, at:at + 4], ps[:, 0:4], add1, modb[:, at:at + 4], ALU.add,
                                         ALU.add).then_inc(drained[MARK[("mod", l, blk)][0]], 1)

            def until_mod(l, v):
                until_drained(dve, ("mod", l, 2 * v))
                until_drained(dve, ("mod", l, 2 * v + 1))

            def diagonals(l):
                for name, v in (("g1", GATE1), ("s2", SCALE2), ("sh2", SHIFT2), ("g2", GATE2)):
                    until_mod(l, v)
                    for k in range(KC):
                        col = MODC[(l, v)] + k
                        ins = dve.tensor_scalar(diag[name][:, k, :], ident[:, :], mod[:, col:col + 1], None, ALU.mult)
                    ins.then_inc(diag_ready, 1)

            def soft(ins):
                ins.then_inc(soft_dve, 1)
                softs[0] += 1

            softs = [0]

            def softplus(x, out, n, act0):
                t_, u_, l_, m_ = (sp[i][:, 0:n] for i in range(4))
                dve.wait_ge(soft_act, act0 + 2)
                soft(dve.tensor_scalar(u_, t_, 1.0, None, ALU.add))
                dve.wait_ge(soft_act, act0 + 3)

                def then(ins):
                    soft(ins)
                    dve.wait_ge(soft_dve, softs[0])
                then(dve.tensor_scalar(u_, u_, -1.0, None, ALU.add))
                then(dve.tensor_scalar(m_, u_, 0.0, None, ALU.is_equal))
                then(dve.tensor_tensor(u_, u_, m_, ALU.add))
                then(dve.tensor_tensor(l_, l_, m_, ALU.add))
                then(dve.reciprocal(u_, u_))
                then(dve.tensor_tensor(l_, l_, u_, ALU.mult))
                then(dve.tensor_tensor(l_, l_, t_, ALU.mult))
                step(dve.scalar_tensor_tensor(out, x, 0.0, l_, ALU.max, ALU.add))
                settle()

            ps = until_filled(dve, "vecs")
            for r, n in enumerate((120, 120, XT)):
                ins = dve.tensor_copy(cols[:, r, 0:n], ps[:, P * r:P * r + n])
            ins.then_inc(drained[4], 1)
            until_drained(dve, "vecs")
            dve.wait_ge(cond_ready, 1)
            for a in range(0, ADA_FIRST, 2):
                ada_sum(a)
                for i in (a, a + 1):
                    ada(*ada_blocks[i])
            until_mod(0, SHIFT1)
            until_mod(0, SCALE1)
            move_modulated("hT0", 1, HT, MODC[(0, SCALE1)], MODC[(0, SHIFT1)])
            dve.wait_ge(small_in, SMALL)
            ps = until_filled(dve, "dt")
            dve.tensor_tensor(dtx[:, :, :], ps[:, 0:P].rearrange("p (a b) -> p a b", a=T),
                              dtb_bc.unsqueeze(1).to_broadcast([P, T, HEADS]), ALU.add).then_inc(drained[6], 1)
            until_drained(dve, "dt")
            softplus(dtx[:, :, :].rearrange("p a b -> p (a b)"), dts[:, :, :].rearrange("p a b -> p (a b)"), P, 1)
            step(dve.tensor_scalar(negA[:, :], negA[:, :], -1.0, None, ALU.mult))
            settle()
            dve.tensor_tensor(dA[:, :, :], dts[:, :, :], negA[:, :].unsqueeze(1).to_broadcast([P, T, HEADS]),
                              ALU.mult).then_inc(dA_ready, 1)

            n = 0
            for key in stream_order():
                if key[0] == "xbc":
                    for j in range(4 * key[1], 4 * key[1] + 4):
                        if n % 2 == 0:
                            ada_sum(ada_beside(n // 4, n % 4 // 2)[0])
                        ps = until_filled(dve, ("xbc", j))
                        dve.wait_ge(acc_ready, n + 1)
                        for s in range(1, CONV):
                            ins = dve.scalar_tensor_tensor(conv_acc[n % 2][:, s:S], ps[:, 0:S - s],
                                                           convw[:, CONV - 1 - s, j:j + 1], conv_acc[n % 2][:, s:S],
                                                           ALU.mult, ALU.add)
                            if s < CONV - 1:
                                step(ins)
                                settle()
                        ins.then_inc(drained[MARK[("xbc", j)][0]], 1)
                        if n % 2:
                            for a in ada_beside(n // 4, n % 4 // 2):
                                ada(*ada_blocks[a])
                        n += 1

            dve.wait_ge(conv_done, CT)

            def heads(v):
                return v.rearrange("p (h d) -> p h d", h=GH)

            def bch(v):
                return v.unsqueeze(2).to_broadcast([P, GH, HD])

            def scan_a(q):
                ch, g = divmod(q, GROUPS)
                hs = slice(GH * g, GH * g + GH)
                ps = until_filled(dve, ("xs", q))
                if q >= 2:
                    dve.wait_ge(xdte_ready, min(q - 1, NQ - GROUPS))
                    until_drained(dve, ("yd", q - 2))
                dve.tensor_tensor(heads(xdt[q % 2]), heads(ps), bch(dts[:, ch, hs]), ALU.mult).then_inc(xdt_ready, 1)
                dve.tensor_tensor(heads(xsD[q % 2]), heads(ps), bch(dsk_bc[:, hs]), ALU.mult).then_inc(drained[4], 1)
                ps = until_filled(dve, ("bc", q))
                dve.tensor_copy(Btok[q % 2], ps[:, 0:P])
                dve.tensor_tensor(CBm[q % 2], ps[:, P:2 * P], upper[:, :], ALU.mult).then_inc(drained[5], 1)

            def scan_g(q):
                until_drained(dve, ("bc", q))
                for half in range(2):
                    until_drained(dve, ("seg", q, half))
                    if q:
                        until_filled(dve, ("yd", q - 1))
                    dve.tensor_tensor(mixm[half].rearrange("p (h l) -> p h l", h=4),
                                      decay[half].rearrange("p (h l) -> p h l", h=4),
                                      CBm[q % 2].unsqueeze(1).to_broadcast([P, 4, P]), ALU.mult).then_inc(mixm_ready, 1)

            def scan_b(q):
                ch, g = divmod(q, GROUPS)
                hs = slice(GH * g, GH * g + GH)
                if q >= 2:
                    dve.wait_ge(yz_ready, q - 1)
                if ch:
                    ps = until_filled(dve, ("yoff", q))
                    until_drained(dve, ("sums", ch))
                    dve.tensor_tensor(heads(yoff[q % 2]), heads(ps), bch(exps[ch % 2][:, hs]), ALU.mult).then_inc(drained[6], 1)
                if ch < T - 1:
                    ps = until_filled(dve, ("st", q))
                    if ch:
                        dve.wait_ge(state_scaled, q - GROUPS + 1)
                        dve.tensor_tensor(state[:, g, :], state[:, g, :], ps, ALU.add).then_inc(drained[3], 1)
                    else:
                        dve.tensor_copy(state[:, g, :], ps).then_inc(drained[3], 1)
                ps = until_filled(dve, ("yd", q))
                until_drained(dve, ("xs", q))
                dve.tensor_tensor(yg[q % 2], ps, xsD[q % 2], ALU.add).then_inc(drained[7], 1)

            def move_y(ch):
                for g in range(2, 4):
                    ps = until_filled(dve, ("yT", ch, g))
                    for j in range(4):
                        k = 4 * g + j
                        ins = dve.tensor_scalar(xbcT[:, k, TILES[ch]], ps[:, P * j:P * j + P], normw[:, k:k + 1], None,
                                                ALU.mult)
                    ins.then_inc(drained[MARK[("yT", ch, g)][0]], 1)
            scan_a(0)
            for q in range(NQ):
                scan_g(q)
                if q + 1 < NQ:
                    scan_a(q + 1)
                scan_b(q)
                if q % GROUPS == 0 and q:
                    move_y(q // GROUPS - 1)
            dve.wait_ge(squared, NQ)
            step(dve.tensor_reduce(ssum[:, :], ssq[:, :, :], AX, ALU.add))
            settle()
            dve.tensor_scalar(sd[:, :], ssum[:, :], 1.0 / DI, EPS, ALU.mult, ALU.add).then_inc(var_ready, 1)
            diagonals(0)
            move_y(T - 1)
            dve.wait_ge(sd_ready, 1)
            step(dve.reciprocal(rsy[:, :], sd[:, :]))
            settle()

            def statistics(k, t, R):
                settle()
                for n in range(2):
                    ins = dve.bn_stats(bn[:, t, n, :], R[:, t, 512 * n:512 * n + 512])
                step(ins)
                settle()
                step(dve.bn_aggr(mv[:, t, :], bn[:, t, :, :]))
                settle()
                dve.tensor_scalar(sd[:, t:t + 1], mv[:, t, 1:2], EPS, None, ALU.add).then_inc(var_ready, 1)

            def normalise(k, t, R, lnrow):
                dve.wait_ge(sd_ready, 2 + T * k + t)
                step(dve.reciprocal(rstd[:, t:t + 1], sd[:, t:t + 1]))
                settle()
                step(dve.tensor_scalar(X[:, t, :], R[:, t, :], mv[:, t, 0:1], rstd[:, t:t + 1], ALU.subtract, ALU.mult))
                settle()
                if t == 0:
                    dve.wait_ge(lnrow_in, 32 * (k + 1))
                dve.tensor_tensor(X[:, t, :], X[:, t, :], lnrow[0], ALU.mult).then_inc(ln_scaled, 1)

            def mixed(l, R):
                for half in range(2):
                    until_drained(dve, ((("g1", l), half)))
                k = 2 * l
                for n in range(2):
                    for t in range(T):
                        r = R[:, t, 512 * n:512 * n + 512]
                        ps = until_filled(dve, ("mix", l, n, t))
                        gb = g1bc[:, 512 * n:512 * n + 512]
                        if l == 0:
                            ins = dve.scalar_tensor_tensor(r, ps, rsy[:, t:t + 1], gb, ALU.mult, ALU.mult)
                        else:
                            ins = dve.tensor_tensor(r, ps, gb, ALU.mult)
                        ins.then_inc(drained[MARK[("mix", l, n, t)][0]], 1)
                        until_drained(dve, ("mix", l, n, t))
                        step(dve.scalar_tensor_tensor(r, X[:, t, 512 * n:512 * n + 512], ALPHA, r, ALU.mult, ALU.add))
                        if n:
                            statistics(k, t, R)
                            if t:
                                normalise(k, t - 1, R, lnrow_mix)
                normalise(k, T - 1, R, lnrow_mix)
            mixed(0, Rmix[0])

            def experts(l):
                for half in range(2):
                    until_drained(dve, (("s2", l), half))
                for t in range(T):
                    dve.wait_ge(x_ready, T * 2 * l + t + 1)
                    dve.tensor_tensor(H2[:, t, :], X[:, t, :], s2bc, ALU.mult).then_inc(h2_scaled, 1)
                move_turned(("h2T", l), 1, HT)

                until_drained(dve, ("router", l))
                step(dve.tensor_tensor(sel[:, :, :], scores[:, :, :], rb_bc[l].unsqueeze(1).to_broadcast([P, T, E]), ALU.add))
                settle()
                for t in range(T):
                    for g in range(EG):
                        ins = dve.max(top8[:, EG * t + g, :], sel[:, t, EPG * g:EPG * g + EPG])
                step(ins)
                settle()
                step(dve.tensor_tensor(gsc[:, :, :].rearrange("p a b -> p (a b)"), top8[:, :, 0], top8[:, :, 1], ALU.add))
                settle()
                for t in range(T):
                    other = gsc[:, t, :].unsqueeze(1).to_broadcast([P, EG, EG])
                    own = gsc[:, t, :].unsqueeze(2).to_broadcast([P, EG, EG])
                    dve.tensor_tensor(gcmp[0][:, t, :, :], other, own, ALU.is_gt)
                    step(dve.tensor_tensor(gcmp[1][:, t, :, :], other, own, ALU.is_equal))
                    settle()
                    step(dve.tensor_tensor(gcmp[1][:, t, :, :], gcmp[1][:, t, :, :], low8[:, :, :], ALU.mult))
                    settle()
                    step(dve.tensor_tensor(gcmp[0][:, t, :, :], gcmp[0][:, t, :, :], gcmp[1][:, t, :, :], ALU.add))
                settle()
                step(dve.tensor_reduce(grank[:, :, :].rearrange("p a b -> p (a b)"),
                                       gcmp[0][:, :, :, :].rearrange("p a b c -> p (a b) c"), AX, ALU.add))
                settle()
                step(dve.tensor_scalar(grank[:, :, :], grank[:, :, :], float(TOPG), -BIG, ALU.is_ge, ALU.mult))
                settle()
                step(dve.tensor_tensor(sel[:, :, :].rearrange("p t (g e) -> p (t g) e", g=EG),
                                       sel[:, :, :].rearrange("p t (g e) -> p (t g) e", g=EG),
                                       grank[:, :, :].rearrange("p a b -> p (a b)").unsqueeze(2).to_broadcast([P, T * EG, EPG]),
                                       ALU.add))
                settle()
                for t in range(T):
                    ins = dve.max(top8[:, t, :], sel[:, t, :])
                step(ins)
                settle()
                for t in range(T):
                    ins = dve.match_replace(pos[:, t, :], top8[:, t, :], sel[:, t, :], -3.0e38)
                step(ins)
                settle()
                step(dve.tensor_tensor(mask[:, :, :], pos[:, :, :], sel[:, :, :], ALU.not_equal))
                settle()
                for t in range(T):
                    ins = dve.tensor_tensor_scan(krank[:, t, :], mask[:, t, :], mask[:, t, :], 0.0, ALU.add, ALU.bypass)
                step(dve.tensor_copy(mask_b[:, :, :], mask[:, :, :]))
                settle()
                step(dve.tensor_tensor(krank[:, :, :], krank[:, :, :], mask[:, :, :], ALU.subtract))
                settle()
                dve.tensor_copy(V[:, :, :, 2], krank[:, :, :]).then_inc(mask_ready, 1)
                ps = until_filled(dve, ("places", l))
                step(dve.scalar_tensor_tensor(pos[:, :, :].rearrange("p a b -> p (a b)"),
                                              mask[:, :, :].rearrange("p a b -> p (a b)"), -4096.0, ps[:, 0:T * E],
                                              ALU.mult, ALU.add))
                dve.tensor_reduce(most[:, 0:1], ps[:, E * T:E * T + E], AX, ALU.max).then_inc(drained[7], 1)
                until_drained(dve, ("places", l))
                dve.tensor_copy(mosti[:, :], most[:, :]).then_inc(most_ready, 1)
                settle()
                step(dve.tensor_scalar(pos[:, :, :], pos[:, :, :], 4096.0, None, ALU.add))
                settle()

                def build_table(n0):
                    for e in range(E):
                        if e >= 2:
                            dve.wait_ge(onehot_used, (E - 1) * (n0 // E) + e - 1)
                        for t in range(T):
                            ins = dve.tensor_scalar(onehot[e % 2][:, t, :], slot_no[:, :], pos[:, t, e:e + 1], None,
                                                    ALU.is_equal)
                        ins.then_inc(onehot_ready, 1)
                    ps = until_filled(dve, ("table", l))
                    dve.tensor_reduce(destf[:, :], ps[:, 0:3 * E].rearrange("p (e c) -> p e c", c=3), AX,
                                      ALU.add).then_inc(drained[4], 1)
                    until_drained(dve, ("table", l))
                    step(dve.tensor_scalar(table[:, :, 0], destf[:, :], float(NOWHERE), None, ALU.add))
                    settle()
                    dve.tensor_scalar(table[:, :, 1], table[:, :, 0], 3, None,
                                      ALU.logical_shift_right).then_inc(table_ready, 1)
                build_table(E * l)

                step(dve.tensor_tensor(gate[:, :, :], mask[:, :, :], scores[:, :, :], ALU.mult))
                settle()
                step(dve.tensor_reduce(gsum[:, :], gate[:, :, :], AX, ALU.add))
                settle()
                step(dve.reciprocal(gsum[:, :], gsum[:, :]))
                settle()
                for t in range(T):
                    ins = dve.tensor_scalar(gate[:, t, :], gate[:, t, :], gsum[:, t:t + 1], ROUTED_SCALE, ALU.mult, ALU.mult)
                step(ins)
                settle()
                for k in range(TOPK):
                    step(dve.scalar_tensor_tensor(sel[:, :, :].rearrange("p a b -> p (a b)"),
                                                  krank[:, :, :].rearrange("p a b -> p (a b)"), float(k),
                                                  gate[:, :, :].rearrange("p a b -> p (a b)"), ALU.is_equal, ALU.mult))
                    settle()
                    step(dve.tensor_reduce(gk[:, :, k], sel[:, :, :], AX, ALU.add))
                    settle()

                base = MARK[("loop", l)]

                def glu(g, u):
                    b = 5 + u % 2
                    dve.wait_ge(filled[b], base[b] + 4 * g + u // 2 + 1)
                    dve.wait_ge(drained[1 + u % 2], base[1 + u % 2] + 4 * g + u // 2 + 1)
                    dve.tensor_tensor(aT[u % 2], s1[u % 2], psum[:, b, 0:P], ALU.mult).then_inc(drained[b], 1)

                def rows_out(g, u, first=False):
                    if not (first and u < YROWS and l == 0):
                        dve.wait_ge(y_out[u % YROWS], 16 * (2 * g + u // YROWS) + 16 * (E // YROWS) * l)
                    for half in range(2):
                        b = 3 + 4 * half
                        dve.wait_ge(filled[b], base[b] + SLOTS * g + u + 1)
                        cols_ = slice(512 * half, 512 * half + 512)
                        dve.tensor_tensor(yrow[u % YROWS][:, cols_], psum[:, b, :], g2bc[:, cols_], ALU.mult
                                          ).then_inc(drained[b], 1)

                def group(g, first=False):
                    for u in range(SLOTS):
                        glu(g, u)
                        if u:
                            rows_out(g, u - 1, first)
                        elif not first:
                            rows_out(g - 1, SLOTS - 1)
                group(0, first=True)
                with dve.Fori(1, NG) as g:
                    group(g)
                rows_out(NG - 1, SLOTS - 1)

                def more_blocks():
                    done = more[l]
                    own = [0]

                    def unit(b, e):
                        i = E * b + e
                        OWN = 3

                        def own_step(ins, n):
                            ins.then_inc(done["step"], 1)
                            dve.wait_ge(done["step"], OWN * i + n)
                        dve.tensor_copy(V1[:, :, 0:3], V[:, :, bass.ds(e, 1), :].rearrange("p t o c -> p (t o) c"))
                        own_step(dve.tensor_copy(pos1[:, :], pos[:, :, bass.ds(e, 1)].rearrange("p t o -> p (t o)")), 1)
                        own_step(dve.tensor_scalar(pos1[:, :], pos1[:, :], -float(P * (b + 1)), None, ALU.add), 2)
                        for t in range(T):
                            ins = dve.tensor_scalar(onehot[0][:, t, :], slot_no[:, :], pos1[:, t:t + 1], None, ALU.is_equal)
                        ins.then_inc(done["onehot"], 1)
                        dve.wait_ge(done["dest"], i + 1)
                        own_step(dve.tensor_reduce(destf[:, 0:1], psum[:, 6, 0:3], AX, ALU.add), 3)
                        dve.tensor_scalar(idx[0][:, 0:1], destf[:, 0:1], float(NOWHERE), None, ALU.add).then_inc(done["idx"], 1)
                        dve.wait_ge(done["idx"], 2 * i + 1)
                        dve.tensor_scalar(idx[0][:, 1:2], idx[0][:, 0:1], 3, None, ALU.logical_shift_right).then_inc(done["idx"], 1)
                        dve.wait_ge(done["silu"], i + 1)
                        dve.tensor_tensor(aT[0], s1[0], psum[:, 3, 0:P], ALU.mult).then_inc(done["gated"], 1)
                        dve.wait_ge(done["down"], i + 1)
                        for half in range(2):
                            cols_ = slice(512 * half, 512 * half + 512)
                            dve.tensor_tensor(yrow[0][:, cols_], psum[:, 4 + half, :], g2bc[:, cols_], ALU.mult
                                              ).then_inc(done["yrow"], 1)
                        dve.wait_ge(done["sent"], 16 * i + 16)
                    for b in range(YROWS):
                        dve.wait_ge(y_out[b], 16 * (E // YROWS) * (l + 1))
                    for b in range(MORE):
                        with dve.Fori(0, E) as e:
                            unit(b, e)
                when_more(dve, l, more_blocks)

                settle()
                dve.wait_ge(base_ready, T * (l + 1))
                k = 2 * l + 1
                for j in range(2 * T):
                    t, half = divmod(j, 2)
                    dve.wait_ge(part_in[j % 3], 16 * (j // 3 + 1 + PARTS_OF[j % 3] * l))
                    r = SH[:, t, 512 * half:512 * half + 512]
                    for i in range(TOPK):
                        step(dve.scalar_tensor_tensor(r, part[j % 3][:, i, :], gk[:, t, i:i + 1], r, ALU.mult, ALU.add))
                        settle()
                    PART[l].append(steps[0])
                    if half:
                        statistics(k, t, SH)
                        if t:
                            normalise(k, t - 1, SH, lnrow_moe)
                normalise(k, T - 1, SH, lnrow_moe)

            def attention():
                for v in (0, 1):
                    until_mod("kv", v)
                move_modulated("uT", 1, HT, MODC[("kv", 1)], MODC[("kv", 0)])
                ps = until_filled(dve, "forget")
                x2 = dts[:, 0:2, :].rearrange("p a b -> p (a b)")
                dve.scalar_tensor_tensor(x2.rearrange("p (a b) -> p a b", a=T), ps[:, 0:T * AH].rearrange("p (a b) -> p a b", a=T),
                                         -1.0, fb_bc.unsqueeze(1).to_broadcast([P, T, AH]), ALU.mult,
                                         ALU.subtract).then_inc(drained[6], 1)
                until_drained(dve, "forget")
                soft(dve.tensor_scalar(x2, x2, 1.0, None, ALU.mult))
                softplus(x2, logf[:, :, :].rearrange("p a b -> p (a b)"), T * AH, 4)
                dve.tensor_scalar(logf[:, :, :], logf[:, :, :], -1.0, None, ALU.mult).then_inc(logf_ready, 1)
                for j in range(1, KC, 2):
                    move(("kT", j), kT[:, j, :])
                ps = until_filled(dve, "cumf")
                dve.tensor_copy(cumf[:, :, :].rearrange("p a b -> p (a b)"), ps[:, 0:T * AH]).then_inc(drained[7], 1)
                for n in range(2):
                    for t in range(1, T, 2):
                        move(("v", n, t), vtok[:, t, 512 * n:512 * n + 512])
                ps = until_filled(dve, "cumfT")
                dve.tensor_copy(cumfT[:, :], ps[0:T * AH, 0:P]).then_inc(drained[7], 1)
                move_modulated("qhT", 1, HT, MODC[(1, SCALE1)], MODC[(1, SHIFT1)])
                for j in range(1, KC, 2):
                    move(("qT", j), qT[:, j, :])
                diagonals(1)

                def maximum(n):
                    h, i = divmod(n, T)
                    nk = P * (i + 1)
                    dve.wait_ge(masked, n + 1)
                    if n >= 3:
                        dve.wait_ge(prob_ready, n - 2)
                    ps = until_filled(dve, ("ncf", h))
                    ins = dve.tensor_tensor_reduce(shifted[n % 3][:, 0:nk], logit[n % 3][:, 0:nk], ps[:, 0:nk], 1.0, -3.0e38,
                                                   ALU.subtract, ALU.max, mx[:, n % 4:n % 4 + 1])
                    if i == T - 1:
                        ins.then_inc(drained[MARK[("ncf", h)][0]], 1)
                        until_drained(dve, ("ncf", h))
                    else:
                        step(ins)
                        settle()
                    dve.tensor_scalar(mx[:, 4 + n % 4:5 + n % 4], mx[:, n % 4:n % 4 + 1], -1.0, None, ALU.mult).then_inc(max_ready, 1)

                def move_probs(n):
                    h, i = divmod(n, T)
                    ps = until_filled(dve, ("pT", n))
                    dve.tensor_copy(probT[n % 2][:, 0:i + 1, :], ps[:, 0:P * (i + 1)].rearrange("p (a b) -> p a b", b=P)
                                    ).then_inc(drained[MARK[("pT", n)][0]], 1)

                def head_out(h):
                    ps = until_filled(dve, ("o", h))
                    dve.wait_ge(prob_ready, T * h + T)
                    step(dve.reciprocal(rinv[:, h % 2, :], rsum[:, h % 2, :]))
                    settle()
                    dve.tensor_tensor(otok[:, :, HD * h:HD * h + HD], ps[:, 0:T * HD].rearrange("p (a b) -> p a b", a=T),
                                      rinv[:, h % 2, :].unsqueeze(2).to_broadcast([P, T, HD]), ALU.mult
                                      ).then_inc(drained[MARK[("o", h)][0]], 1)
                NU = AH * T
                maximum(0)
                for n in range(NU):
                    if n + 1 < NU:
                        maximum(n + 1)
                    move_probs(n)
                    if n % T == 1 and n > T:
                        head_out(n // T - 1)
                head_out(AH - 1)
                move_turned("oT", 1, HT)
                mixed(1, Rmix[1])

            if phases >= 2:
                experts(0)
            if phases >= 3:
                attention()
            if phases >= 4:
                experts(1)

        @block.gpsimd
        def _(pool):
            steps = [0]

            def step(ins):
                ins.then_inc(pool_step, 1)
                steps[0] += 1

            def settle():
                pool.wait_ge(pool_step, steps[0])

            last_row, last_part = pool.alloc_register("last_row"), pool.alloc_register("last_part")
            pool.reg_mov(last_row, S - 1)
            pool.reg_mov(last_part, S * TOPK - 1)
            step(pool.memset(ident[:, :], 0.0))
            step(pool.memset(upper[:, :], 1.0))
            step(pool.memset(after[:, :], 1.0))
            step(pool.memset(before_b[:, :], 1.0))
            step(pool.memset(low8[:, :, :], 1.0))
            pool.memset(ones[:, :], 1.0).then_inc(consts, 1)
            pool.memset(ones_b[:, :], 1.0).then_inc(consts, 1)
            pool.iota(slot_no[:, :], [[1, P]], base=0, channel_multiplier=0,
                      allow_small_or_imprecise_dtypes=True).then_inc(consts, 1)
            pool.iota(V[:, :, :, 0], [[0, T], [0, E]], base=0, channel_multiplier=TOPK,
                      allow_small_or_imprecise_dtypes=True).then_inc(consts, 1)
            pool.iota(V[:, :, :, 1], [[P * TOPK, T], [0, E]], base=-NOWHERE, channel_multiplier=0,
                      allow_small_or_imprecise_dtypes=True).then_inc(consts, 1)
            settle()
            pool.affine_select(out=ident[:, :], in_=ident[:, :], compare_op=ALU.not_equal, fill=1.0, base=0,
                               pattern=[[-1, P]], channel_multiplier=1).then_inc(consts, 1)
            pool.affine_select(out=upper[:, :], in_=upper[:, :], compare_op=ALU.is_ge, fill=0.0, base=0,
                               pattern=[[1, P]], channel_multiplier=-1).then_inc(consts, 1)
            pool.affine_select(out=after[:, :], in_=after[:, :], compare_op=ALU.is_gt, fill=0.0, base=0,
                               pattern=[[-1, P]], channel_multiplier=1).then_inc(consts, 1)
            pool.affine_select(out=before_b[:, :], in_=before_b[:, :], compare_op=ALU.is_gt, fill=0.0, base=0,
                               pattern=[[1, P]], channel_multiplier=-1).then_inc(consts, 1)
            pool.affine_select(out=low8[:, :, :], in_=low8[:, :, :], compare_op=ALU.is_gt, fill=0.0, base=0,
                               pattern=[[1, EG], [-1, EG]], channel_multiplier=0).then_inc(consts, 1)
            pool.wait_ge(consts, CONSTS)

            for a in range(1, len(ada_blocks), 2):
                pool.wait_ge(ada_scaled, a // 2 + 1)
                w = ada_pool[a // 2 % 2]
                for n in (4, 2):
                    step(pool.tensor_tensor(w[:, 0:n, :], w[:, 0:n, :], w[:, n:2 * n, :], ALU.add))
                    settle()
                if a >= 2:
                    until_filled(pool, ("mod",) + ada_blocks[a - 2])
                pool.tensor_tensor(ada_acc[1], w[:, 0, :], w[:, 1, :], ALU.add).then_inc(ada_summed[1], 1)

            pool.wait_ge(dA_ready, 1)
            pool.wait_ge(ada_summed[0], len(ada_blocks) // 2)

            def segments(q):
                ch, g = divmod(q, GROUPS)
                for half in range(2):
                    if q:
                        until_filled(pool, ("seg", q - 1, half))
                    for j in range(4):
                        h = GH * g + 4 * half + j
                        ins = pool.tensor_scalar(stepm[4 * half + j], after[:, :], dA[:, ch, h:h + 1], 1.0, ALU.mult, ALU.mult)
                    ins.then_inc(stepm_ready, 1)

            def heads(v):
                return v.rearrange("p (h d) -> p h d", h=GH)

            def bch(v):
                return v.unsqueeze(2).to_broadcast([P, GH, HD])

            def scan_pool(q):
                ch, g = divmod(q, GROUPS)
                until_drained(pool, ("sums", ch))
                pool.wait_ge(xdt_ready, q + 1)
                if q >= 2 and ch < T - 1:
                    until_filled(pool, ("st", q - 2))
                if ch < T - 1:
                    pool.tensor_tensor(heads(xdte[q % 2]), heads(xdt[q % 2]),
                                       bch(exps[ch % 2][:, HEADS + GH * g:HEADS + GH * g + GH]), ALU.mult).then_inc(xdte_ready, 1)
                if 0 < ch < T - 1:
                    until_filled(pool, ("yoff", q))
                    pool.tensor_tensor(heads(state[:, g, :]), heads(state[:, g, :]),
                                       bch(exps[ch % 2][:, 2 * HEADS + GH * g:2 * HEADS + GH * g + GH]),
                                       ALU.mult).then_inc(state_scaled, 1)
                until_drained(pool, ("yd", q))
                if ch:
                    until_drained(pool, ("yoff", q))
                    step(pool.tensor_tensor(yg[q % 2], yg[q % 2], yoff[q % 2], ALU.add))
                    settle()
                z = zs[:, ch, GW * g:GW * g + GW]
                pool.tensor_tensor(z, yg[q % 2], z, ALU.mult).then_inc(yz_ready, 1)
            segments(0)
            for q in range(NQ):
                if q + 1 < NQ:
                    segments(q + 1)
                scan_pool(q)

            def layer_norm(k, lnrow):
                for t in range(T):
                    pool.wait_ge(ln_scaled, T * k + t + 1)
                    pool.tensor_tensor(X[:, t, :], X[:, t, :], lnrow[1], ALU.add).then_inc(x_ready, 1)
            layer_norm(0, lnrow_mix)

            def experts(l):
                for half in range(2):
                    until_drained(pool, (("sh2", l), half))
                for t in range(T):
                    pool.wait_ge(h2_scaled, T * l + t + 1)
                    pool.tensor_tensor(H2[:, t, :], H2[:, t, :], sh2bc, ALU.add).then_inc(h2_ready, 1)
                for t in range(T):
                    pool.wait_ge(h2_ready, T * l + t + 1)
                    pool.dma_start(rows_dram[TILES[t], :], H2[:, t, :]).then_inc(h2_out, 16)
                until_drained(pool, (("shared_in", l, 0)))
                until_drained(pool, (("shared_in", l, 1)))
                pool.tensor_tensor(aS[0], aS[0], aS[1], ALU.mult).then_inc(sh_gated, 1)
                for half in range(2):
                    until_drained(pool, (("g2", l), half))
                for t in range(T):
                    for n in range(2):
                        until_drained(pool, ("shared", l, t, n))
                    step(pool.tensor_tensor(SH[:, t, :], SH[:, t, :], g2bc, ALU.mult))
                    settle()
                    pool.wait_ge(x_scaled, T * l + t + 1)
                    pool.tensor_tensor(SH[:, t, :], SH[:, t, :], X[:, t, :], ALU.add).then_inc(base_ready, 1)
                pool.wait_ge(table_ready, l + 1)
                pool.wait_ge(h2_out, 16 * T * (l + 1))
                base = MARK[("loop", l)]

                def carrier(n):
                    return pool.tensor_tensor(passed[:, n:n + 1], ones[:, 0:1], ones[:, 1:2], ALU.mult)

                def fetch(g, u, first=False):
                    if not first:
                        pool.wait_ge(y_out[u % YROWS], 16 * (2 * g + u // YROWS - 1) + 16 * (E // YROWS) * l)
                    if not (first and u < 4):
                        pool.wait_ge(filled[4], base[4] + SLOTS * g + u - 3)
                    pool.tensor_copy(idx[u][:, :], table[:, bass.ds(SLOTS * g + u, 1), :].rearrange("p a b -> p (a b)")
                                     ).then_inc(idx_ready[0], 1)
                    pool.wait_ge(idx_ready[0], E * l + SLOTS * g + u + 1)
                    carrier(SLOTS)
                    pool.indirect_dma_start(out=xg[u % 4], out_offset=None, in_=rows_dram,
                                            in_offset=bass.IndirectOffsetOnAxis(ap=idx[u][:, 1:2], axis=0),
                                            bounds_check=last_row, oob_is_err=False).then_inc(xg_in[u % 4], 16)

                def send(g, u):
                    for b in (3, 7):
                        pool.wait_ge(drained[b], base[b] + SLOTS * g + u + 1)
                    carrier(u)
                    pool.indirect_dma_start(out=part_dram,
                                            out_offset=bass.IndirectOffsetOnAxis(ap=idx[u][:, 0:1], axis=0),
                                            in_=yrow[u % YROWS], in_offset=None,
                                            bounds_check=last_part, oob_is_err=False).then_inc(y_out[u % YROWS], 16)

                AHEAD = 5

                def group(g, first=False, last=False):
                    for u in range(SLOTS):
                        v = u + AHEAD
                        if v < SLOTS:
                            fetch(g, v, first)
                        elif not last:
                            fetch(g + 1, v - SLOTS)
                        send(g, u)
                for t in range(T):
                    until_filled(pool, ((("h2T", l)), t, 1))
                for u in range(AHEAD):
                    fetch(0, u, True)
                group(0, first=True)
                with pool.Fori(1, NG - 1) as g:
                    group(g)
                group(NG - 1, last=True)

                def more_blocks():
                    done = more[l]

                    def unit(i):
                        pool.wait_ge(done["idx"], 2 * i + 2)
                        carrier(SLOTS + 1).then_inc(done["carried"], 1)
                        pool.indirect_dma_start(out=xg[0], out_offset=None, in_=rows_dram,
                                                in_offset=bass.IndirectOffsetOnAxis(ap=idx[0][:, 1:2], axis=0),
                                                bounds_check=last_row, oob_is_err=False).then_inc(done["rows"], 16)
                        pool.wait_ge(done["yrow"], 2 * i + 2)
                        pool.wait_ge(done["carried"], i + 1)
                        carrier(SLOTS + 2)
                        pool.indirect_dma_start(out=part_dram,
                                                out_offset=bass.IndirectOffsetOnAxis(ap=idx[0][:, 0:1], axis=0),
                                                in_=yrow[0], in_offset=None,
                                                bounds_check=last_part, oob_is_err=False).then_inc(done["sent"], 16)
                    for b in range(MORE):
                        with pool.Fori(0, E) as e:
                            unit(E * b + e)
                when_more(pool, l, more_blocks)
                layer_norm(2 * l + 1, lnrow_moe)

            def attention():
                NU = AH * T
                for n in range(NU):
                    h, i = divmod(n, T)
                    until_drained(pool, ("qk", n))
                    d = logit[n % 3][:, P * i:P * i + P]
                    pool.affine_select(out=d, in_=d, compare_op=ALU.is_ge, fill=-BIG, base=0, pattern=[[-1, P]],
                                       channel_multiplier=1).then_inc(masked, 1)
                layer_norm(2, lnrow_mix)

            if phases >= 2:
                experts(0)
            if phases >= 3:
                attention()
            if phases >= 4:
                experts(1)

        @block.sync
        def _(sp_):
            def as_rows(v, n):
                return v.rearrange("(n p) -> n p", p=P)

            def load(dst, src, done=small_in):
                sp_.dma_start(dst, src).then_inc(done, 16)

            def ada_cols(a):
                l, blk = ada_blocks[a]
                return cols_of(kv_ada_w if l == "kv" else ada_w[l], 512 * blk)

            def load_ada(a):
                half = KC // 2
                if a:
                    sp_.wait_ge(ada_half, a // 2)
                sp_.dma_start(ada_dve[:, 0:half, :], ada_cols(a)[:, 0:half, :]).then_inc(ada_dve_in[0], 16)
                if a >= 4:
                    sp_.wait_ge(ada_summed[1], a // 2 - 1)
                n = a // 2 % 2
                sp_.dma_start(ada_pool[n], ada_cols(a + 1)).then_inc(ada_pool_in[n], 16)
                if a:
                    sp_.wait_ge(ada_summed[0], a // 2)
                sp_.dma_start(ada_dve[:, half:KC, :], ada_cols(a)[:, half:KC, :]).then_inc(ada_dve_in[1], 16)

            for dst, src in ((rows[0:8, 0, :], as_rows(c[0], 8)),
                             (rows[8:56, 0, :], as_rows(ada_b[0], 48)),
                             (rows[56:104, 0, :], as_rows(ada_b[1], 48)),
                             (rows[104:120, 0, :], as_rows(kv_ada_b, 16)),
                             (rows[0:CONV * CT, 1, :], ssm_conv_w[0].rearrange("k (n p) -> (k n) p", p=P)),
                             (rows[CONV * CT:CONV * CT + CT, 1, :], as_rows(ssm_conv_b[0], CT)),
                             (rows[0:XT, 2, :], as_rows(ssm_norm_w[0], XT))):
                load(dst, src, rows_in_sem)
            load_ada(0)
            for t in range(T):
                sp_.dma_start(X[:, t, :], x[0, TILES[t], :]).then_inc(x_in, 16)
            at = 0
            for v in (ssm_dt_bias[0], ssm_a_log[0], ssm_d[0], kv_fb, moe_bias[0], moe_bias[1]):
                n = v.shape[0]
                load(bcs[:, at:at + n], v.partition_broadcast(P))
                at += n
            load(wdt[:, :, :], ssm_w_in[0].rearrange("(k p) n -> p k n", p=P)[:, :, DI + XBC:DI + XBC + HEADS])
            load(wf[:, :, :], kv_w.rearrange("(k p) n -> p k n", p=P)[:, :, 2 * D:2 * D + AH])
            load(wr[:, :, :], moe_w_router[0].rearrange("(k p) n -> p k n", p=P))
            load_ada(2)

            def stream(i):
                if i >= RING:
                    b, n = MARK[("item", i - RING)]
                    sp_.wait_ge(filled[b], n)
                sp_.dma_start(ring[i % RING], items[i][1]).then_inc(ring_in[i % RING], 16)
            for i in range(2):
                stream(i)
            for n in range(CT // 4):
                for half in range(2):
                    load_ada(ada_beside(n, half)[0])
                stream(n + 2)
            for i in range(CT // 4 + 2, n_items0):
                stream(i)

            def ln_rows(k, dst, g, b):
                sp_.dma_start(dst[0], g.partition_broadcast(P)).then_inc(lnrow_in, 16)
                sp_.dma_start(dst[1], b.partition_broadcast(P)).then_inc(lnrow_in, 16)

            def experts(l):
                b, n = MARK[("mix", l, 1, T - 1)]
                sp_.wait_ge(filled[b], n)
                sp_.dma_start(shw[:, 0, :].rearrange("p (k f) -> p k f", k=KC),
                              moe_ws1[l].rearrange("(k p) f -> p k f", p=P)).then_inc(shw_in, 16)
                sp_.dma_start(shw[:, 1, :].rearrange("p (k f) -> p k f", k=KC),
                              moe_ws3[l].rearrange("(k p) f -> p k f", p=P)).then_inc(shw_in, 16)
                sp_.dma_start(shw[:, 2, :], moe_ws2[l]).then_inc(shw_in, 16)

                def fetch(i, u):
                    for n, w in enumerate((moe_w1, moe_w3)):
                        src = w[l][bass.ds(i, 1), :, :] if not isinstance(i, int) else w[l][i:i + 1, :, :]
                        sp_.dma_start(exp_w[u][:, n, :].rearrange("p (k f) -> p k f", k=KC),
                                      src.rearrange("o (k p) f -> p (o k) f", p=P)).then_inc(exp_in[u], 16)
                    src = moe_w2[l][bass.ds(i, 1), :, :] if not isinstance(i, int) else moe_w2[l][i:i + 1, :, :]
                    sp_.dma_start(exp_w[u][:, 2, :], src.rearrange("o f d -> f (o d)")).then_inc(exp_in[u], 16)
                base = MARK[("loop", l)]
                for u in range(4, SLOTS):
                    fetch(u, u)
                sp_.wait_ge(x_ready, T * (2 * l + 1))
                for u in range(4):
                    fetch(u, u)
                with sp_.Fori(1, NG) as g:
                    for u in range(SLOTS):
                        sp_.wait_ge(filled[7], base[7] + SLOTS * g + u - SLOTS + 1)
                        fetch(SLOTS * g + u, u)
                for b in range(YROWS):
                    sp_.wait_ge(y_out[b], 16 * (E // YROWS) * (l + 1))

                def more_blocks():
                    done = more[l]

                    def unit(b, e):
                        sp_.wait_ge(done["onehot"], E * b + e + 1)
                        for n, w in enumerate((moe_w1, moe_w3)):
                            sp_.dma_start(exp_w[0][:, n, :].rearrange("p (k f) -> p k f", k=KC),
                                          w[l][bass.ds(e, 1), :, :].rearrange("o (k p) f -> p (o k) f", p=P)
                                          ).then_inc(done["weights"], 16)
                        sp_.dma_start(exp_w[0][:, 2, :], moe_w2[l][bass.ds(e, 1), :, :].rearrange("o f d -> f (o d)")
                                      ).then_inc(done["weights"], 16)
                    for b in range(MORE):
                        with sp_.Fori(0, E) as e:
                            unit(b, e)
                    sp_.wait_ge(done["sent"], 16 * MORE * E)
                when_more(sp_, l, more_blocks)
                ln_rows(2 * l + 1, lnrow_moe, ln2_g[l], ln2_b[l])
                rows_of = part_dram.rearrange("(t p k) d -> t p k d", p=P, k=TOPK)
                for j in range(2 * T):
                    t, half = divmod(j, 2)
                    if j >= 3:
                        sp_.wait_ge(dve_step, PART[l][j - 3])
                    sp_.dma_start(part[j % 3], rows_of[t, :, :, 512 * half:512 * half + 512]).then_inc(part_in[j % 3], 16)

            sp_.wait_ge(squared, NQ)
            until_filled(sp_, ("mix", 0, 0, 0))
            ln_rows(0, lnrow_mix, ln1_g[0], ln1_b[0])
            if phases >= 2:
                experts(0)
            if phases >= 3:
                until_filled(sp_, "wr0")
                sp_.dma_start(wr[:, :, :], moe_w_router[1].rearrange("(k p) n -> p k n", p=P)).then_inc(wr_in, 16)
                for i in range(n_items0, n_items1):
                    if i < n_items0 + RING:
                        sp_.dma_start(ring[i % RING], items[i][1]).then_inc(ring_in[i % RING], 16)
                    else:
                        stream(i)
                until_filled(sp_, ("mix", 1, 0, 0))
                ln_rows(2, lnrow_mix, ln1_g[1], ln1_b[1])
            if phases >= 4:
                experts(1)
            for t in range(T):
                sp_.wait_ge(x_ready, T * (phases - 1) + t + 1)
                sp_.dma_start(out[0, TILES[t], :], X[:, t, :]).then_inc(out_done, 16)
            sp_.wait_ge(out_done, 16 * T)


_INS = ["x", "c", "ada_w", "ada_b", "ln1_g", "ln1_b", "ln2_g", "ln2_b", "ssm_w_in", "ssm_conv_w", "ssm_conv_b",
        "ssm_dt_bias", "ssm_a_log", "ssm_d", "ssm_norm_w", "ssm_w_out", "kv_ada_w", "kv_ada_b", "kv_w", "kv_fb",
        "attn_w_q", "attn_w_o", "moe_w_router", "moe_bias", "moe_w1", "moe_w3", "moe_w2", "moe_ws1", "moe_ws3",
        "moe_ws2"]
_OUTS = [((1, 512, 1024), "float32")]


def kernel(**inputs):
    import numpy as _np
    import concourse.bacc as _bacc
    from concourse import mybir as _mybir
    from concourse.bass_utils import run_bass_kernel_spmd as _run

    nc = _bacc.Bacc("TRN2", target_bir_lowering=False, num_devices=1)
    arrays, args = {}, []
    for name in _INS:
        a = _np.ascontiguousarray(inputs[name])
        arrays[f"in_{name}_dram"] = a
        args.append(nc.dram_tensor(f"in_{name}_dram", a.shape, _mybir.dt.from_np(a.dtype), kind="ExternalInput").ap())
    for i, (shape, dtype) in enumerate(_OUTS):
        dt = _mybir.dt.from_np(_np.dtype(dtype))
        args.append(nc.dram_tensor(f"out_{i}_dram", shape, dt, kind="ExternalOutput").ap())
    trunk(nc, *args)
    r = _run(nc, [arrays], core_ids=[0])
    got = tuple(r.results[0][f"out_{i}_dram"] for i in range(len(_OUTS)))
    return got[0]
```

```python
from contextlib import ExitStack

import concourse.bass as bass
from concourse import mybir

F32 = mybir.dt.float32
BF16 = mybir.dt.bfloat16
I32 = mybir.dt.int32
ALU = mybir.AluOpType
ACT = mybir.ActivationFunctionType
AX = mybir.AxisListType.X

P = 128
D = 1024
S = 512
T = S // P
KC = D // P
DI = 2048
HEADS = 32
HD = 64
GROUPS = 4
NST = 128
GH = HEADS // GROUPS
GW = GH * HD
GN = GROUPS * NST
CONV = 4
XBC = DI + 2 * GN
XT = DI // P
CT = XBC // P
AH = 16
E = 64
EG = 8
EPG = E // EG
TOPG = 4
TOPK = 8
F = D // 8
ROUTED_SCALE = 2.5
ALPHA = 4.0 ** 0.25
EPS = 1e-5
ASCALE = HD ** -0.5
BIG = 1.0e30
RING = 3
SLOTS = 8
YROWS = 4
DVE_ROWS = 5
NOWHERE = 2 * S * TOPK


def trunk(nc, x, c, ada_w, ada_b, ln1_g, ln1_b, ln2_g, ln2_b, ssm_w_in, ssm_conv_w, ssm_conv_b,
          ssm_dt_bias, ssm_a_log, ssm_d, ssm_norm_w, ssm_w_out, kv_ada_w, kv_ada_b, kv_w, kv_fb,
          attn_w_q, attn_w_o, moe_w_router, moe_bias, moe_w1, moe_w3, moe_w2, moe_ws1, moe_ws3,
          moe_ws2, out):
    ctx = ExitStack()
    with ctx:
        def sb(name, shape, dt=F32):
            return ctx.enter_context(nc.sbuf_tensor(name, shape, dt))

        def sem(name):
            return ctx.enter_context(nc.semaphore(name))

        KB = 256
        arena = sb("arena", [P, 191 * KB])

        def view(kb, *dims):
            n = 1
            for d in dims:
                n *= d
            v = arena[:, int(kb * KB):int(kb * KB) + n]
            names = "abcd"[:len(dims)]
            if len(dims) == 1:
                return v
            return v.rearrange(f"p ({' '.join(names)}) -> p {' '.join(names)}",
                               **dict(zip(names[1:], dims[1:])))

        X = view(0, T, D)
        HT = view(16, KC, S)
        ring = [view(143 + 16 * r, KC, 512) for r in range(RING)]
        exp_w = [view(95 + 12 * r, 3, 1024) for r in range(SLOTS)]
        xbcT = view(32, CT, S)
        zs = view(80, T, DI)
        ada_dve = view(120, KC, 512)
        ada_pool = [view(80 + 16 * i, KC, 512) for i in range(2)]
        ada_acc = [view(116 + 2 * i, 512) for i in range(2)]
        conv_acc = [view(112 + 2 * i, S) for i in range(2)]
        xdt = [view(112 + 2 * i, GW) for i in range(2)]
        xsD = [view(116 + 2 * i, GW) for i in range(2)]
        xdte = [view(120 + 2 * i, GW) for i in range(2)]
        decay = [view(124 + 2 * i, 4 * P) for i in range(2)]
        mixm = [view(128 + 2 * i, 4 * P) for i in range(2)]
        stepm = [view(132 + 0.5 * i, P) for i in range(8)]
        Btok = [view(136 + 0.5 * i, P) for i in range(2)]
        CBm = [view(137 + 0.5 * i, P) for i in range(2)]
        state = view(16, GROUPS, GW)
        yg = [view(24 + 2 * i, GW) for i in range(2)]
        yoff = [view(28 + 2 * i, GW) for i in range(2)]
        kT = view(32, KC, S)
        vtok = view(48, T, D)
        qT = [view(64, KC, S), view(120, KC, S)]
        otok = view(80, T, D)
        logit = [view(96 + 2 * i, S) for i in range(3)]
        shifted = [view(102 + 2 * i, S) for i in range(3)]
        prob = [view(108 + 2 * i, S) for i in range(3)]
        probT = [view(114 + 2 * i, T, P) for i in range(2)]
        g1bc = view(139, D)
        Rmix = [view(16, T, D), view(32, T, D)]
        lnrow_mix = [view(112, D), view(116, D)]
        diag = {name: view(120 + 4 * i, KC, P) for i, name in enumerate(("g1", "s2", "sh2", "g2"))}
        H2 = view(32, T, D)
        SH = view(48, T, D)
        s2bc = view(68, D)
        sh2bc = view(72, D)
        g2bc = view(76, D)
        shw = view(80, 3, 1024)
        aS = [view(92, S), SH[:, T - 1, 512:1024]]
        xg = [view(32 + 4 * i, D) for i in range(4)]
        xeT = [view(80 + 4 * i, KC, P) for i in range(2)]
        s1 = [view(88 + 0.5 * i, P) for i in range(2)]
        aT = [view(89 + 0.5 * i, P) for i in range(2)]
        yrow = [view(16 + 4 * i, D) for i in range(YROWS)]
        part = [view(kb, TOPK, 512) for kb in (95, 111, 32)]
        lnrow_moe = [view(80, D), view(84, D)]
        scores, sel, mask, gate, krank = (view(64 + i, T, E) for i in range(5))
        top8 = view(70, T * EG, 8)
        gcmp = [view(71 + i, T, EG, EG) for i in range(2)]
        pos = view(72, T, E)

        def view_b(kb, *dims):
            v = view(kb, dims[0] * dims[1] // 2).bitcast(BF16)
            return v.rearrange("p (a b) -> p a b", b=dims[1])
        mask_b = view_b(73, T, E)
        onehot = [view_b(kb, T, P) for kb in (73.5, 69, 70, 71)]

        ident = sb("ident", [P, P])
        upper = sb("upper", [P, P])
        after = sb("after", [P, P])
        ones = sb("ones", [P, P])
        before_b = sb("before_b", [P, P], BF16)
        ones_b = sb("ones_b", [P, P], BF16)
        slot_no = sb("slot_no", [P, P], BF16)
        low8 = sb("low8", [P, EG, EG])
        cols = sb("cols", [P, 3, P])
        bcs = sb("bcs", [P, 240])
        condT = sb("condT", [P, KC])
        mod = sb("mod", [P, 112])
        wdt = view(139, KC, HEADS)
        wf = sb("wf", [P, KC, AH])
        wr = sb("wr", [P, KC, E])
        dtx = sb("dtx", [P, T, HEADS])
        dts = sb("dts", [P, T, HEADS])
        dA = sb("dA", [P, T, HEADS])
        negA = sb("negA", [P, HEADS])
        sp_all = sb("sp", [P, 4, P])
        sp = [sp_all[:, i, :] for i in range(4)]
        rows = sp_all[:, 0:3, :]
        logf = sb("logf", [P, T, AH])
        ssum = sb("ssum", [P, T])
        exps = [sb(f"exps{i}", [P, 96]) for i in range(2)]
        ssq = sb("ssq", [P, T, GROUPS])
        rsy = sb("rsy", [P, T])
        cumf = sb("cumf", [P, T, AH])
        cumfT = sb("cumfT", [P, P])
        mx = sb("mx", [P, 8])
        rsum = sb("rsum", [P, 2, T])
        rinv = sb("rinv", [P, 2, T])
        bn = sb("bn", [P, T, 2, 6])
        mv = sb("mv", [P, T, 2])
        sd = sb("sd", [P, T])
        rstd = sb("rstd", [P, T])
        gsc = sb("gsc", [P, T, EG])
        grank = sb("grank", [P, T, EG])
        gk = sb("gk", [P, T, TOPK])
        gsum = sb("gsum", [P, T])
        V = sb("V", [P, T, E, 3], BF16)
        destf = sb("destf", [P, E])
        table = view(90, E, 2).bitcast(I32)
        pos1 = view(74.75, T)
        V1 = view_b(74.5, T, 4)
        idx = [sb(f"idx{i}", [P, 2], I32) for i in range(8)]
        passed = sb("passed", [P, SLOTS + 3])
        load_keys = view(75.5, E)
        load_top = view(75.75, 32)
        load_expert = view(75.875, 32).bitcast(I32)
        more_key = sb("more_key", [P, 2])
        more_keyi = sb("more_keyi", [P, 2], I32)
        psum = ctx.enter_context(nc.psum_tensor("psum", [P, 8, 512], F32))

        rows_dram = nc.dram_tensor("h2_rows", [S, D], F32, kind="Internal").ap()
        part_dram = nc.dram_tensor("expert_rows", [S * TOPK, D], F32, kind="Internal").ap()

        c_col = cols[:, 0, 0:8]
        modb = cols[:, 0, 8:120]
        convw = cols[:, 1, 0:CONV * CT].rearrange("p (k j) -> p k j", k=CONV)
        convb = cols[:, 1, CONV * CT:CONV * CT + CT]
        normw = cols[:, 2, 0:XT]
        dtb_bc, alog_bc, dsk_bc, fb_bc = bcs[:, 0:32], bcs[:, 32:64], bcs[:, 64:96], bcs[:, 96:112]
        rb_bc = [bcs[:, 112:176], bcs[:, 176:240]]
        MODC = {(l, v): 48 * l + 8 * v for l in range(2) for v in range(6)}
        MODC[("kv", 0)], MODC[("kv", 1)] = 96, 104
        SHIFT1, SCALE1, GATE1, SHIFT2, SCALE2, GATE2 = range(6)

        filled = [sem(f"filled{b}") for b in range(8)]
        drained = [sem(f"drained{b}") for b in range(8)]
        ring_in = [sem(f"ring_in{r}") for r in range(RING)]
        exp_in = [sem(f"exp_in{r}") for r in range(SLOTS)]
        vectors_in = sem("vectors_in")
        small_in = sem("small_in")
        ada_dve_in = [sem(f"ada_dve_in{i}") for i in range(2)]
        ada_half = sem("ada_half")
        ada_pool_in = [sem(f"ada_pool_in{i}") for i in range(2)]
        ada_scaled = sem("ada_scaled")
        ada_summed = [sem(f"ada_summed{i}") for i in range(2)]
        x_in = sem("x_in")
        consts = sem("consts")
        act_step = sem("act_step")
        dve_step = sem("dve_step")
        pool_step = sem("pool_step")
        vec_cols = sem("vec_cols")
        cond_ready = sem("cond_ready")
        acc_ready = sem("acc_ready")
        conv_done = sem("conv_done")
        soft_act = sem("soft_act")
        soft_dve = sem("soft_dve")
        dA_ready = sem("dA_ready")
        exps_ready = sem("exps_ready")
        stepm_ready = sem("stepm_ready")
        xdt_ready = sem("xdt_ready")
        xdte_ready = sem("xdte_ready")
        decay_ready = sem("decay_ready")
        mixm_ready = sem("mixm_ready")
        state_scaled = sem("state_scaled")
        yz_ready = sem("yz_ready")
        squared = sem("squared")
        diag_ready = sem("diag_ready")
        bc_ready = sem("bc_ready")
        res_ready = sem("res_ready")
        sd_ready = sem("sd_ready")
        var_ready = sem("var_ready")
        lnrow_in = sem("lnrow_in")
        ln_scaled = sem("ln_scaled")
        x_scaled = sem("x_scaled")
        base_ready = sem("base_ready")
        x_ready = sem("x_ready")
        h2_scaled = sem("h2_scaled")
        h2_ready = sem("h2_ready")
        h2_out = sem("h2_out")
        shw_in = sem("shw_in")
        wr_in = sem("wr_in")
        scores_ready = sem("scores_ready")
        mask_ready = sem("mask_ready")
        onehot_ready = sem("onehot_ready")
        onehot_used = sem("onehot_used")
        table_ready = sem("table_ready")
        sh_gated = sem("sh_gated")
        most_ready = sem("most_ready")
        more = [{name: sem(f"more_{name}{l}") for name in (
            "onehot", "dest", "idx", "rows", "turned", "moved", "weights", "up", "silu", "gated", "down", "yrow",
            "sent", "step", "carried")} for l in range(2)]
        idx_ready = sem("idx_ready")
        xg_in = [sem(f"xg_in{i}") for i in range(4)]
        y_out = [sem(f"y_out{i}") for i in range(YROWS)]
        s1_ready = sem("s1_ready")
        part_in = [sem(f"part_in{i}") for i in range(3)]
        part_scaled = sem("part_scaled")
        part_added = sem("part_added")
        q_zeros = sem("q_zeros")
        masked = sem("masked")
        max_ready = sem("max_ready")
        prob_ready = sem("prob_ready")
        logf_ready = sem("logf_ready")
        out_done = sem("out_done")

        MARK = {}
        PART = ([], [])
        PARTS_OF = [len(range(i, 2 * T, 3)) for i in range(3)]

        def until_filled(eng, key):
            b, n = MARK[key]
            eng.wait_ge(filled[b], n)
            return psum[:, b, :]

        def until_drained(eng, key):
            b, n = MARK[key]
            eng.wait_ge(drained[b], n)

        MORE = ([(0, 0, 8, 0)], [(0, 8, 32, 0), (1, 0, 16, 32), (2, 0, 10, 48)])
        MORE_UNITS = (8, 58)
        OVER = (P + 1) * P - 1

        def table_bank(u):
            return 6 - u % 2

        def tables_before(b, u, first):
            if b not in (5, 6):
                return 0
            at = u if first else E // SLOTS - 1
            return len([v for v in range(at) if table_bank(v) == b])

        def when_more(eng, l, blocks):
            eng.wait_ge(most_ready, l + 1)
            for stage in range(2):
                key = eng.value_load(more_keyi[0:1, stage:stage + 1])
                with eng.If(key > OVER):
                    blocks(stage)
                with eng.Else():
                    eng.nop()

        items = []

        def cols_of(w, n0, n=512):
            return w.rearrange("(k p) n -> p k n", p=P)[:, :, n0:n0 + n]

        w_in = ssm_w_in[0]
        for n, blk in enumerate([4, 5, 0, 1, 2, 3, "z0", "z1", "z2", "z3"]):
            if isinstance(blk, int):
                items.append((("xbc", blk), cols_of(w_in, DI + 512 * blk)))
            else:
                items.append((("z", int(blk[1])), cols_of(w_in, 512 * int(blk[1]))))
        for n in range(2):
            for kh in range(2):
                items.append((("w_out", n, kh), cols_of(ssm_w_out[0][D * kh:D * (kh + 1), :], 512 * n)))
        n_items0 = len(items)
        ada_blocks = [(0, b) for b in range(12)] + [("kv", b) for b in range(4)] + [(1, b) for b in range(12)]
        ADA_FIRST = 4
        ADA_PAIRED = 20

        def ada_beside(n, half):
            h = 2 * n + half
            return () if h % 3 == 2 else (ADA_FIRST + 2 * (h - h // 3), ADA_FIRST + 2 * (h - h // 3) + 1)

        def ada_beside_z(n, half):
            return ADA_PAIRED + 2 * n + half

        def ada_engine(a):
            return a % 2 if a < ADA_PAIRED else 0

        def ada_count(a):
            return a // 2 if a < ADA_PAIRED else a - ADA_PAIRED // 2
        ADA_OF = (len(ada_blocks) - ADA_PAIRED // 2, ADA_PAIRED // 2)

        for n in range(4):
            items.append((("kvw", n), cols_of(kv_w, 512 * n)))
        for n in range(2):
            items.append((("wq", n), cols_of(attn_w_q[0], 512 * n)))
        for n in range(2):
            items.append((("wo", n), cols_of(attn_w_o[0], 512 * n)))
        n_items1 = len(items)

        CONSTS = 10
        ROWS = 7 * 16
        SMALL = 9 * 16
        TILES = [slice(P * t, P * t + P) for t in range(T)]
        NQ = T * GROUPS
        NG = E // SLOTS

        def stream_order():
            for key, _ in items:
                if key[0] == "w_out":
                    return
                yield key

        block = ctx.enter_context(nc.Block())

        @block.tensor
        def _(pe):
            uses = [0] * 8
            taken = [0]

            def claim(b):
                if uses[b]:
                    pe.wait_ge(drained[b], uses[b])
                uses[b] += 1
                return psum[:, b, :]

            def fill(ins, b, key):
                ins.then_inc(filled[b], 1)
                MARK[key] = (b, uses[b])

            def take(key):
                i = taken[0]
                assert items[i][0] == key, (items[i][0], key)
                taken[0] += 1
                pe.wait_ge(ring_in[i % RING], 16 * (i // RING + 1))
                return ring[i % RING], ("item", i)

            def done_item(tag, key):
                MARK[tag] = MARK[key]

            def ada(a):
                l, blk = ada_blocks[a]
                e = ada_engine(a)
                b = 4 + e
                pe.wait_ge(ada_summed[e], ada_count(a) + 1)
                ps = claim(b)
                for j in range(4):
                    mm = pe.matmul(ps[:, j:j + 1], ada_acc[e][:, P * j:P * j + P], ones[:, 0:1], start=True, stop=True)
                fill(mm, b, ("mod", l, blk))

            def turn(name, src, ready):
                for t in range(T):
                    ready(t)
                    for half in range(2):
                        b = 4 * half + t % 2
                        ps = claim(b)
                        for j in range(4):
                            k = 4 * half + j
                            mm = pe.transpose(ps[:, P * j:P * j + P], src[:, t, P * k:P * k + P], ident[:, :])
                        fill(mm, b, (name, t, half))

            def turned(name, t):
                for half in range(2):
                    until_drained(pe, (name, t, half))

            def spread(name, need, banks=(1, 2)):
                pe.wait_ge(diag_ready, need)
                src = diag[name[0]]
                for half in range(2):
                    b = banks[half]
                    ps = claim(b)
                    mm = pe.matmul(ps[:, :], ones[:, :], src[:, 4 * half:4 * half + 4, :].rearrange("p a b -> p (a b)"),
                                   start=True, stop=True)
                    fill(mm, b, (name, half))

            def moe_spreads(l):
                spread(("s2", l), 4 * l + 2)
                spread(("sh2", l), 4 * l + 3, banks=(0, 3))
                spread(("g2", l), 4 * l + 4)

            pe.wait_ge(consts, CONSTS)
            pe.wait_ge(vectors_in, ROWS)
            ps = claim(4)
            for r, n in enumerate((120, 120, XT)):
                mm = pe.transpose(ps[:, P * r:P * r + n], rows[0:n, r, :], ident[0:n, 0:n])
            fill(mm, 4, "vecs")
            for a in range(ADA_FIRST):
                ada(a)

            def x_loaded(t):
                if t == 0:
                    pe.wait_ge(x_in, 16 * T)
            turn("hT0", X, x_loaded)
            for t in range(T):
                turned("hT0", t)
            pe.wait_ge(small_in, SMALL)
            ps = claim(6)
            for t in range(T):
                for k in range(KC):
                    mm = pe.matmul(ps[:, HEADS * t:HEADS * (t + 1)], HT[:, k, P * t:P * t + P], wdt[:, k, :],
                                   start=(k == 0), stop=(k == KC - 1))
            fill(mm, 6, "dt")
            at = 0
            nb = 0
            while items[at][0][0] != "w_out":
                kind = items[at][0]
                if kind[0] == "xbc":
                    w, tag = take(kind)
                    for j in range(4):
                        b = (0, 1, 2, 3)[nb % 4]
                        nb += 1
                        ps = claim(b)
                        for k in range(KC):
                            mm = pe.matmul(ps[:, :], w[:, k, P * j:P * j + P], HT[:, k, :],
                                           start=(k == 0), stop=(k == KC - 1))
                        fill(mm, b, ("xbc", 4 * kind[1] + j))
                        if j % 2:
                            for a in ada_beside(at, j // 2):
                                ada(a)
                    done_item(tag, ("xbc", 4 * kind[1] + 3))
                else:
                    w, tag = take(kind)
                    for t in range(T):
                        b = (0, 1, 2, 3)[nb % 4]
                        nb += 1
                        ps = claim(b)
                        for k in range(KC):
                            mm = pe.matmul(ps[:, :], HT[:, k, P * t:P * t + P], w[:, k, :],
                                           start=(k == 0), stop=(k == KC - 1))
                        fill(mm, b, ("z", kind[1], t))
                        if t % 2:
                            ada(ada_beside_z(kind[1], t // 2))
                    done_item(tag, ("z", kind[1], T - 1))
                at += 1

            pe.wait_ge(dA_ready, 1)
            pe.wait_ge(conv_done, CT)

            def tok(t):
                return slice(P * t, P * t + P)

            def scan_a(q):
                ch, g = divmod(q, GROUPS)
                if g == 0:
                    ps = claim(0)
                    for n, m in enumerate((upper, after, ones)):
                        mm = pe.matmul(ps[:, HEADS * n:HEADS * (n + 1)], m[:, :], dA[:, ch, :], start=True, stop=True)
                    fill(mm, 0, ("sums", ch))
                ps = claim(4)
                for j in range(4):
                    mm = pe.transpose(ps[:, P * j:P * j + P], xbcT[:, 4 * g + j, tok(ch)], ident[:, :])
                fill(mm, 4, ("xs", q))
                ps = claim(5)
                pe.transpose(ps[:, 0:P], xbcT[:, XT + g, tok(ch)], ident[:, :])
                mm = pe.matmul(ps[:, P:2 * P], xbcT[:, XT + g, tok(ch)], xbcT[:, XT + GROUPS + g, tok(ch)],
                               start=True, stop=True)
                fill(mm, 5, ("bc", q))
                for half in range(2):
                    pe.wait_ge(stepm_ready, 2 * q + half + 1)
                    ps = claim(1 + half)
                    for j in range(4):
                        mm = pe.matmul(ps[:, P * j:P * j + P], stepm[4 * half + j], upper[:, :], start=True, stop=True)
                    fill(mm, 1 + half, ("seg", q, half))

            def scan_b(q):
                ch, g = divmod(q, GROUPS)
                if ch:
                    until_drained(pe, ("st", q - GROUPS))
                    ps = claim(6)
                    mm = pe.matmul(ps[:, :], xbcT[:, XT + GROUPS + g, tok(ch)], state[:, g, :], start=True, stop=True)
                    fill(mm, 6, ("yoff", q))
                if ch < T - 1:
                    pe.wait_ge(xdte_ready, q + 1)
                    until_drained(pe, ("bc", q))
                    ps = claim(3)
                    mm = pe.matmul(ps[:, :], Btok[q % 2], xdte[q % 2], start=True, stop=True)
                    fill(mm, 3, ("st", q))
                pe.wait_ge(xdt_ready, q + 1)
                ps = claim(7)
                for h in range(GH):
                    if h % 4 == 0:
                        pe.wait_ge(mixm_ready, 2 * q + h // 4 + 1)
                    mm = pe.matmul(ps[:, HD * h:HD * h + HD], mixm[h // 4][:, P * (h % 4):P * (h % 4) + P],
                                   xdt[q % 2][:, HD * h:HD * h + HD], start=True, stop=True)
                fill(mm, 7, ("yd", q))

            def turn_y(ch):
                for g in range(GROUPS):
                    b = (0, 3, 4, 5)[g]
                    pe.wait_ge(yz_ready, GROUPS * ch + g + 1)
                    ps = claim(b)
                    for j in range(4):
                        k = 4 * g + j
                        mm = pe.transpose(ps[:, P * j:P * j + P], zs[:, ch, P * k:P * k + P], ident[:, :])
                    fill(mm, b, ("yT", ch, g))

            NQ = T * GROUPS
            scan_a(0)
            for q in range(NQ):
                if q + 1 < NQ:
                    scan_a(q + 1)
                scan_b(q)
                if q % GROUPS == 0 and q:
                    turn_y(q // GROUPS - 1)
            turn_y(T - 1)

            spread(("g1", 0), 1)
            for n in range(2):
                if n:
                    moe_spreads(0)
                w0, tag0 = take(("w_out", n, 0))
                w1, tag1 = take(("w_out", n, 1))
                for t in range(T):
                    if n == 0:
                        for g in range(GROUPS):
                            until_drained(pe, ("yT", t, g))
                    b = 4 + t
                    ps = claim(b)
                    for k in range(XT):
                        w = (w0, w1)[k // KC]
                        mm = pe.matmul(ps[:, :], xbcT[:, k, tok(t)], w[:, k % KC, :],
                                       start=(k == 0), stop=(k == XT - 1))
                    fill(mm, b, ("mix", 0, n, t))
                done_item(tag0, ("mix", 0, n, T - 1))
                done_item(tag1, ("mix", 0, n, T - 1))

            def experts(l):
                def ready(t):
                    pe.wait_ge(h2_ready, T * l + t + 1)
                turn(("h2T", l), H2, ready)
                if l:
                    pe.wait_ge(wr_in, 16)
                ps = claim(6)
                for t in range(T):
                    turned(("h2T", l), t)
                    for k in range(KC):
                        mm = pe.matmul(ps[:, E * t:E * t + E], HT[:, k, tok(t)], wr[:, k, :],
                                       start=(k == 0), stop=(k == KC - 1))
                fill(mm, 6, ("router", l))
                if l == 0:
                    done_item("wr0", ("router", 0))
                pe.wait_ge(shw_in, 48 * (l + 1))
                for n in range(2):
                    b = 1 + n
                    ps = claim(b)
                    w = shw[:, n, :].rearrange("p (k f) -> p k f", k=KC)
                    for k in range(KC):
                        mm = pe.matmul(ps[:, :], w[:, k, :], HT[:, k, :], start=(k == 0), stop=(k == KC - 1))
                    fill(mm, b, ("shared_in", l, n))
                pe.wait_ge(mask_ready, l + 1)
                ps = claim(7)
                for t in range(T):
                    for u in range(t + 1):
                        mm = pe.matmul(ps[:, E * t:E * t + E], (before_b if u == t else ones_b)[:, :], mask_b[:, u, :],
                                       start=(u == 0), stop=(u == t))
                for u in range(T):
                    mm = pe.matmul(ps[:, E * T:E * T + E], ones_b[:, :], mask_b[:, u, :], start=(u == 0), stop=(u == T - 1))
                fill(mm, 7, ("places", l))
                pe.wait_ge(sh_gated, l + 1)
                for t in range(T):
                    for n in range(2):
                        b = (0, 3)[n]
                        ps = claim(b)
                        mm = pe.matmul(ps[:, :], aS[0][:, tok(t)], shw[:, 2, 512 * n:512 * n + 512], start=True, stop=True)
                        fill(mm, b, ("shared", l, t, n))

                def table_part(n, ps, experts_):
                    for i in experts_:
                        e = SLOTS * n + i
                        pe.wait_ge(onehot_ready, E * l + e + 1)
                        for t in range(T):
                            mm = pe.matmul(ps[:, 3 * i:3 * i + 3], onehot[e % 4][:, t, :], V[:, t, e, :],
                                           start=(t == 0), stop=(t == T - 1))
                        if i < SLOTS - 1:
                            mm.then_inc(onehot_used, 1)
                    return mm
                fill(table_part(0, claim(4), range(SLOTS)), 4, ("table", l))

                base = list(uses)
                ebase = E * l

                def rows_in(g, u):
                    i = SLOTS * g + u
                    pe.wait_ge(xg_in[u % 4], 16 * (2 * g + u // 4 + 1 + ebase // 4))
                    for half in range(2):
                        b = 4 * half
                        pe.wait_ge(drained[b], base[b] + i)
                        for j in range(4):
                            k = 4 * half + j
                            mm = pe.transpose(psum[:, b, P * j:P * j + P], xg[u % 4][:, P * k:P * k + P], ident[:, :])
                        mm.then_inc(filled[b], 1)

                def up(g, u, first=False):
                    i = SLOTS * g + u
                    pe.wait_ge(exp_in[u], 48 * (g + 1 + l * (E // SLOTS)))
                    pe.wait_ge(drained[0], base[0] + i + 1)
                    pe.wait_ge(drained[4], base[4] + i + 1)
                    for n in range(2):
                        b = 1 + 4 * n + u % 2
                        pe.wait_ge(drained[b], base[b] + 4 * g + u // 2 + tables_before(b, u, first))
                        w = exp_w[u][:, n, :].rearrange("p (k f) -> p k f", k=KC)
                        for k in range(KC):
                            mm = pe.matmul(psum[:, b, 0:P], w[:, k, :], xeT[u % 2][:, k, :],
                                           start=(k == 0), stop=(k == KC - 1))
                        mm.then_inc(filled[b], 1)

                def down(g, u, first=False):
                    i = SLOTS * g + u
                    b = 5 + u % 2
                    pe.wait_ge(drained[b], base[b] + 4 * g + u // 2 + 1 + tables_before(b, u, first))
                    for n in range(2):
                        b = 3 + 4 * n
                        pe.wait_ge(drained[b], base[b] + i)
                        mm = pe.matmul(psum[:, b, :], aT[u % 2], exp_w[u][:, 2, 512 * n:512 * n + 512],
                                       start=True, stop=True)
                        mm.then_inc(filled[b], 1)

                def group(g, first=False, last=False, after_first=False):
                    for u in range(SLOTS):
                        if not (last and u == SLOTS - 1):
                            rows_in(*((g, u + 1) if u + 1 < SLOTS else (g + 1, 0)))
                        table = first and u + 1 < NG
                        if table:
                            b = table_bank(u)
                            pe.wait_ge(drained[b], base[b] + u)
                            table_part(u + 1, psum[:, b, :], range(SLOTS // 2))
                        up(g, u, first)
                        if table:
                            table_part(u + 1, psum[:, b, :], range(SLOTS // 2, SLOTS)).then_inc(filled[b], 1)
                        if u:
                            down(g, u - 1, first)
                        elif not first:
                            down(g - 1, SLOTS - 1)
                NG = E // SLOTS
                rows_in(0, 0)
                group(0, first=True)
                with pe.Fori(1, NG - 1) as g:
                    group(g)
                group(NG - 1, last=True)
                down(NG - 1, SLOTS - 1)

                def more_blocks(stage):
                    done = more[l]
                    if stage == 0:
                        for b in range(8):
                            n = E if b in (0, 4, 3, 7) else E // 2
                            pe.wait_ge(drained[b], base[b] + n + tables_before(b, 0, False))

                    def unit(i):
                        pe.wait_ge(done["onehot"], i + 1)
                        for t in range(T):
                            mm = pe.matmul(psum[:, 6, 0:3], onehot[0][:, t, :], V1[:, t, 0:3], start=(t == 0), stop=(t == T - 1))
                        mm.then_inc(done["dest"], 1)
                        pe.wait_ge(done["rows"], 16 * i + 16)
                        for k in range(KC):
                            mm = pe.transpose(psum[:, k // 4, P * (k % 4):P * (k % 4) + P], xg[0][:, P * k:P * k + P], ident[:, :])
                        mm.then_inc(done["turned"], 1)
                        pe.wait_ge(done["moved"], 2 * i + 2)
                        pe.wait_ge(done["weights"], 48 * i + 48)
                        for n in range(2):
                            w = exp_w[0][:, n, :].rearrange("p (k f) -> p k f", k=KC)
                            for k in range(KC):
                                mm = pe.matmul(psum[:, 2 + n, 0:P], w[:, k, :], xeT[0][:, k, :],
                                               start=(k == 0), stop=(k == KC - 1))
                        mm.then_inc(done["up"], 1)
                        pe.wait_ge(done["gated"], i + 1)
                        for n in range(2):
                            mm = pe.matmul(psum[:, 4 + n, :], aT[0], exp_w[0][:, 2, 512 * n:512 * n + 512], start=True, stop=True)
                        mm.then_inc(done["down"], 1)
                    for b, j0, j1, before in MORE[stage]:
                        with pe.Fori(j0, j1) as j:
                            unit(before + j)
                    pe.wait_ge(done["yrow"], 2 * MORE_UNITS[stage])
                when_more(pe, l, more_blocks)
                MARK[("loop", l)] = list(base)
                for b in (0, 4, 3, 7):
                    uses[b] += E
                for b in (1, 2, 5, 6):
                    uses[b] += E // 2
                for u in range(NG - 1):
                    uses[table_bank(u)] += 1

            experts(0)

            def attention():
                def ready(t):
                    pe.wait_ge(x_ready, T + t + 1)
                turn("uT", X, ready)
                for t in range(T):
                    turned("uT", t)
                ps = claim(6)
                for t in range(T):
                    for k in range(KC):
                        mm = pe.matmul(ps[:, AH * t:AH * (t + 1)], HT[:, k, tok(t)], wf[:, k, :],
                                       start=(k == 0), stop=(k == KC - 1))
                fill(mm, 6, "forget")
                nb = 0
                for n in range(2):
                    w, tag = take(("kvw", n))
                    for j in range(4):
                        b = (0, 1, 2, 3)[nb % 4]
                        nb += 1
                        ps = claim(b)
                        for k in range(KC):
                            mm = pe.matmul(ps[:, :], w[:, k, P * j:P * j + P], HT[:, k, :],
                                           start=(k == 0), stop=(k == KC - 1))
                        fill(mm, b, ("kT", 4 * n + j))
                    done_item(tag, ("kT", 4 * n + 3))
                pe.wait_ge(logf_ready, 1)
                ps = claim(7)
                lf = logf
                for t in range(T):
                    for u in range(t + 1):
                        mm = pe.matmul(ps[:, AH * t:AH * (t + 1)], (upper if u == t else ones)[:, :], lf[:, u, :],
                                       start=(u == 0), stop=(u == t))
                fill(mm, 7, "cumf")
                for n in range(2):
                    w, tag = take(("kvw", 2 + n))
                    for t in range(T):
                        b = (0, 1, 2, 3)[nb % 4]
                        nb += 1
                        ps = claim(b)
                        for k in range(KC):
                            mm = pe.matmul(ps[:, :], HT[:, k, tok(t)], w[:, k, :], start=(k == 0), stop=(k == KC - 1))
                        fill(mm, b, ("v", n, t))
                    done_item(tag, ("v", n, T - 1))
                until_drained(pe, "cumf")
                ps = claim(7)
                mm = pe.transpose(ps[0:T * AH, 0:P], cumf[:, :, :].rearrange("p a b -> p (a b)"), ident[:, :])
                fill(mm, 7, "cumfT")
                turn("qhT", X, lambda t: None)
                for t in range(T):
                    turned("qhT", t)
                for n in range(2):
                    w, tag = take(("wq", n))
                    for j in range(4):
                        b = (0, 1, 2, 3)[nb % 4]
                        nb += 1
                        ps = claim(b)
                        for k in range(KC):
                            mm = pe.matmul(ps[:, :], w[:, k, P * j:P * j + P], HT[:, k, :],
                                           start=(k == 0), stop=(k == KC - 1))
                        fill(mm, b, ("qT", 4 * n + j))
                    done_item(tag, ("qT", 4 * n + 3))
                until_drained(pe, "cumfT")
                for j in range(KC):
                    until_drained(pe, ("qT", j))
                    until_drained(pe, ("kT", j))
                for n in range(2):
                    for t in range(T):
                        until_drained(pe, ("v", n, t))

                def scores_of(n):
                    h, i = divmod(n, T)
                    if i == 0:
                        ps = claim(h % 2)
                        for t in range(T):
                            r = AH * t + h
                            mm = pe.matmul(ps[:, tok(t)], ident[:, r:r + 1].to_broadcast([P, P]),
                                           cumfT[:, :], start=True, stop=True)
                        fill(mm, h % 2, ("ncf", h))
                    ps = claim(2 + n % 2)
                    nk = P * (i + 1)
                    mm = pe.matmul(ps[:, 0:nk], qT[h % 2][:, h // 2, tok(i)], kT[:, h // 2, 0:nk],
                                   start=True, stop=True)
                    fill(mm, 2 + n % 2, ("qk", n))

                def turn_probs(n):
                    h, i = divmod(n, T)
                    pe.wait_ge(prob_ready, n + 1)
                    ps = claim(4 + n % 2)
                    for j in range(i + 1):
                        mm = pe.transpose(ps[:, tok(j)], prob[n % 3][:, tok(j)], ident[:, :])
                    fill(mm, 4 + n % 2, ("pT", n))

                def weigh(n):
                    h, i = divmod(n, T)
                    until_drained(pe, ("pT", n))
                    b = 6 + h % 2
                    if i == 0:
                        claim(b)
                    ps = psum[:, b, :]
                    for j in range(i + 1):
                        pair = slice(P * (h // 2), P * (h // 2) + P)
                        mm = pe.matmul(ps[:, tok(i)], probT[n % 2][:, j, :], vtok[:, j, pair],
                                       start=(j == 0), stop=(j == i))
                    if i == T - 1:
                        fill(mm, b, ("o", h))

                NU = AH * T
                scores_of(0)
                scores_of(1)
                for n in range(NU):
                    if n + 2 < NU:
                        scores_of(n + 2)
                    turn_probs(n)
                    if n:
                        weigh(n - 1)
                weigh(NU - 1)

                def o_ready(t):
                    if t == 0:
                        until_drained(pe, ("o", AH - 1))
                        until_drained(pe, ("o", AH - 2))
                turn("oT", otok, o_ready)
                for n in range(2):
                    if n:
                        spread(("g1", 1), 5)
                        moe_spreads(1)
                    w, tag = take(("wo", n))
                    for t in range(T):
                        turned("oT", t)
                        b = 4 + t
                        ps = claim(b)
                        for k in range(KC):
                            mm = pe.matmul(ps[:, :], HT[:, k, tok(t)], w[:, k, :], start=(k == 0), stop=(k == KC - 1))
                        fill(mm, b, ("mix", 1, n, t))
                    done_item(tag, ("mix", 1, n, T - 1))

            attention()
            experts(1)


        @block.scalar
        def _(act):
            def move(key, dst, func=ACT.Copy, **kw):
                ps = until_filled(act, key)
                act.activation(dst, ps, func, **kw).then_inc(drained[MARK[key][0]], 1)

            def move_turned(name, half, dst):
                for t in range(T):
                    ps = until_filled(act, (name, t, half))
                    act.activation(dst[:, 4 * half:4 * half + 4, TILES[t]], ps.rearrange("p (a b) -> p a b", a=4),
                                   ACT.Copy).then_inc(drained[MARK[(name, t, half)][0]], 1)

            def move_modulated(name, half, dst, scale, shift):
                for t in range(T):
                    ps = until_filled(act, (name, t, half))
                    for j in range(4):
                        k = 4 * half + j
                        ins = act.activation(dst[:, k, TILES[t]], ps[:, P * j:P * j + P], ACT.Identity,
                                             scale=mod[:, scale + k:scale + k + 1], bias=mod[:, shift + k:shift + k + 1])
                    ins.then_inc(drained[MARK[(name, t, half)][0]], 1)

            def until_mod(l, v):
                until_drained(act, ("mod", l, (8 * v) // 4))
                until_drained(act, ("mod", l, (8 * v) // 4 + 1))

            def move_spread(name, dst):
                for half in range(2):
                    move((name, half), dst[:, 512 * half:512 * half + 512])

            soft = [0]

            def softplus_act(x, n, x_done):
                x_done()
                act.activation(sp[0][:, 0:n], x, ACT.Abs).then_inc(soft_act, 1)
                soft[0] += 1
                act.wait_ge(soft_act, soft[0])
                act.activation(sp[0][:, 0:n], sp[0][:, 0:n], ACT.Exp, scale=-1.0).then_inc(soft_act, 1)
                soft[0] += 1

            def softplus_ln(n, m):
                act.wait_ge(soft_dve, m)
                act.activation(sp[2][:, 0:n], sp[1][:, 0:n], ACT.Ln).then_inc(soft_act, 1)
                soft[0] += 1

            def ada_scale(a):
                w = ada_pool[a // 2 % 2]
                act.wait_ge(ada_pool_in[a // 2 % 2], 16 * (a // 4 + 1))
                for k in range(KC):
                    ins = act.activation(w[:, k, :], w[:, k, :], ACT.Copy, scale=condT[:, k:k + 1])
                ins.then_inc(ada_scaled, 1)

            until_drained(act, "vecs")
            act.activation(condT[:, :], c_col, ACT.Silu).then_inc(cond_ready, 1)
            act.wait_ge(cond_ready, 1)
            for a in range(1, ADA_FIRST, 2):
                ada_scale(a)
            for v in (SHIFT1, SCALE1):
                until_mod(0, v)
            move_modulated("hT0", 0, HT, MODC[(0, SCALE1)], MODC[(0, SHIFT1)])
            act.wait_ge(small_in, SMALL)
            act.activation(negA[:, :], alog_bc, ACT.Exp).then_inc(soft_act, 1)
            soft[0] += 1
            softplus_act(dtx[:, :, :].rearrange("p a b -> p (a b)"), P, lambda: until_drained(act, "dt"))
            softplus_ln(P, 1)
            waiting = []

            def finish_conv():
                if waiting:
                    j, n = waiting.pop()
                    until_drained(act, ("xbc", j))
                    act.activation(xbcT[:, j, :], conv_acc[n % 2], ACT.Silu).then_inc(conv_done, 1)
            n = 0
            for key in stream_order():
                if key[0] == "xbc":
                    for j in range(4 * key[1], 4 * key[1] + 4):
                        if n % 2 == 0:
                            for a in ada_beside(n // 4, n % 4 // 2)[1:]:
                                ada_scale(a)
                        ps = until_filled(act, ("xbc", j))
                        if n >= 2:
                            act.wait_ge(conv_done, n - 1)
                        act.activation(conv_acc[n % 2], ps, ACT.Identity, scale=convw[:, CONV - 1, j:j + 1],
                                       bias=convb[:, j:j + 1]).then_inc(acc_ready, 1)
                        finish_conv()
                        waiting.append((j, n))
                        n += 1
                elif key[0] == "z":
                    finish_conv()
                    if key[1] == 0:
                        act.wait_ge(ada_summed[1], ADA_OF[1])
                    for t in range(T):
                        move(("z", key[1], t), zs[:, t, 512 * key[1]:512 * key[1] + 512], ACT.Silu)

            act.wait_ge(dA_ready, 1)
            act.wait_ge(ada_summed[0], ADA_OF[0])

            def segments(q, half):
                ch, g = divmod(q, GROUPS)
                for j in range(4):
                    h = GH * g + 4 * half + j
                    ins = act.activation(stepm[4 * half + j], after[:, :], ACT.Copy, scale=dA[:, ch, h:h + 1])
                ins.then_inc(stepm_ready, 1)

            def scan_exps(q):
                ch, g = divmod(q, GROUPS)
                if g == 0:
                    if ch >= 2:
                        act.wait_ge(yz_ready, GROUPS * (ch - 1))
                    ps = until_filled(act, ("sums", ch))
                    act.activation(exps[ch % 2][:, :], ps[:, 0:96], ACT.Exp).then_inc(drained[0], 1)
                for half in range(2):
                    ps = until_filled(act, ("seg", q, half))
                    if q + 1 < NQ:
                        segments(q + 1, half)
                    if q:
                        act.wait_ge(mixm_ready, 2 * (q - 1) + half + 1)
                    act.activation(decay[half], ps, ACT.Exp).then_inc(drained[1 + half], 1)

            def square(q):
                ch, g = divmod(q, GROUPS)
                act.wait_ge(yz_ready, q + 1)
                if q:
                    act.wait_ge(squared, q)
                act.activation(view(139, GW), zs[:, ch, GW * g:GW * g + GW], ACT.Square,
                               accum_out=ssq[:, ch, g:g + 1]).then_inc(squared, 1)

            def move_y(ch):
                for g in range(2):
                    ps = until_filled(act, ("yT", ch, g))
                    for j in range(4):
                        k = 4 * g + j
                        ins = act.activation(xbcT[:, k, TILES[ch]], ps[:, P * j:P * j + P], ACT.Copy,
                                             scale=normw[:, k:k + 1])
                    ins.then_inc(drained[MARK[("yT", ch, g)][0]], 1)
            for half in range(2):
                segments(0, half)
            scan_exps(0)
            for q in range(NQ):
                if q + 1 < NQ:
                    scan_exps(q + 1)
                if q:
                    square(q - 1)
                if q % GROUPS == 0 and q:
                    move_y(q // GROUPS - 1)
            square(NQ - 1)
            move_y(T - 1)

            act.wait_ge(var_ready, 1)
            act.activation(sd[:, :], sd[:, :], ACT.Sqrt).then_inc(sd_ready, 1)
            act.wait_ge(squared, NQ)
            move_spread(("g1", 0), g1bc)

            def root(k, t):
                act.wait_ge(var_ready, 2 + T * k + t)
                act.activation(sd[:, t:t + 1], sd[:, t:t + 1], ACT.Sqrt).then_inc(sd_ready, 1)

            def roots(k):
                for t in range(T):
                    root(k, t)

            def moe_spreads(l):
                move_spread(("s2", l), s2bc)
                move_spread(("sh2", l), sh2bc)
                move_spread(("g2", l), g2bc)
            moe_spreads(0)
            roots(0)

            def experts(l):
                for t in range(T):
                    act.wait_ge(h2_scaled, T * l + t + 1)
                    act.activation(X[:, t, :], X[:, t, :], ACT.Copy, scale=ALPHA).then_inc(x_scaled, 1)
                move_turned(("h2T", l), 0, HT)
                ps = until_filled(act, ("router", l))
                act.activation(scores[:, :, :].rearrange("p a b -> p (a b)"), ps[:, 0:T * E], ACT.Sigmoid).then_inc(drained[6], 1)
                move(("shared_in", l, 0), aS[0], ACT.Silu)
                move(("shared_in", l, 1), aS[1])
                for t in range(T):
                    for n in range(2):
                        move(("shared", l, t, n), SH[:, t, 512 * n:512 * n + 512])
                base = MARK[("loop", l)]

                def rows_in(g, u):
                    for half in range(2):
                        b = 4 * half
                        act.wait_ge(filled[b], base[b] + SLOTS * g + u + 1)
                        act.activation(xeT[u % 2][:, 4 * half:4 * half + 4, :],
                                       psum[:, b, :].rearrange("p (a b) -> p a b", a=4), ACT.Copy).then_inc(drained[b], 1)

                def silu(g, u):
                    b = 1 + u % 2
                    act.wait_ge(filled[b], base[b] + 4 * g + u // 2 + 1)
                    act.activation(s1[u % 2], psum[:, b, 0:P], ACT.Silu).then_inc(drained[b], 1)

                def group(g, last=False):
                    for u in range(SLOTS):
                        if not (last and u == SLOTS - 1):
                            rows_in(*((g, u + 1) if u + 1 < SLOTS else (g + 1, 0)))
                        silu(g, u)
                rows_in(0, 0)
                group(0)
                with act.Fori(1, NG - 1) as g:
                    group(g)
                group(NG - 1, last=True)

                def more_blocks(stage):
                    done = more[l]

                    def unit(i):
                        act.wait_ge(done["turned"], i + 1)
                        for half in range(2):
                            act.activation(xeT[0][:, 4 * half:4 * half + 4, :],
                                           psum[:, half, :].rearrange("p (a b) -> p a b", a=4),
                                           ACT.Copy).then_inc(done["moved"], 1)
                        act.wait_ge(done["up"], i + 1)
                        act.activation(s1[0], psum[:, 2, 0:P], ACT.Silu).then_inc(done["silu"], 1)
                    for b, j0, j1, before in MORE[stage]:
                        with act.Fori(j0, j1) as j:
                            unit(before + j)
                when_more(act, l, more_blocks)
                for j in range(2 * T):
                    t = j // 2
                    act.wait_ge(part_in[j % 3], 16 * (j // 3 + 1 + PARTS_OF[j % 3] * l))
                    for i in range(DVE_ROWS, TOPK):
                        row = part[j % 3][:, i, :]
                        ins = act.activation(row, row, ACT.Copy, scale=gk[:, t, i:i + 1])
                    ins.then_inc(part_scaled, 1)
                    if j % 2 and t:
                        root(2 * l + 1, t - 1)
                root(2 * l + 1, T - 1)

            def attention():
                for v in (0, 1):
                    until_mod("kv", v)
                move_modulated("uT", 0, HT, MODC[("kv", 1)], MODC[("kv", 0)])
                softplus_act(dts[:, 0:2, :].rearrange("p a b -> p (a b)"), T * AH, lambda: act.wait_ge(soft_dve, 9))
                for j in range(0, KC, 2):
                    move(("kT", j), kT[:, j, :])
                    if j == 0:
                        softplus_ln(T * AH, 10)
                for n in range(2):
                    for t in range(0, T, 2):
                        move(("v", n, t), vtok[:, t, 512 * n:512 * n + 512])
                for v in (SHIFT1, SCALE1):
                    until_mod(1, v)
                move_modulated("qhT", 0, HT, MODC[(1, SCALE1)], MODC[(1, SHIFT1)])
                act.wait_ge(q_zeros, 3)
                for j in range(0, KC, 2):
                    ps = until_filled(act, ("qT", j))
                    act.activation(qT[0][0:HD, j, :], ps[0:HD, :], ACT.Copy)
                    act.activation(qT[1][HD:P, j, :], ps[HD:P, :], ACT.Copy).then_inc(drained[MARK[("qT", j)][0]], 1)
                until_drained(act, "cumf")

                def scaled(n):
                    h, i = divmod(n, T)
                    if n >= 3:
                        act.wait_ge(max_ready, n - 2)
                    ps = until_filled(act, ("qk", n))
                    act.activation(logit[n % 3][:, 0:P * (i + 1)], ps[:, 0:P * (i + 1)], ACT.Identity, scale=ASCALE,
                                   bias=cumf[:, i, h:h + 1]).then_inc(drained[MARK[("qk", n)][0]], 1)

                def soften(n):
                    h, i = divmod(n, T)
                    act.wait_ge(max_ready, n + 1)
                    if n >= 3:
                        until_filled(act, ("pT", n - 3))
                    if i == 0 and h >= 2:
                        until_drained(act, ("o", h - 2))
                    nk = P * (i + 1)
                    act.activation(prob[n % 3][:, 0:nk], shifted[n % 3][:, 0:nk], ACT.Exp, bias=mx[:, 4 + n % 4:5 + n % 4],
                                   accum_out=rsum[:, h % 2, i:i + 1]).then_inc(prob_ready, 1)
                NU = AH * T
                scaled(0)
                scaled(1)
                for n in range(NU):
                    soften(n)
                    if n + 2 < NU:
                        scaled(n + 2)
                move_turned("oT", 0, HT)
                move_spread(("g1", 1), g1bc)
                moe_spreads(1)
                roots(2)

            experts(0)
            attention()
            experts(1)

        @block.vector
        def _(dve):
            steps = [0]

            def step(ins):
                ins.then_inc(dve_step, 1)
                steps[0] += 1

            def settle():
                dve.wait_ge(dve_step, steps[0])

            def move(key, dst):
                ps = until_filled(dve, key)
                dve.tensor_copy(dst, ps).then_inc(drained[MARK[key][0]], 1)

            def move_turned(name, half, dst):
                for t in range(T):
                    ps = until_filled(dve, (name, t, half))
                    dve.tensor_copy(dst[:, 4 * half:4 * half + 4, TILES[t]],
                                    ps.rearrange("p (a b) -> p a b", a=4)).then_inc(drained[MARK[(name, t, half)][0]], 1)

            def move_modulated(name, half, dst, scale, shift):
                for t in range(T):
                    ps = until_filled(dve, (name, t, half))
                    for j in range(4):
                        k = 4 * half + j
                        ins = dve.tensor_scalar(dst[:, k, TILES[t]], ps[:, P * j:P * j + P],
                                                mod[:, scale + k:scale + k + 1], mod[:, shift + k:shift + k + 1],
                                                ALU.mult, ALU.add)
                    ins.then_inc(drained[MARK[(name, t, half)][0]], 1)

            def ada_sum(a):
                n = ada_count(a)
                if n:
                    before = a - 2 if a <= ADA_PAIRED else a - 1
                    until_filled(dve, ("mod",) + ada_blocks[before])
                dve.wait_ge(ada_dve_in[0], 16 * (n + 1))
                step(dve.tensor_scalar(ada_acc[0], ada_dve[:, 0, :], condT[:, 0:1], None, ALU.mult))
                for k in range(1, KC):
                    if k == KC // 2:
                        dve.wait_ge(ada_half, n + 1)
                        dve.wait_ge(ada_dve_in[1], 16 * (n + 1))
                    else:
                        settle()
                    ins = dve.scalar_tensor_tensor(ada_acc[0], ada_dve[:, k, :], condT[:, k:k + 1], ada_acc[0],
                                                   ALU.mult, ALU.add)
                    if k == KC // 2 - 1:
                        ins.then_inc(ada_half, 1)
                    elif k < KC - 1:
                        step(ins)
                ins.then_inc(ada_summed[0], 1)

            def ada(l, blk):
                ps = until_filled(dve, ("mod", l, blk))
                at = {0: 0, 1: 48, "kv": 96}[l] + 4 * blk
                add1 = 1.0 if (blk // 2 in (1, 2, 4, 5)) else 0.0
                dve.scalar_tensor_tensor(mod[:, at:at + 4], ps[:, 0:4], add1, modb[:, at:at + 4], ALU.add,
                                         ALU.add).then_inc(drained[MARK[("mod", l, blk)][0]], 1)

            def until_mod(l, v):
                until_drained(dve, ("mod", l, 2 * v))
                until_drained(dve, ("mod", l, 2 * v + 1))

            def diagonals(l):
                for name, v in (("g1", GATE1), ("s2", SCALE2), ("sh2", SHIFT2), ("g2", GATE2)):
                    until_mod(l, v)
                    for k in range(KC):
                        col = MODC[(l, v)] + k
                        ins = dve.tensor_scalar(diag[name][:, k, :], ident[:, :], mod[:, col:col + 1], None, ALU.mult)
                    ins.then_inc(diag_ready, 1)

            def soft(ins):
                ins.then_inc(soft_dve, 1)
                softs[0] += 1

            softs = [0]

            def softplus(x, out, n, act0):
                t_, u_, l_, m_ = (sp[i][:, 0:n] for i in range(4))
                dve.wait_ge(soft_act, act0 + 2)
                soft(dve.tensor_scalar(u_, t_, 1.0, None, ALU.add))
                dve.wait_ge(soft_act, act0 + 3)

                def then(ins):
                    soft(ins)
                    dve.wait_ge(soft_dve, softs[0])
                then(dve.tensor_scalar(u_, u_, -1.0, None, ALU.add))
                then(dve.tensor_scalar(m_, u_, 0.0, None, ALU.is_equal))
                then(dve.tensor_tensor(u_, u_, m_, ALU.add))
                then(dve.tensor_tensor(l_, l_, m_, ALU.add))
                then(dve.reciprocal(u_, u_))
                then(dve.tensor_tensor(l_, l_, u_, ALU.mult))
                then(dve.tensor_tensor(l_, l_, t_, ALU.mult))
                step(dve.scalar_tensor_tensor(out, x, 0.0, l_, ALU.max, ALU.add))
                settle()

            ps = until_filled(dve, "vecs")
            for r, n in enumerate((120, 120, XT)):
                ins = dve.tensor_copy(cols[:, r, 0:n], ps[:, P * r:P * r + n])
            ins.then_inc(drained[4], 1)
            until_drained(dve, "vecs")
            dve.wait_ge(cond_ready, 1)
            for a in range(0, ADA_FIRST, 2):
                ada_sum(a)
                for i in (a, a + 1):
                    ada(*ada_blocks[i])
            until_mod(0, SHIFT1)
            until_mod(0, SCALE1)
            move_modulated("hT0", 1, HT, MODC[(0, SCALE1)], MODC[(0, SHIFT1)])
            dve.wait_ge(small_in, SMALL)
            ps = until_filled(dve, "dt")
            dve.tensor_tensor(dtx[:, :, :], ps[:, 0:P].rearrange("p (a b) -> p a b", a=T),
                              dtb_bc.unsqueeze(1).to_broadcast([P, T, HEADS]), ALU.add).then_inc(drained[6], 1)
            until_drained(dve, "dt")
            softplus(dtx[:, :, :].rearrange("p a b -> p (a b)"), dts[:, :, :].rearrange("p a b -> p (a b)"), P, 1)
            step(dve.tensor_scalar(negA[:, :], negA[:, :], -1.0, None, ALU.mult))
            settle()
            dve.tensor_tensor(dA[:, :, :], dts[:, :, :], negA[:, :].unsqueeze(1).to_broadcast([P, T, HEADS]),
                              ALU.mult).then_inc(dA_ready, 1)

            n = 0
            for key in stream_order():
                if key[0] == "xbc":
                    for j in range(4 * key[1], 4 * key[1] + 4):
                        if n % 2 == 0:
                            for a in ada_beside(n // 4, n % 4 // 2)[0:1]:
                                ada_sum(a)
                        ps = until_filled(dve, ("xbc", j))
                        dve.wait_ge(acc_ready, n + 1)
                        for s in range(1, CONV):
                            ins = dve.scalar_tensor_tensor(conv_acc[n % 2][:, s:S], ps[:, 0:S - s],
                                                           convw[:, CONV - 1 - s, j:j + 1], conv_acc[n % 2][:, s:S],
                                                           ALU.mult, ALU.add)
                            if s < CONV - 1:
                                step(ins)
                                settle()
                        ins.then_inc(drained[MARK[("xbc", j)][0]], 1)
                        if n % 2:
                            for a in ada_beside(n // 4, n % 4 // 2):
                                ada(*ada_blocks[a])
                        n += 1
                else:
                    for half in range(2):
                        a = ada_beside_z(key[1], half)
                        ada_sum(a)
                        ada(*ada_blocks[a])

            dve.wait_ge(conv_done, CT)

            def heads(v):
                return v.rearrange("p (h d) -> p h d", h=GH)

            def bch(v):
                return v.unsqueeze(2).to_broadcast([P, GH, HD])

            def scan_a(q):
                ch, g = divmod(q, GROUPS)
                hs = slice(GH * g, GH * g + GH)
                ps = until_filled(dve, ("xs", q))
                if q >= 2:
                    dve.wait_ge(xdte_ready, min(q - 1, NQ - GROUPS))
                    until_drained(dve, ("yd", q - 2))
                dve.tensor_tensor(heads(xdt[q % 2]), heads(ps), bch(dts[:, ch, hs]), ALU.mult).then_inc(xdt_ready, 1)
                dve.tensor_tensor(heads(xsD[q % 2]), heads(ps), bch(dsk_bc[:, hs]), ALU.mult).then_inc(drained[4], 1)
                ps = until_filled(dve, ("bc", q))
                dve.tensor_copy(Btok[q % 2], ps[:, 0:P])
                dve.tensor_tensor(CBm[q % 2], ps[:, P:2 * P], upper[:, :], ALU.mult).then_inc(drained[5], 1)

            def scan_g(q):
                until_drained(dve, ("bc", q))
                for half in range(2):
                    until_drained(dve, ("seg", q, half))
                    if q:
                        until_filled(dve, ("yd", q - 1))
                    dve.tensor_tensor(mixm[half].rearrange("p (h l) -> p h l", h=4),
                                      decay[half].rearrange("p (h l) -> p h l", h=4),
                                      CBm[q % 2].unsqueeze(1).to_broadcast([P, 4, P]), ALU.mult).then_inc(mixm_ready, 1)

            def scan_b(q):
                ch, g = divmod(q, GROUPS)
                hs = slice(GH * g, GH * g + GH)
                if q >= 2:
                    dve.wait_ge(yz_ready, q - 1)
                if ch:
                    ps = until_filled(dve, ("yoff", q))
                    until_drained(dve, ("sums", ch))
                    dve.tensor_tensor(heads(yoff[q % 2]), heads(ps), bch(exps[ch % 2][:, hs]), ALU.mult).then_inc(drained[6], 1)
                if ch < T - 1:
                    ps = until_filled(dve, ("st", q))
                    if ch:
                        dve.wait_ge(state_scaled, q - GROUPS + 1)
                        dve.tensor_tensor(state[:, g, :], state[:, g, :], ps, ALU.add).then_inc(drained[3], 1)
                    else:
                        dve.tensor_copy(state[:, g, :], ps).then_inc(drained[3], 1)
                ps = until_filled(dve, ("yd", q))
                until_drained(dve, ("xs", q))
                dve.tensor_tensor(yg[q % 2], ps, xsD[q % 2], ALU.add).then_inc(drained[7], 1)

            def move_y(ch):
                for g in range(2, 4):
                    ps = until_filled(dve, ("yT", ch, g))
                    for j in range(4):
                        k = 4 * g + j
                        ins = dve.tensor_scalar(xbcT[:, k, TILES[ch]], ps[:, P * j:P * j + P], normw[:, k:k + 1], None,
                                                ALU.mult)
                    ins.then_inc(drained[MARK[("yT", ch, g)][0]], 1)
            scan_a(0)
            for q in range(NQ):
                scan_g(q)
                if q + 1 < NQ:
                    scan_a(q + 1)
                scan_b(q)
                if q % GROUPS == 0 and q:
                    move_y(q // GROUPS - 1)
            dve.wait_ge(squared, NQ)
            step(dve.tensor_reduce(ssum[:, :], ssq[:, :, :], AX, ALU.add))
            settle()
            dve.tensor_scalar(sd[:, :], ssum[:, :], 1.0 / DI, EPS, ALU.mult, ALU.add).then_inc(var_ready, 1)
            diagonals(0)
            move_y(T - 1)
            dve.wait_ge(sd_ready, 1)
            step(dve.reciprocal(rsy[:, :], sd[:, :]))
            settle()

            def statistics(k, t, R):
                settle()
                for n in range(2):
                    ins = dve.bn_stats(bn[:, t, n, :], R[:, t, 512 * n:512 * n + 512])
                step(ins)
                settle()
                step(dve.bn_aggr(mv[:, t, :], bn[:, t, :, :]))
                settle()
                dve.tensor_scalar(sd[:, t:t + 1], mv[:, t, 1:2], EPS, None, ALU.add).then_inc(var_ready, 1)

            def normalise(k, t, R, lnrow):
                dve.wait_ge(sd_ready, 2 + T * k + t)
                step(dve.reciprocal(rstd[:, t:t + 1], sd[:, t:t + 1]))
                settle()
                step(dve.tensor_scalar(X[:, t, :], R[:, t, :], mv[:, t, 0:1], rstd[:, t:t + 1], ALU.subtract, ALU.mult))
                settle()
                if t == 0:
                    dve.wait_ge(lnrow_in, 32 * (k + 1))
                dve.tensor_tensor(X[:, t, :], X[:, t, :], lnrow[0], ALU.mult).then_inc(ln_scaled, 1)

            def mixed(l, R):
                for half in range(2):
                    until_drained(dve, ((("g1", l), half)))
                k = 2 * l
                for n in range(2):
                    for t in range(T):
                        r = R[:, t, 512 * n:512 * n + 512]
                        ps = until_filled(dve, ("mix", l, n, t))
                        gb = g1bc[:, 512 * n:512 * n + 512]
                        if l == 0:
                            ins = dve.scalar_tensor_tensor(r, ps, rsy[:, t:t + 1], gb, ALU.mult, ALU.mult)
                        else:
                            ins = dve.tensor_tensor(r, ps, gb, ALU.mult)
                        ins.then_inc(drained[MARK[("mix", l, n, t)][0]], 1)
                        until_drained(dve, ("mix", l, n, t))
                        step(dve.scalar_tensor_tensor(r, X[:, t, 512 * n:512 * n + 512], ALPHA, r, ALU.mult, ALU.add))
                        if n:
                            statistics(k, t, R)
                            if t:
                                normalise(k, t - 1, R, lnrow_mix)
                normalise(k, T - 1, R, lnrow_mix)
            mixed(0, Rmix[0])

            def experts(l):
                for half in range(2):
                    until_drained(dve, (("s2", l), half))
                for t in range(T):
                    dve.wait_ge(x_ready, T * 2 * l + t + 1)
                    dve.tensor_tensor(H2[:, t, :], X[:, t, :], s2bc, ALU.mult).then_inc(h2_scaled, 1)
                move_turned(("h2T", l), 1, HT)

                until_drained(dve, ("router", l))
                step(dve.tensor_tensor(sel[:, :, :], scores[:, :, :], rb_bc[l].unsqueeze(1).to_broadcast([P, T, E]), ALU.add))
                settle()
                for t in range(T):
                    for g in range(EG):
                        ins = dve.max(top8[:, EG * t + g, :], sel[:, t, EPG * g:EPG * g + EPG])
                step(ins)
                settle()
                step(dve.tensor_tensor(gsc[:, :, :].rearrange("p a b -> p (a b)"), top8[:, :, 0], top8[:, :, 1], ALU.add))
                settle()
                other = gsc[:, :, :].unsqueeze(2).to_broadcast([P, T, EG, EG])
                own = gsc[:, :, :].unsqueeze(3).to_broadcast([P, T, EG, EG])
                dve.tensor_tensor(gcmp[0], other, own, ALU.is_gt)
                step(dve.tensor_tensor(gcmp[1], other, own, ALU.is_equal))
                settle()
                step(dve.tensor_tensor(gcmp[1], gcmp[1], low8[:, :, :].unsqueeze(1).to_broadcast([P, T, EG, EG]), ALU.mult))
                settle()
                step(dve.tensor_tensor(gcmp[0], gcmp[0], gcmp[1], ALU.add))
                settle()
                step(dve.tensor_reduce(grank[:, :, :].rearrange("p a b -> p (a b)"),
                                       gcmp[0][:, :, :, :].rearrange("p a b c -> p (a b) c"), AX, ALU.add))
                settle()
                step(dve.tensor_scalar(grank[:, :, :], grank[:, :, :], float(TOPG), -BIG, ALU.is_ge, ALU.mult))
                settle()
                step(dve.tensor_tensor(sel[:, :, :].rearrange("p t (g e) -> p (t g) e", g=EG),
                                       sel[:, :, :].rearrange("p t (g e) -> p (t g) e", g=EG),
                                       grank[:, :, :].rearrange("p a b -> p (a b)").unsqueeze(2).to_broadcast([P, T * EG, EPG]),
                                       ALU.add))
                settle()
                for t in range(T):
                    ins = dve.max(top8[:, t, :], sel[:, t, :])
                step(ins)
                settle()
                for t in range(T):
                    ins = dve.match_replace(pos[:, t, :], top8[:, t, :], sel[:, t, :], -3.0e38)
                step(ins)
                settle()
                step(dve.tensor_tensor(mask[:, :, :], pos[:, :, :], sel[:, :, :], ALU.not_equal))
                settle()
                for t in range(T):
                    ins = dve.tensor_tensor_scan(krank[:, t, :], mask[:, t, :], mask[:, t, :], 0.0, ALU.add, ALU.bypass)
                step(dve.tensor_copy(mask_b[:, :, :], mask[:, :, :]))
                settle()
                step(dve.tensor_tensor(krank[:, :, :], krank[:, :, :], mask[:, :, :], ALU.subtract))
                settle()
                dve.tensor_copy(V[:, :, :, 2], krank[:, :, :]).then_inc(mask_ready, 1)
                ps = until_filled(dve, ("places", l))
                step(dve.scalar_tensor_tensor(pos[:, :, :].rearrange("p a b -> p (a b)"),
                                              mask[:, :, :].rearrange("p a b -> p (a b)"), -4096.0, ps[:, 0:T * E],
                                              ALU.mult, ALU.add))
                dve.scalar_tensor_tensor(load_keys, ps[:, E * T:E * T + E], float(P), slot_no[:, 0:E], ALU.mult, ALU.add
                                         ).then_inc(drained[7], 1)
                settle()
                step(dve.tensor_scalar(pos[:, :, :], pos[:, :, :], 4096.0, None, ALU.add))
                settle()

                def onehots(n, experts_):
                    for i in experts_:
                        e = SLOTS * n + i
                        if e >= 4 and i != 3:
                            dve.wait_ge(onehot_used, (E - NG) * l + e - 4 - (e - 4) // SLOTS + 1)
                        for t in range(T):
                            ins = dve.tensor_scalar(onehot[e % 4][:, t, :], slot_no[:, :], pos[:, t, e:e + 1], None,
                                                    ALU.is_equal)
                        ins.then_inc(onehot_ready, 1)

                def finish_table(n, b):
                    es = slice(SLOTS * n, SLOTS * n + SLOTS)
                    dve.tensor_reduce(destf[:, es], psum[:, b, 0:3 * SLOTS].rearrange("p (e c) -> p e c", c=3), AX,
                                      ALU.add).then_inc(drained[b], 1)

                def write_table(n):
                    es = slice(SLOTS * n, SLOTS * n + SLOTS)
                    step(dve.tensor_scalar(table[:, es, 0], destf[:, es], float(NOWHERE), None, ALU.add))
                    settle()
                    dve.tensor_scalar(table[:, es, 1], table[:, es, 0], 3, None,
                                      ALU.logical_shift_right).then_inc(table_ready, 1)
                onehots(0, range(SLOTS))
                until_filled(dve, ("table", l))
                finish_table(0, 4)
                until_drained(dve, ("table", l))
                write_table(0)

                def rank_loads():
                    for r in range(4):
                        step(dve.max(load_top[:, 8 * r:8 * r + 8], load_keys))
                        settle()
                        if r < 3:
                            step(dve.match_replace(load_keys, load_top[:, 8 * r:8 * r + 8], load_keys, -1.0))
                            settle()
                    step(dve.tensor_copy(load_expert, load_top))
                    dve.tensor_copy(more_key[:, 0:1], load_top[:, 0:1])
                    step(dve.scalar_tensor_tensor(more_key[:, 1:2], load_top[:, 0:1], -float(P * P), load_top[:, 8:9],
                                                  ALU.add, ALU.max))
                    settle()
                    step(dve.tensor_scalar(load_expert, load_expert, P - 1, None, ALU.bitwise_and))
                    settle()
                    dve.tensor_copy(more_keyi[:, :], more_key[:, :]).then_inc(most_ready, 1)

                def gates_whole():
                    step(dve.tensor_tensor(gate[:, :, :], mask[:, :, :], scores[:, :, :], ALU.mult))
                    settle()
                    step(dve.tensor_reduce(gsum[:, :], gate[:, :, :], AX, ALU.add))
                    settle()
                    step(dve.reciprocal(gsum[:, :], gsum[:, :]))
                    settle()
                    for t in range(T):
                        ins = dve.tensor_scalar(gate[:, t, :], gate[:, t, :], gsum[:, t:t + 1], ROUTED_SCALE, ALU.mult, ALU.mult)
                    step(ins)
                    settle()

                def gates_of(k):
                    step(dve.scalar_tensor_tensor(sel[:, :, :].rearrange("p a b -> p (a b)"),
                                                  krank[:, :, :].rearrange("p a b -> p (a b)"), float(k),
                                                  gate[:, :, :].rearrange("p a b -> p (a b)"), ALU.is_equal, ALU.mult))
                    settle()
                    step(dve.tensor_reduce(gk[:, :, k], sel[:, :, :], AX, ALU.add))
                    settle()

                base = MARK[("loop", l)]

                def glu(g, u, first=False):
                    b = 5 + u % 2
                    dve.wait_ge(filled[b], base[b] + 4 * g + u // 2 + 1 + tables_before(b, u, first))
                    dve.wait_ge(drained[1 + u % 2], base[1 + u % 2] + 4 * g + u // 2 + 1)
                    dve.tensor_tensor(aT[u % 2], s1[u % 2], psum[:, b, 0:P], ALU.mult).then_inc(drained[b], 1)

                def rows_out(g, u, first=False):
                    if not (first and u < YROWS and l == 0):
                        dve.wait_ge(y_out[u % YROWS], 16 * (2 * g + u // YROWS) + 16 * (E // YROWS) * l)
                    for half in range(2):
                        b = 3 + 4 * half
                        dve.wait_ge(filled[b], base[b] + SLOTS * g + u + 1)
                        cols_ = slice(512 * half, 512 * half + 512)
                        dve.tensor_tensor(yrow[u % YROWS][:, cols_], psum[:, b, :], g2bc[:, cols_], ALU.mult
                                          ).then_inc(drained[b], 1)

                def group(g, first=False, last=False):
                    for u in range(SLOTS):
                        table = first and u + 1 < NG
                        if table:
                            onehots(u + 1, range(SLOTS // 2, SLOTS))
                        if last:
                            if u == 0:
                                gates_whole()
                            if u == SLOTS - 1:
                                rank_loads()
                            gates_of(u)
                        glu(g, u, first)
                        if table:
                            b = table_bank(u)
                            dve.wait_ge(filled[b], base[b] + u + 1)
                            finish_table(u + 1, b)
                            dve.wait_ge(drained[b], base[b] + u + 1)
                            write_table(u + 1)
                            if u + 2 < NG:
                                onehots(u + 2, range(SLOTS // 2))
                        if u:
                            rows_out(g, u - 1, first)
                        elif not first:
                            rows_out(g - 1, SLOTS - 1)
                onehots(1, range(SLOTS // 2))
                group(0, first=True)
                with dve.Fori(1, NG - 1) as g:
                    group(g)
                group(NG - 1, last=True)
                rows_out(NG - 1, SLOTS - 1)

                def more_blocks(stage):
                    done = more[l]

                    def unit(b, j, i):
                        e = dve.value_load(load_expert[0:1, bass.ds(j, 1)], min_val=0, max_val=E - 1)
                        OWN = 3

                        def own_step(ins, n):
                            ins.then_inc(done["step"], 1)
                            dve.wait_ge(done["step"], OWN * i + n)
                        dve.tensor_copy(V1[:, :, 0:3], V[:, :, bass.ds(e, 1), :].rearrange("p t o c -> p (t o) c"))
                        own_step(dve.tensor_copy(pos1[:, :], pos[:, :, bass.ds(e, 1)].rearrange("p t o -> p (t o)")), 1)
                        own_step(dve.tensor_scalar(pos1[:, :], pos1[:, :], -float(P * (b + 1)), None, ALU.add), 2)
                        for t in range(T):
                            ins = dve.tensor_scalar(onehot[0][:, t, :], slot_no[:, :], pos1[:, t:t + 1], None, ALU.is_equal)
                        ins.then_inc(done["onehot"], 1)
                        dve.wait_ge(done["dest"], i + 1)
                        own_step(dve.tensor_reduce(destf[:, 0:1], psum[:, 6, 0:3], AX, ALU.add), 3)
                        dve.tensor_scalar(idx[0][:, 0:1], destf[:, 0:1], float(NOWHERE), None, ALU.add).then_inc(done["idx"], 1)
                        dve.wait_ge(done["idx"], 2 * i + 1)
                        dve.tensor_scalar(idx[0][:, 1:2], idx[0][:, 0:1], 3, None, ALU.logical_shift_right).then_inc(done["idx"], 1)
                        dve.wait_ge(done["silu"], i + 1)
                        dve.tensor_tensor(aT[0], s1[0], psum[:, 3, 0:P], ALU.mult).then_inc(done["gated"], 1)
                        dve.wait_ge(done["down"], i + 1)
                        for half in range(2):
                            cols_ = slice(512 * half, 512 * half + 512)
                            dve.tensor_tensor(yrow[0][:, cols_], psum[:, 4 + half, :], g2bc[:, cols_], ALU.mult
                                              ).then_inc(done["yrow"], 1)
                        dve.wait_ge(done["sent"], 16 * i + 16)
                    for b in range(YROWS):
                        dve.wait_ge(y_out[b], 16 * (E // YROWS) * (l + 1))
                    for b, j0, j1, before in MORE[stage]:
                        with dve.Fori(j0, j1) as j:
                            unit(b, j, before + j)
                when_more(dve, l, more_blocks)

                settle()
                dve.wait_ge(base_ready, T * (l + 1))
                k = 2 * l + 1
                for j in range(2 * T):
                    t, half = divmod(j, 2)
                    dve.wait_ge(part_in[j % 3], 16 * (j // 3 + 1 + PARTS_OF[j % 3] * l))
                    r = SH[:, t, 512 * half:512 * half + 512]
                    for i in range(DVE_ROWS):
                        step(dve.scalar_tensor_tensor(r, part[j % 3][:, i, :], gk[:, t, i:i + 1], r, ALU.mult, ALU.add))
                        settle()
                    dve.wait_ge(part_added, 2 * T * l + j + 1)
                    step(dve.tensor_tensor(r, r, part[j % 3][:, DVE_ROWS, :], ALU.add))
                    PART[l].append(steps[0])
                    if half:
                        statistics(k, t, SH)
                        if t:
                            normalise(k, t - 1, SH, lnrow_moe)
                normalise(k, T - 1, SH, lnrow_moe)

            def attention():
                for v in (0, 1):
                    until_mod("kv", v)
                move_modulated("uT", 1, HT, MODC[("kv", 1)], MODC[("kv", 0)])
                ps = until_filled(dve, "forget")
                x2 = dts[:, 0:2, :].rearrange("p a b -> p (a b)")
                dve.scalar_tensor_tensor(x2.rearrange("p (a b) -> p a b", a=T), ps[:, 0:T * AH].rearrange("p (a b) -> p a b", a=T),
                                         -1.0, fb_bc.unsqueeze(1).to_broadcast([P, T, AH]), ALU.mult,
                                         ALU.subtract).then_inc(drained[6], 1)
                until_drained(dve, "forget")
                soft(dve.tensor_scalar(x2, x2, 1.0, None, ALU.mult))
                softplus(x2, logf[:, :, :].rearrange("p a b -> p (a b)"), T * AH, 4)
                dve.tensor_scalar(logf[:, :, :], logf[:, :, :], -1.0, None, ALU.mult).then_inc(logf_ready, 1)
                for j in range(1, KC, 2):
                    move(("kT", j), kT[:, j, :])
                ps = until_filled(dve, "cumf")
                dve.tensor_copy(cumf[:, :, :].rearrange("p a b -> p (a b)"), ps[:, 0:T * AH]).then_inc(drained[7], 1)
                for n in range(2):
                    for t in range(1, T, 2):
                        move(("v", n, t), vtok[:, t, 512 * n:512 * n + 512])
                dve.wait_ge(q_zeros, 3)
                ps = until_filled(dve, "cumfT")
                dve.tensor_copy(cumfT[0:T * AH, :], ps[0:T * AH, 0:P]).then_inc(drained[7], 1)
                move_modulated("qhT", 1, HT, MODC[(1, SCALE1)], MODC[(1, SHIFT1)])
                for j in range(1, KC, 2):
                    ps = until_filled(dve, ("qT", j))
                    dve.tensor_copy(qT[0][0:HD, j, :], ps[0:HD, :])
                    dve.tensor_copy(qT[1][HD:P, j, :], ps[HD:P, :]).then_inc(drained[MARK[("qT", j)][0]], 1)

                def maximum(n):
                    h, i = divmod(n, T)
                    nk = P * (i + 1)
                    dve.wait_ge(masked, n + 1)
                    if n >= 3:
                        dve.wait_ge(prob_ready, n - 2)
                    ps = until_filled(dve, ("ncf", h))
                    ins = dve.tensor_tensor_reduce(shifted[n % 3][:, 0:nk], logit[n % 3][:, 0:nk], ps[:, 0:nk], 1.0, -3.0e38,
                                                   ALU.subtract, ALU.max, mx[:, n % 4:n % 4 + 1])
                    if i == T - 1:
                        ins.then_inc(drained[MARK[("ncf", h)][0]], 1)
                        until_drained(dve, ("ncf", h))
                    else:
                        step(ins)
                        settle()
                    dve.tensor_scalar(mx[:, 4 + n % 4:5 + n % 4], mx[:, n % 4:n % 4 + 1], -1.0, None, ALU.mult).then_inc(max_ready, 1)

                def move_probs(n):
                    h, i = divmod(n, T)
                    ps = until_filled(dve, ("pT", n))
                    dve.tensor_copy(probT[n % 2][:, 0:i + 1, :], ps[:, 0:P * (i + 1)].rearrange("p (a b) -> p a b", b=P)
                                    ).then_inc(drained[MARK[("pT", n)][0]], 1)

                def head_out(h):
                    ps = until_filled(dve, ("o", h))
                    dve.wait_ge(prob_ready, T * h + T)
                    step(dve.reciprocal(rinv[:, h % 2, :], rsum[:, h % 2, :]))
                    settle()
                    own = ps.rearrange("p (a b) -> p a b", a=T)[:, :, HD * (h % 2):HD * (h % 2) + HD]
                    dve.tensor_tensor(otok[:, :, HD * h:HD * h + HD], own,
                                      rinv[:, h % 2, :].unsqueeze(2).to_broadcast([P, T, HD]), ALU.mult
                                      ).then_inc(drained[MARK[("o", h)][0]], 1)
                NU = AH * T
                maximum(0)
                for n in range(NU):
                    if n + 1 < NU:
                        maximum(n + 1)
                    move_probs(n)
                    if n % T == 1 and n > T:
                        head_out(n // T - 1)
                head_out(AH - 1)
                move_turned("oT", 1, HT)
                diagonals(1)
                mixed(1, Rmix[1])

            experts(0)
            attention()
            experts(1)

        @block.gpsimd
        def _(pool):
            steps = [0]

            def step(ins):
                ins.then_inc(pool_step, 1)
                steps[0] += 1

            def settle():
                pool.wait_ge(pool_step, steps[0])

            last_row, last_part = pool.alloc_register("last_row"), pool.alloc_register("last_part")
            pool.reg_mov(last_row, S - 1)
            pool.reg_mov(last_part, S * TOPK - 1)
            step(pool.memset(ident[:, :], 0.0))
            step(pool.memset(upper[:, :], 1.0))
            step(pool.memset(after[:, :], 1.0))
            step(pool.memset(before_b[:, :], 1.0))
            step(pool.memset(low8[:, :, :], 1.0))
            pool.memset(ones[:, :], 1.0).then_inc(consts, 1)
            pool.memset(ones_b[:, :], 1.0).then_inc(consts, 1)
            pool.iota(slot_no[:, :], [[1, P]], base=0, channel_multiplier=0,
                      allow_small_or_imprecise_dtypes=True).then_inc(consts, 1)
            pool.iota(V[:, :, :, 0], [[0, T], [0, E]], base=0, channel_multiplier=TOPK,
                      allow_small_or_imprecise_dtypes=True).then_inc(consts, 1)
            pool.iota(V[:, :, :, 1], [[P * TOPK, T], [0, E]], base=-NOWHERE, channel_multiplier=0,
                      allow_small_or_imprecise_dtypes=True).then_inc(consts, 1)
            settle()
            pool.affine_select(out=ident[:, :], in_=ident[:, :], compare_op=ALU.not_equal, fill=1.0, base=0,
                               pattern=[[-1, P]], channel_multiplier=1).then_inc(consts, 1)
            pool.affine_select(out=upper[:, :], in_=upper[:, :], compare_op=ALU.is_ge, fill=0.0, base=0,
                               pattern=[[1, P]], channel_multiplier=-1).then_inc(consts, 1)
            pool.affine_select(out=after[:, :], in_=after[:, :], compare_op=ALU.is_gt, fill=0.0, base=0,
                               pattern=[[-1, P]], channel_multiplier=1).then_inc(consts, 1)
            pool.affine_select(out=before_b[:, :], in_=before_b[:, :], compare_op=ALU.is_gt, fill=0.0, base=0,
                               pattern=[[1, P]], channel_multiplier=-1).then_inc(consts, 1)
            pool.affine_select(out=low8[:, :, :], in_=low8[:, :, :], compare_op=ALU.is_gt, fill=0.0, base=0,
                               pattern=[[1, EG], [-1, EG]], channel_multiplier=0).then_inc(consts, 1)
            pool.wait_ge(consts, CONSTS)

            for a in range(1, ADA_PAIRED, 2):
                pool.wait_ge(ada_scaled, a // 2 + 1)
                w = ada_pool[a // 2 % 2]
                for n in (4, 2):
                    step(pool.tensor_tensor(w[:, 0:n, :], w[:, 0:n, :], w[:, n:2 * n, :], ALU.add))
                    settle()
                if a >= 2:
                    until_filled(pool, ("mod",) + ada_blocks[a - 2])
                pool.tensor_tensor(ada_acc[1], w[:, 0, :], w[:, 1, :], ALU.add).then_inc(ada_summed[1], 1)

            def heads(v):
                return v.rearrange("p (h d) -> p h d", h=GH)

            def bch(v):
                return v.unsqueeze(2).to_broadcast([P, GH, HD])

            def scan_pool(q):
                ch, g = divmod(q, GROUPS)
                until_drained(pool, ("sums", ch))
                pool.wait_ge(xdt_ready, q + 1)
                if q >= 2 and ch < T - 1:
                    until_filled(pool, ("st", q - 2))
                if ch < T - 1:
                    pool.tensor_tensor(heads(xdte[q % 2]), heads(xdt[q % 2]),
                                       bch(exps[ch % 2][:, HEADS + GH * g:HEADS + GH * g + GH]), ALU.mult).then_inc(xdte_ready, 1)
                if 0 < ch < T - 1:
                    until_filled(pool, ("yoff", q))
                    pool.tensor_tensor(heads(state[:, g, :]), heads(state[:, g, :]),
                                       bch(exps[ch % 2][:, 2 * HEADS + GH * g:2 * HEADS + GH * g + GH]),
                                       ALU.mult).then_inc(state_scaled, 1)
                until_drained(pool, ("yd", q))
                if ch:
                    until_drained(pool, ("yoff", q))
                    step(pool.tensor_tensor(yg[q % 2], yg[q % 2], yoff[q % 2], ALU.add))
                    settle()
                z = zs[:, ch, GW * g:GW * g + GW]
                pool.tensor_tensor(z, yg[q % 2], z, ALU.mult).then_inc(yz_ready, 1)
            for q in range(NQ):
                scan_pool(q)

            def shift(k, t, lnrow):
                pool.wait_ge(ln_scaled, T * k + t + 1)
                pool.tensor_tensor(X[:, t, :], X[:, t, :], lnrow[1], ALU.add).then_inc(x_ready, 1)

            def layer_norm(k, lnrow):
                for t in range(T):
                    shift(k, t, lnrow)
            layer_norm(0, lnrow_mix)

            def experts(l):
                for half in range(2):
                    until_drained(pool, (("sh2", l), half))
                for t in range(T):
                    pool.wait_ge(h2_scaled, T * l + t + 1)
                    pool.tensor_tensor(H2[:, t, :], H2[:, t, :], sh2bc, ALU.add).then_inc(h2_ready, 1)
                for t in range(T):
                    pool.wait_ge(h2_ready, T * l + t + 1)
                    pool.dma_start(rows_dram[TILES[t], :], H2[:, t, :]).then_inc(h2_out, 16)
                until_drained(pool, (("shared_in", l, 0)))
                until_drained(pool, (("shared_in", l, 1)))
                pool.tensor_tensor(aS[0], aS[0], aS[1], ALU.mult).then_inc(sh_gated, 1)

                def base_part(n):
                    t, add = divmod(n, 2)
                    if add:
                        settle()
                        pool.wait_ge(x_scaled, T * l + t + 1)
                        pool.tensor_tensor(SH[:, t, :], SH[:, t, :], X[:, t, :], ALU.add).then_inc(base_ready, 1)
                    else:
                        for half in range(2):
                            until_drained(pool, (("g2", l), half))
                            until_drained(pool, ("shared", l, t, half))
                        step(pool.tensor_tensor(SH[:, t, :], SH[:, t, :], g2bc, ALU.mult))
                pool.wait_ge(table_ready, NG * l + 1)
                pool.wait_ge(h2_out, 16 * T * (l + 1))
                base = MARK[("loop", l)]

                def carrier(n):
                    return pool.tensor_tensor(passed[:, n:n + 1], ones[:, 0:1], ones[:, 1:2], ALU.mult)

                def fetch(g, u, first=False):
                    if not first:
                        pool.wait_ge(y_out[u % YROWS], 16 * (2 * g + u // YROWS - 1) + 16 * (E // YROWS) * l)
                    if not (first and u < 4):
                        pool.wait_ge(filled[4], base[4] + SLOTS * g + u - 3)
                    pool.tensor_copy(idx[u][:, :], table[:, bass.ds(SLOTS * g + u, 1), :].rearrange("p a b -> p (a b)")
                                     ).then_inc(idx_ready, 1)
                    pool.wait_ge(idx_ready, E * l + SLOTS * g + u + 1)
                    carrier(SLOTS)
                    pool.indirect_dma_start(out=xg[u % 4], out_offset=None, in_=rows_dram,
                                            in_offset=bass.IndirectOffsetOnAxis(ap=idx[u][:, 1:2], axis=0),
                                            bounds_check=last_row, oob_is_err=False).then_inc(xg_in[u % 4], 16)

                def send(g, u):
                    for b in (3, 7):
                        pool.wait_ge(drained[b], base[b] + SLOTS * g + u + 1)
                    carrier(u)
                    pool.indirect_dma_start(out=part_dram,
                                            out_offset=bass.IndirectOffsetOnAxis(ap=idx[u][:, 0:1], axis=0),
                                            in_=yrow[u % YROWS], in_offset=None,
                                            bounds_check=last_part, oob_is_err=False).then_inc(y_out[u % YROWS], 16)

                AHEAD = 5

                def group(g, first=False, last=False):
                    for u in range(SLOTS):
                        v = u + AHEAD
                        if first and v == SLOTS:
                            pool.wait_ge(table_ready, NG * l + 2)
                        if v < SLOTS:
                            fetch(g, v, first)
                        elif not last:
                            fetch(g + 1, v - SLOTS)
                        send(g, u)
                        if first:
                            base_part(u)
                for t in range(T):
                    until_filled(pool, ((("h2T", l)), t, 1))
                for u in range(AHEAD):
                    fetch(0, u, True)
                group(0, first=True)
                pool.wait_ge(table_ready, NG * (l + 1))
                with pool.Fori(1, NG - 1) as g:
                    group(g)
                group(NG - 1, last=True)

                def more_blocks(stage):
                    done = more[l]

                    def unit(i):
                        pool.wait_ge(done["idx"], 2 * i + 2)
                        carrier(SLOTS + 1).then_inc(done["carried"], 1)
                        pool.indirect_dma_start(out=xg[0], out_offset=None, in_=rows_dram,
                                                in_offset=bass.IndirectOffsetOnAxis(ap=idx[0][:, 1:2], axis=0),
                                                bounds_check=last_row, oob_is_err=False).then_inc(done["rows"], 16)
                        pool.wait_ge(done["yrow"], 2 * i + 2)
                        pool.wait_ge(done["carried"], i + 1)
                        carrier(SLOTS + 2)
                        pool.indirect_dma_start(out=part_dram,
                                                out_offset=bass.IndirectOffsetOnAxis(ap=idx[0][:, 0:1], axis=0),
                                                in_=yrow[0], in_offset=None,
                                                bounds_check=last_part, oob_is_err=False).then_inc(done["sent"], 16)
                    for b, j0, j1, before in MORE[stage]:
                        with pool.Fori(j0, j1) as j:
                            unit(before + j)
                when_more(pool, l, more_blocks)
                for j in range(2 * T):
                    pool.wait_ge(part_scaled, 2 * T * l + j + 1)
                    rows_ = part[j % 3]
                    for i in range(DVE_ROWS + 1, TOPK):
                        ins = pool.tensor_tensor(rows_[:, DVE_ROWS, :], rows_[:, DVE_ROWS, :], rows_[:, i, :], ALU.add)
                        if i < TOPK - 1:
                            step(ins)
                            settle()
                    ins.then_inc(part_added, 1)
                    if j % 2 and j // 2 >= 2:
                        shift(2 * l + 1, j // 2 - 2, lnrow_moe)
                for t in (T - 2, T - 1):
                    shift(2 * l + 1, t, lnrow_moe)

            def attention():
                pool.wait_ge(x_ready, 2 * T)
                pool.memset(qT[0][HD:P, :, :], 0.0).then_inc(q_zeros, 1)
                pool.wait_ge(q_zeros, 1)
                pool.memset(qT[1][0:HD, :, :], 0.0).then_inc(q_zeros, 1)
                pool.wait_ge(q_zeros, 2)
                pool.memset(cumfT[T * AH:P, :], 0.0).then_inc(q_zeros, 1)
                NU = AH * T
                for n in range(NU):
                    h, i = divmod(n, T)
                    until_drained(pool, ("qk", n))
                    d = logit[n % 3][:, P * i:P * i + P]
                    pool.affine_select(out=d, in_=d, compare_op=ALU.is_ge, fill=-BIG, base=0, pattern=[[-1, P]],
                                       channel_multiplier=1).then_inc(masked, 1)
                layer_norm(2, lnrow_mix)

            experts(0)
            attention()
            experts(1)

        @block.sync
        def _(sp_):
            def as_rows(v, n):
                return v.rearrange("(n p) -> n p", p=P)

            def load(dst, src, done=small_in):
                sp_.dma_start(dst, src).then_inc(done, 16)

            def ada_cols(a):
                l, blk = ada_blocks[a]
                return cols_of(kv_ada_w if l == "kv" else ada_w[l], 512 * blk)

            def load_ada_dve(a, half):
                n = ada_count(a)
                rows_ = slice(KC // 2 * half, KC // 2 * (half + 1))
                if n:
                    sp_.wait_ge((ada_half, ada_summed[0])[half], n)
                sp_.dma_start(ada_dve[:, rows_, :], ada_cols(a)[:, rows_, :]).then_inc(ada_dve_in[half], 16)

            def load_ada_pool(a):
                n = ada_count(a)
                if n >= 2:
                    sp_.wait_ge(ada_summed[1], n - 1)
                sp_.dma_start(ada_pool[n % 2], ada_cols(a)).then_inc(ada_pool_in[n % 2], 16)

            def load_ada(a):
                load_ada_dve(a, 0)
                load_ada_pool(a + 1)
                load_ada_dve(a, 1)

            for dst, src in ((rows[0:8, 0, :], as_rows(c[0], 8)),
                             (rows[8:56, 0, :], as_rows(ada_b[0], 48)),
                             (rows[56:104, 0, :], as_rows(ada_b[1], 48)),
                             (rows[104:120, 0, :], as_rows(kv_ada_b, 16)),
                             (rows[0:CONV * CT, 1, :], ssm_conv_w[0].rearrange("k (n p) -> (k n) p", p=P)),
                             (rows[CONV * CT:CONV * CT + CT, 1, :], as_rows(ssm_conv_b[0], CT)),
                             (rows[0:XT, 2, :], as_rows(ssm_norm_w[0], XT))):
                load(dst, src, vectors_in)
            load_ada(0)
            load_ada(2)
            for t in range(T):
                sp_.dma_start(X[:, t, :], x[0, TILES[t], :]).then_inc(x_in, 16)
            at = 0
            for v in (ssm_dt_bias[0], ssm_a_log[0], ssm_d[0], kv_fb, moe_bias[0], moe_bias[1]):
                n = v.shape[0]
                load(bcs[:, at:at + n], v.partition_broadcast(P))
                at += n
            load(wdt[:, :, :], ssm_w_in[0].rearrange("(k p) n -> p k n", p=P)[:, :, DI + XBC:DI + XBC + HEADS])
            load(wf[:, :, :], kv_w.rearrange("(k p) n -> p k n", p=P)[:, :, 2 * D:2 * D + AH])
            load(wr[:, :, :], moe_w_router[0].rearrange("(k p) n -> p k n", p=P))

            def stream(i):
                if i >= RING:
                    b, n = MARK[("item", i - RING)]
                    sp_.wait_ge(filled[b], n)
                sp_.dma_start(ring[i % RING], items[i][1]).then_inc(ring_in[i % RING], 16)
            for i in range(2):
                stream(i)
            for n in range(CT // 4):
                for half in range(2):
                    for a in ada_beside(n, half)[0:1]:
                        load_ada(a)
                stream(n + 2)
            for n in range(XT // 4):
                for a in (ada_beside_z(n, 0), ada_beside_z(n, 1)):
                    for half in range(2):
                        load_ada_dve(a, half)
                stream(CT // 4 + 2 + n)
            for i in range(CT // 4 + XT // 4 + 2, n_items0):
                stream(i)

            def ln_rows(k, dst, g, b):
                sp_.dma_start(dst[0], g.partition_broadcast(P)).then_inc(lnrow_in, 16)
                sp_.dma_start(dst[1], b.partition_broadcast(P)).then_inc(lnrow_in, 16)

            def experts(l):
                b, n = MARK[("mix", l, 1, T - 1)]
                sp_.wait_ge(filled[b], n)
                sp_.dma_start(shw[:, 0, :].rearrange("p (k f) -> p k f", k=KC),
                              moe_ws1[l].rearrange("(k p) f -> p k f", p=P)).then_inc(shw_in, 16)
                sp_.dma_start(shw[:, 1, :].rearrange("p (k f) -> p k f", k=KC),
                              moe_ws3[l].rearrange("(k p) f -> p k f", p=P)).then_inc(shw_in, 16)
                sp_.dma_start(shw[:, 2, :], moe_ws2[l]).then_inc(shw_in, 16)

                def fetch(i, u):
                    for n, w in enumerate((moe_w1, moe_w3)):
                        src = w[l][bass.ds(i, 1), :, :] if not isinstance(i, int) else w[l][i:i + 1, :, :]
                        sp_.dma_start(exp_w[u][:, n, :].rearrange("p (k f) -> p k f", k=KC),
                                      src.rearrange("o (k p) f -> p (o k) f", p=P)).then_inc(exp_in[u], 16)
                    src = moe_w2[l][bass.ds(i, 1), :, :] if not isinstance(i, int) else moe_w2[l][i:i + 1, :, :]
                    sp_.dma_start(exp_w[u][:, 2, :], src.rearrange("o f d -> f (o d)")).then_inc(exp_in[u], 16)
                base = MARK[("loop", l)]
                for u in range(4, SLOTS):
                    fetch(u, u)
                sp_.wait_ge(x_ready, T * (2 * l + 1))
                for u in range(4):
                    fetch(u, u)
                with sp_.Fori(1, NG) as g:
                    for u in range(SLOTS):
                        sp_.wait_ge(filled[7], base[7] + SLOTS * g + u - SLOTS + 1)
                        fetch(SLOTS * g + u, u)
                for b in range(YROWS):
                    sp_.wait_ge(y_out[b], 16 * (E // YROWS) * (l + 1))

                def more_blocks(stage):
                    done = more[l]

                    def unit(j, i):
                        e = sp_.value_load(load_expert[0:1, bass.ds(j, 1)], min_val=0, max_val=E - 1)
                        sp_.wait_ge(done["onehot"], i + 1)
                        for n, w in enumerate((moe_w1, moe_w3)):
                            sp_.dma_start(exp_w[0][:, n, :].rearrange("p (k f) -> p k f", k=KC),
                                          w[l][bass.ds(e, 1), :, :].rearrange("o (k p) f -> p (o k) f", p=P)
                                          ).then_inc(done["weights"], 16)
                        sp_.dma_start(exp_w[0][:, 2, :], moe_w2[l][bass.ds(e, 1), :, :].rearrange("o f d -> f (o d)")
                                      ).then_inc(done["weights"], 16)
                    for b, j0, j1, before in MORE[stage]:
                        with sp_.Fori(j0, j1) as j:
                            unit(j, before + j)
                    sp_.wait_ge(done["sent"], 16 * MORE_UNITS[stage])
                when_more(sp_, l, more_blocks)
                ln_rows(2 * l + 1, lnrow_moe, ln2_g[l], ln2_b[l])
                rows_of = part_dram.rearrange("(t p k) d -> t p k d", p=P, k=TOPK)
                for j in range(2 * T):
                    t, half = divmod(j, 2)
                    if j >= 3:
                        sp_.wait_ge(dve_step, PART[l][j - 3])
                    sp_.dma_start(part[j % 3], rows_of[t, :, :, 512 * half:512 * half + 512]).then_inc(part_in[j % 3], 16)

            sp_.wait_ge(squared, NQ)
            until_filled(sp_, ("mix", 0, 0, 0))
            ln_rows(0, lnrow_mix, ln1_g[0], ln1_b[0])
            experts(0)
            until_filled(sp_, "wr0")
            sp_.dma_start(wr[:, :, :], moe_w_router[1].rearrange("(k p) n -> p k n", p=P)).then_inc(wr_in, 16)
            for i in range(n_items0, n_items1):
                if i < n_items0 + RING:
                    sp_.dma_start(ring[i % RING], items[i][1]).then_inc(ring_in[i % RING], 16)
                else:
                    stream(i)
            until_filled(sp_, ("mix", 1, 0, 0))
            ln_rows(2, lnrow_mix, ln1_g[1], ln1_b[1])
            experts(1)
            for t in range(T):
                sp_.wait_ge(x_ready, T * 3 + t + 1)
                sp_.dma_start(out[0, TILES[t], :], X[:, t, :]).then_inc(out_done, 16)
            sp_.wait_ge(out_done, 16 * T)


_INS = ["x", "c", "ada_w", "ada_b", "ln1_g", "ln1_b", "ln2_g", "ln2_b", "ssm_w_in", "ssm_conv_w", "ssm_conv_b",
        "ssm_dt_bias", "ssm_a_log", "ssm_d", "ssm_norm_w", "ssm_w_out", "kv_ada_w", "kv_ada_b", "kv_w", "kv_fb",
        "attn_w_q", "attn_w_o", "moe_w_router", "moe_bias", "moe_w1", "moe_w3", "moe_w2", "moe_ws1", "moe_ws3",
        "moe_ws2"]
_OUTS = [((1, 512, 1024), "float32")]


def kernel(**inputs):
    import numpy as _np
    import concourse.bacc as _bacc
    from concourse import mybir as _mybir
    from concourse.bass_utils import run_bass_kernel_spmd as _run

    nc = _bacc.Bacc("TRN2", target_bir_lowering=False, num_devices=1)
    arrays, args = {}, []
    for name in _INS:
        a = _np.ascontiguousarray(inputs[name])
        arrays[f"in_{name}_dram"] = a
        args.append(nc.dram_tensor(f"in_{name}_dram", a.shape, _mybir.dt.from_np(a.dtype), kind="ExternalInput").ap())
    for i, (shape, dtype) in enumerate(_OUTS):
        dt = _mybir.dt.from_np(_np.dtype(dtype))
        args.append(nc.dram_tensor(f"out_{i}_dram", shape, dt, kind="ExternalOutput").ap())
    trunk(nc, *args)
    r = _run(nc, [arrays], core_ids=[0])
    got = tuple(r.results[0][f"out_{i}_dram"] for i in range(len(_OUTS)))
    return got[0]
```
